# Optimizing a Trainium2 kernel written in Bass

```python
import jax, jax.numpy as jnp
from jax import lax
import numpy as np

D_MODEL = 1024
BATCH = 1
SEQ = 512
DEPTH = 2

N_META = 16
GRID_W = 64
CHUNK = 64
META_PAD = CHUNK - N_META

M_HEADS = 4
M_WIDTH = D_MODEL // 2
M_HEAD_DIM = M_WIDTH // M_HEADS
M_CONV = 5
R_HEADS = 4
R_WIDTH = D_MODEL // 2
R_HEAD_DIM = R_WIDTH // R_HEADS
ROPE_BASE = 10000.0
EVEN_IN = 4 * M_WIDTH + 4 * M_HEADS + 4 * R_WIDTH
EVEN_MIX = M_WIDTH + R_WIDTH

NA_HEAD_DIM = 64
NA_HEADS = D_MODEL // NA_HEAD_DIM
NA_WIDTH = NA_HEADS * NA_HEAD_DIM
NA_WIN_ROWS = 8
NA_WIN_COLS = 16
ODD_IN = 3 * NA_WIDTH

N_EXPERTS = 16
EC_CAPACITY_FACTOR = 2
EXPERT_FF = D_MODEL

N_EVEN = (DEPTH + 1) // 2
N_ODD = DEPTH // 2
EPS = 1e-6

kernel_name = 'hybrid_mlstm_retention_natten_ecmoe_encoder'

def rms_norm(x, g):
    xf = x.astype(jnp.float32)
    y = xf * lax.rsqrt(jnp.mean(xf * xf, axis=-1, keepdims=True) + EPS)
    return (y * g.astype(jnp.float32)).astype(x.dtype)

def centred_depthwise_conv(x, w):
    k = w.shape[0]
    return lax.conv_general_dilated(
        x, w[:, None, :].astype(x.dtype), window_strides=(1,),
        padding=[((k - 1) // 2, k // 2)], dimension_numbers=('NWC', 'WIO', 'NWC'),
        feature_group_count=x.shape[-1])

def rotary(x, pos):
    half = x.shape[-1] // 2
    inv = ROPE_BASE ** (-jnp.arange(half, dtype=jnp.float32) / half)
    ang = pos.astype(jnp.float32)[:, None] * inv[None, :]
    cos, sin = jnp.cos(ang)[:, None, :], jnp.sin(ang)[:, None, :]
    x1, x2 = x[..., :half], x[..., half:]
    return jnp.concatenate([x1 * cos - x2 * sin, x2 * cos + x1 * sin], axis=-1)

def to_scan_order(x, reverse):
    meta, real = x[:, :N_META], x[:, N_META:]
    if reverse:
        real = jnp.flip(real, axis=1)
    pad = jnp.zeros((x.shape[0], META_PAD) + x.shape[2:], x.dtype)
    return jnp.concatenate([pad, meta, real], axis=1)

def from_scan_order(y, reverse):
    meta, real = y[:, META_PAD:CHUNK], y[:, CHUNK:]
    if reverse:
        real = jnp.flip(real, axis=1)
    return jnp.concatenate([meta, real], axis=1)

def to_chunks(x):
    b, lp = x.shape[:2]
    x = x.reshape((b, lp // CHUNK, CHUNK) + x.shape[2:])
    return jnp.moveaxis(x, (1, 3), (0, 2))

def from_chunks(y):
    y = jnp.moveaxis(y, (0, 2), (1, 3))
    return y.reshape((y.shape[0], y.shape[1] * y.shape[2]) + y.shape[3:])

def mlstm_scan(q, k, v, log_i, log_f):
    bsz, _, nh, dh = q.shape
    causal = jnp.tril(jnp.ones((CHUNK, CHUNK), bool))

    def step(carry, inp):
        c_st, n_st, m_prev = carry
        qt, kt, vt, it, ft = inp
        b = jnp.cumsum(ft, axis=-1)
        a = it - b
        m = b + jnp.maximum(m_prev[..., None], lax.cummax(a, axis=2))
        log_d = b[..., :, None] + a[..., None, :] - m[..., :, None]
        dmat = jnp.exp(jnp.where(causal, log_d, -jnp.inf))
        w_inter = jnp.exp(b + m_prev[..., None] - m)
        s = jnp.einsum('bhqd,bhkd->bhqk', qt, kt) * dmat
        num = (w_inter[..., None] * jnp.einsum('bhqd,bhde->bhqe', qt, c_st)
               + jnp.einsum('bhqk,bhke->bhqe', s, vt))
        den = w_inter * jnp.einsum('bhqd,bhd->bhq', qt, n_st) + s.sum(-1)
        out = num / jnp.maximum(jnp.abs(den), jnp.exp(-m))[..., None]
        m_new = m[..., -1]
        w_state = jnp.exp(b[..., -1] + m_prev - m_new)
        kw = kt * jnp.exp(b[..., -1:] + a - m_new[..., None])[..., None]
        c_new = w_state[..., None, None] * c_st + jnp.einsum('bhkd,bhke->bhde', kw, vt)
        n_new = w_state[..., None] * n_st + kw.sum(2)
        return (c_new, n_new, m_new), out

    init = (jnp.zeros((bsz, nh, dh, dh), jnp.float32), jnp.zeros((bsz, nh, dh), jnp.float32),
            jnp.zeros((bsz, nh), jnp.float32))
    _, ys = lax.scan(step, init, (to_chunks(q), to_chunks(k), to_chunks(v),
                                  to_chunks(log_i), to_chunks(log_f)))
    return from_chunks(ys)

def retention_scan(q, k, v, log_gamma):
    bsz, _, nh, dh = q.shape
    pos = jnp.arange(CHUNK, dtype=jnp.float32)
    causal = jnp.tril(jnp.ones((CHUNK, CHUNK), bool))
    rel = (pos[:, None] - pos[None, :])[None] * log_gamma[:, None, None]
    decay_intra = jnp.exp(jnp.where(causal[None], rel, -jnp.inf))
    decay_q = jnp.exp((pos + 1.0)[None, :] * log_gamma[:, None])
    decay_k = jnp.exp((CHUNK - 1.0 - pos)[None, :] * log_gamma[:, None])
    decay_chunk = jnp.exp(CHUNK * log_gamma)

    def step(r_st, inp):
        qt, kt, vt = inp
        s = jnp.einsum('bhqd,bhkd->bhqk', qt, kt) * decay_intra
        out = (jnp.einsum('bhqk,bhke->bhqe', s, vt)
               + decay_q[..., None] * jnp.einsum('bhqd,bhde->bhqe', qt, r_st))
        r_new = (decay_chunk[:, None, None] * r_st
                 + jnp.einsum('bhkd,bhke->bhde', kt * decay_k[..., None], vt))
        return r_new, out

    _, ys = lax.scan(step, jnp.zeros((bsz, nh, dh, dh), jnp.float32),
                     (to_chunks(q), to_chunks(k), to_chunks(v)))
    return from_chunks(ys)

def even_mixer(u, w_in, conv_w, gate_b, m_norm_g, ret_decay_logit, r_norm_g, w_out):
    f32 = jnp.float32
    bsz, seq_len, _ = u.shape
    sizes = [M_WIDTH] * 4 + [4 * M_HEADS] + [R_WIDTH] * 4
    cuts = np.cumsum(sizes)[:-1].tolist()
    mq, mk, mv, mo, gates, rq, rk, rv, rg = jnp.split(u @ w_in, cuts, axis=-1)

    def heads(t, nh):
        return t.reshape(bsz, seq_len, nh, -1).astype(f32)

    qk = jax.nn.silu(centred_depthwise_conv(jnp.concatenate([mq, mk], axis=-1), conv_w))
    mq, mk = jnp.split(qk, 2, axis=-1)
    q, k, v = heads(mq, M_HEADS), heads(mk, M_HEADS) * M_HEAD_DIM ** -0.5, heads(mv, M_HEADS)
    g = gates.astype(f32) + gate_b.astype(f32)
    i_fw, f_fw, i_bw, f_bw = jnp.split(g, 4, axis=-1)
    h_m = jnp.zeros_like(v)
    for reverse, ig, fg in ((False, i_fw, f_fw), (True, i_bw, f_bw)):
        o = mlstm_scan(to_scan_order(q, reverse), to_scan_order(k, reverse),
                       to_scan_order(v, reverse), to_scan_order(ig, reverse),
                       to_scan_order(jax.nn.log_sigmoid(fg), reverse))
        h_m = h_m + from_scan_order(o, reverse)
    m_out = (jax.nn.sigmoid(mo.astype(f32))
             * rms_norm(h_m, m_norm_g.reshape(M_HEADS, M_HEAD_DIM)).reshape(bsz, seq_len, M_WIDTH))

    pos = jnp.arange(seq_len)
    rq_h = rotary(heads(rq, R_HEADS), pos)
    rk_h = rotary(heads(rk, R_HEADS), pos) * R_HEAD_DIM ** -0.5
    rv_h = heads(rv, R_HEADS)
    log_gamma = jax.nn.log_sigmoid(ret_decay_logit.astype(f32))
    h_r = jnp.zeros_like(rv_h)
    for d_idx, reverse in ((0, False), (1, True)):
        o = retention_scan(to_scan_order(rq_h, reverse), to_scan_order(rk_h, reverse),
                           to_scan_order(rv_h, reverse), log_gamma[d_idx])
        h_r = h_r + from_scan_order(o, reverse)
    r_out = (jax.nn.silu(rg.astype(f32))
             * rms_norm(h_r, r_norm_g.reshape(R_HEADS, R_HEAD_DIM)).reshape(bsz, seq_len, R_WIDTH))

    mix = jnp.concatenate([m_out, r_out], axis=-1).astype(u.dtype)
    return mix @ w_out

def odd_mixer(u, w_in, q_norm_g, k_norm_g, rpb, w_out):
    f32 = jnp.float32
    bsz, seq_len, _ = u.shape
    n_tok = seq_len - N_META
    rows = n_tok // GRID_W
    wr = min(NA_WIN_ROWS, rows)
    z = (u @ w_in).reshape(bsz, seq_len, 3, NA_HEADS, NA_HEAD_DIM)
    q = rms_norm(z[:, :, 0], q_norm_g) * NA_HEAD_DIM ** -0.5
    k = rms_norm(z[:, :, 1], k_norm_g)
    v = z[:, :, 2]
    qm, km, vm = q[:, :N_META], k[:, :N_META], v[:, :N_META]
    grid = (bsz, rows, GRID_W, NA_HEADS, NA_HEAD_DIM)
    qg, kg, vg = (t[:, N_META:].reshape(grid) for t in (q, k, v))

    col = jnp.arange(GRID_W)
    col_start = jnp.clip(col - NA_WIN_COLS // 2, 0, GRID_W - NA_WIN_COLS)
    col_in = (col[None, :] >= col_start[:, None]) & (col[None, :] < col_start[:, None] + NA_WIN_COLS)
    dc_idx = jnp.clip(col[None, :] - col[:, None], -(NA_WIN_COLS - 1), NA_WIN_COLS - 1) + NA_WIN_COLS - 1
    rpb_cols = rpb.astype(f32)[:, :, dc_idx]

    p_meta = jax.nn.softmax(jnp.einsum('bqhd,bkhd->bhqk', qm, km).astype(f32), axis=-1)
    out_meta = jnp.einsum('bhqk,bkhd->bqhd', p_meta.astype(v.dtype), vm)

    def row_block(r):
        rs = jnp.clip(r - wr // 2, 0, rows - wr)
        q_row = lax.dynamic_index_in_dim(qg, r, axis=1, keepdims=False)
        k_band = lax.dynamic_slice_in_dim(kg, rs, wr, axis=1)
        v_band = lax.dynamic_slice_in_dim(vg, rs, wr, axis=1)
        s_band = jnp.einsum('bqhd,brkhd->bhqrk', q_row, k_band).astype(f32)
        dr_idx = rs + jnp.arange(wr) - r + NA_WIN_ROWS - 1
        bias = jnp.transpose(jnp.take(rpb_cols, dr_idx, axis=1), (0, 2, 1, 3))
        s_band = jnp.where(col_in[:, None, :], s_band + bias, -jnp.inf)
        s_band = s_band.reshape(bsz, NA_HEADS, GRID_W, wr * GRID_W)
        s_meta = jnp.einsum('bqhd,bkhd->bhqk', q_row, km).astype(f32)
        p = jax.nn.softmax(jnp.concatenate([s_meta, s_band], axis=-1), axis=-1).astype(v.dtype)
        v_flat = v_band.reshape(bsz, wr * GRID_W, NA_HEADS, NA_HEAD_DIM)
        return (jnp.einsum('bhqk,bkhd->bqhd', p[..., :N_META], vm)
                + jnp.einsum('bhqk,bkhd->bqhd', p[..., N_META:], v_flat))

    out_rows = lax.map(row_block, jnp.arange(rows))
    out_real = jnp.moveaxis(out_rows, 0, 1).reshape(bsz, n_tok, NA_WIDTH)
    out = jnp.concatenate([out_meta.reshape(bsz, N_META, NA_WIDTH), out_real], axis=1)
    return out @ w_out

def expert_choice_ffn(u, w_router, w_gate, w_up, w_down):
    bsz, seq_len, _ = u.shape
    cap = EC_CAPACITY_FACTOR * seq_len // N_EXPERTS
    aff = jax.nn.softmax((u @ w_router).astype(jnp.float32), axis=-1)
    gate, idx = lax.top_k(jnp.swapaxes(aff, 1, 2), cap)
    bidx = jnp.arange(bsz)[:, None, None]
    xs = u[bidx, idx]
    hdn = jax.nn.silu(jnp.einsum('becd,edf->becf', xs, w_gate)) * jnp.einsum('becd,edf->becf', xs, w_up)
    ys = jnp.einsum('becf,efd->becd', hdn, w_down) * gate[..., None].astype(u.dtype)
    return jnp.zeros_like(u).at[bidx, idx].add(ys)

def setup_inputs(seed: int = 0) -> dict:
    key = jax.random.key(seed)
    ks = iter(jax.random.split(key, 32))
    n = lambda shape: jax.random.normal(next(ks), shape, jnp.float32)
    fb = jnp.linspace(3.0, 6.0, M_HEADS)
    gate_b = jnp.concatenate([0.1 * n((N_EVEN, M_HEADS)), fb + 0.1 * n((N_EVEN, M_HEADS)),
                              0.1 * n((N_EVEN, M_HEADS)), fb + 0.1 * n((N_EVEN, M_HEADS))], axis=-1)
    base_logit = jnp.log(2.0 ** (5.0 + jnp.arange(R_HEADS, dtype=jnp.float32)) - 1.0)
    return {
        'x': n((BATCH, SEQ, D_MODEL)),
        'meta_tokens': n((N_META, D_MODEL)),
        'attn_norm_g': 1.0 + 0.02 * n((DEPTH, D_MODEL)),
        'ffn_norm_g': 1.0 + 0.02 * n((DEPTH, D_MODEL)),
        'even_w_in': n((N_EVEN, D_MODEL, EVEN_IN)) * D_MODEL ** -0.5,
        'even_conv_w': n((N_EVEN, M_CONV, 2 * M_WIDTH)) * M_CONV ** -0.5,
        'even_gate_b': gate_b,
        'even_m_norm_g': 1.0 + 0.02 * n((N_EVEN, M_WIDTH)),
        'even_ret_decay_logit': base_logit + 0.1 * n((N_EVEN, 2, R_HEADS)),
        'even_r_norm_g': 1.0 + 0.02 * n((N_EVEN, R_WIDTH)),
        'even_w_out': n((N_EVEN, EVEN_MIX, D_MODEL)) * EVEN_MIX ** -0.5,
        'odd_w_in': n((N_ODD, D_MODEL, ODD_IN)) * D_MODEL ** -0.5,
        'odd_q_norm_g': 1.0 + 0.02 * n((N_ODD, NA_HEAD_DIM)),
        'odd_k_norm_g': 1.0 + 0.02 * n((N_ODD, NA_HEAD_DIM)),
        'odd_rpb': 0.1 * n((N_ODD, NA_HEADS, 2 * NA_WIN_ROWS - 1, 2 * NA_WIN_COLS - 1)),
        'odd_w_out': n((N_ODD, NA_WIDTH, D_MODEL)) * NA_WIDTH ** -0.5,
        'router_w': n((DEPTH, D_MODEL, N_EXPERTS)) * D_MODEL ** -0.5,
        'expert_w_gate': n((DEPTH, N_EXPERTS, D_MODEL, EXPERT_FF)) * D_MODEL ** -0.5,
        'expert_w_up': n((DEPTH, N_EXPERTS, D_MODEL, EXPERT_FF)) * D_MODEL ** -0.5,
        'expert_w_down': n((DEPTH, N_EXPERTS, EXPERT_FF, D_MODEL)) * EXPERT_FF ** -0.5,
    }

def reference(x, meta_tokens, attn_norm_g, ffn_norm_g, even_w_in, even_conv_w, even_gate_b,
              even_m_norm_g, even_ret_decay_logit, even_r_norm_g, even_w_out, odd_w_in,
              odd_q_norm_g, odd_k_norm_g, odd_rpb, odd_w_out, router_w, expert_w_gate,
              expert_w_up, expert_w_down):
    bsz = x.shape[0]
    meta = jnp.broadcast_to(meta_tokens.astype(x.dtype)[None], (bsz, N_META, x.shape[-1]))
    h = jnp.concatenate([meta, x], axis=1)
    for layer in range(DEPTH):
        j = layer // 2
        u = rms_norm(h, attn_norm_g[layer])
        if layer % 2 == 0:
            h = h + even_mixer(u, even_w_in[j], even_conv_w[j], even_gate_b[j], even_m_norm_g[j],
                               even_ret_decay_logit[j], even_r_norm_g[j], even_w_out[j])
        else:
            h = h + odd_mixer(u, odd_w_in[j], odd_q_norm_g[j], odd_k_norm_g[j], odd_rpb[j], odd_w_out[j])
        h = h + expert_choice_ffn(rms_norm(h, ffn_norm_g[layer]), router_w[layer],
                                  expert_w_gate[layer], expert_w_up[layer], expert_w_down[layer])
    return h[:, N_META:]


_drawn_inputs = setup_inputs


def setup_inputs(seed=0):
    import zlib

    import numpy as np

    out = dict(_drawn_inputs(seed))
    spreads = {}
    factors = {'ffn_norm_g': 2.715,
     'even_m_norm_g': 4.306,
     'even_r_norm_g': 4.125,
     'odd_q_norm_g': 6.969,
     'odd_k_norm_g': 8.0,
     'odd_rpb': 3.963}
    for name, (base, spread) in spreads.items():
        noise = np.random.default_rng([zlib.crc32(name.encode()), seed]).standard_normal(out[name].shape)
        drawn = base * np.exp(spread * noise) if base else spread * noise
        out[name] = __import__('jax').numpy.asarray(drawn.astype(out[name].dtype))
    for name, factor in factors.items():
        out[name] = (out[name] * factor).astype(out[name].dtype)
    return out
```

```python
from contextlib import ExitStack

import numpy as np

import concourse.bass as bass
from concourse import mybir

ALU = mybir.AluOpType
ACT = mybir.ActivationFunctionType
AX = mybir.AxisListType
F32 = mybir.dt.float32
U32 = mybir.dt.uint32

D = 1024
KB = D // 128
NM = 16
NR = 512
T = NM + NR
NT = 5
GRID_W, GRID_H = 64, 8
EPS = 1e-6
BLK = 512
SLOTS = 6
HD = 128
NH = 4
CONV = 5
AH, AD = 16, 64
NE = 16
CAP = 2 * T // NE
FAR = 1e30
HEAD_SCALE = float(HD) ** -0.5
BAND = [(0, 192), (64, 256), (192, 256), (320, 192)]
BIAS_AT = [0, 208, 208, 480]
BIAS_N = 688
ARENA = 22600
PADS = 6


def rows_of(t):
    return NM if t == 0 else 128


def cols_of(t):
    return (0, NM) if t == 0 else (NM + 128 * (t - 1), NM + 128 * t)


def trunk(nc, a, out, upto=99, dbg=None):
    ctx = ExitStack()
    with ctx:
        def sb(name, shape, dt=F32):
            return ctx.enter_context(nc.sbuf_tensor(name, shape, dt))

        def sem(name):
            return ctx.enter_context(nc.semaphore(name))

        h_dram = nc.dram_tensor("h_mid", [T, D], F32, kind="Internal").ap()
        hn_dram = [nc.dram_tensor(f"h_normed{i}", [T, D], F32, kind="Internal").ap() for i in range(2)]

        ring = sb("ring", [128, SLOTS, KB, BLK])
        ident = sb("ident", [128, 128])
        gcol = sb("gcol", [128, 6, KB])
        small = sb("small", [128, 1600])
        uT = sb("uT", [128, KB, T])
        arena = sb("arena", [128, ARENA])
        bank = [ctx.enter_context(nc.psum_tensor(f"bank{i}", [128, 512], F32)) for i in range(8)]

        minus_half = small[:, 1599:1600]
        H = arena[:, ARENA - NT * D:ARENA].rearrange("p (t d) -> p t d", t=NT)

        def ar(off, n, **kw):
            assert off + n <= ARENA, (off, n)
            v = arena[:, off:off + n]
            if kw:
                names = " ".join(kw)
                v = v.rearrange(f"p ({names} z) -> p {names} z", **kw)
            return v

        def sm(off, n, **kw):
            v = small[:, off:off + n]
            if kw:
                names = " ".join(kw)
                v = v.rearrange(f"p ({names} z) -> p {names} z", **kw)
            return v

        ring_in = [sem(f"ring_in{i}") for i in range(SLOTS)]
        ring_used = [sem(f"ring_used{i}") for i in range(SLOTS)]
        fence = sem("fence")
        consts_in = sem("consts_in")
        dve_step = sem("dve_step")
        act_step = sem("act_step")
        pool_step = sem("pool_step")

        class Chain:

            def __init__(self, eng, s):
                self.eng, self.s, self.n = eng, s, 0

            def __call__(self, ins):
                self.n += 1
                ins.then_inc(self.s, 1)
                self.eng.wait_ge(self.s, self.n)

        fences = {}

        def fenced(eng):
            fences[eng] = fences.get(eng, 0) + 1
            eng.drain().then_inc(fence, 1)
            eng.wait_ge(fence, 4 * fences[eng])

        def ring_wait(pe, u):
            pe.wait_ge(ring_in[u % SLOTS], 16 * (u // SLOTS + 1))

        EVEN = 0
        MOE0 = 10
        ODD = MOE0 + 6 * NE
        MOE1 = ODD + 8
        even_cols = [0, 512, 1024, 1536, 2064, 2576, 3088, 3600]

        def block_of(w, c):
            return w[:, c:c + BLK].rearrange("(k p) c -> p k c", p=128)

        def stream_even(sp):
            sp.wait_ge(norms[0].in_, 16 * NT)
            for u in range(10):
                if u >= SLOTS:
                    sp.wait_ge(ring_used[u % SLOTS], u // SLOTS)
                src = block_of(a["even_w_in"], even_cols[u]) if u < 8 else block_of(a["even_w_out"], BLK * (u - 8))
                sp.dma_start(ring[:, u % SLOTS], src).then_inc(ring_in[u % SLOTS], 16)

        def stream_odd(sp):
            for j in range(8):
                u = ODD + j
                sp.wait_ge(ring_used[u % SLOTS], u // SLOTS)
                if j == 1:
                    sp.wait_ge(norms[2].in_, 16 * NT)
                src = block_of(a["odd_w_in"], BLK * j) if j < 6 else block_of(a["odd_w_out"], BLK * (j - 6))
                sp.dma_start(ring[:, u % SLOTS], src).then_inc(ring_in[u % SLOTS], 16)

        def stream_moe(sp, layer, base):
            names = ["expert_w_gate", "expert_w_up", "expert_w_gate", "expert_w_up", "expert_w_down", "expert_w_down"]
            half = [0, 0, 1, 1, 0, 1]
            with sp.Fori(0, NE) as e:
                for j in range(6):
                    s, n = (base + j) % SLOTS, (base + j) // SLOTS
                    w = a[names[j]][layer].rearrange("e (k p) c -> e p k c", p=128)
                    sp.wait_ge(ring_used[s], e + n)
                    sp.dma_start(ring[:, s], w[bass.ds(e, 1), :, :, BLK * half[j]:BLK * (half[j] + 1)]
                                 .rearrange("e p k c -> p (e k) c")).then_inc(ring_in[s], 16)

        STORES = [1 + 2 * (NT - 1), NT]

        class Norm:
            sq, ms, rs, hn, tr, ev = (sem("n_" + x) for x in ("squares", "mean", "rstd", "normed", "turned", "uT"))

            def __init__(self, k, gain, dram=None, real_rows=None, meta_rows=None):
                self.c, self.gain, self.dram = NT * k, gain, dram
                self.in_ = sem(f"n{k}_h_in")
                self.ss = small[:, 0:5]
                self.mean = small[:, 5:10]
                self.rstd = small[:, 10:15]
                self.hnorm = ar(8916, NT * D, t=NT)
                self.junk = ar(8916 + NT * D, D)

            def act_tile(self, act, t):
                n = rows_of(t)
                if t:
                    act.wait_ge(self.sq, self.c + t)
                act.activation(self.junk[0:n], H[0:n, t], ACT.Square,
                               accum_out=self.ss[0:n, t:t + 1]).then_inc(self.sq, 1)

            def dve_mean(self, dve, t):
                n = rows_of(t)
                dve.wait_ge(self.sq, self.c + t + 1)
                dve.tensor_scalar(self.mean[0:n, t:t + 1], self.ss[0:n, t:t + 1], 1.0 / D, EPS,
                                  ALU.mult, ALU.add).then_inc(self.ms, 1)

            def dve_scale(self, dve, t):
                n = rows_of(t)
                dve.wait_ge(self.rs, self.c + t + 1)
                dve.tensor_scalar(self.hnorm[0:n, t], H[0:n, t], self.rstd[0:n, t:t + 1], None,
                                  ALU.mult).then_inc(self.hn, 1)

            def dve_uT(self, dve, t):
                n = rows_of(t)
                c0, c1 = cols_of(t)
                for g in range(2):
                    dve.wait_ge(self.tr, 2 * self.c + 2 * t + g + 1)
                    ps = bank[4 + (2 * t + g) % 4][:, 0:4 * n].rearrange("p (k c) -> p k c", k=4)
                    dve.tensor_tensor(uT[:, 4 * g:4 * g + 4, c0:c1], ps,
                                      gcol[:, self.gain, 4 * g:4 * g + 4].unsqueeze(2).broadcast_to([128, 4, n]),
                                      ALU.mult).then_inc(self.ev, 1)

            def pool_tile(self, pool, t):
                n = rows_of(t)
                pool.wait_ge(self.ms, self.c + t + 1)
                pool.tensor_tensor(self.rstd[0:n, t:t + 1], self.mean[0:n, t:t + 1], minus_half[0:n, 0:1],
                                   ALU.pow).then_inc(self.rs, 1)

            def pe_tile(self, pe, t):
                n = rows_of(t)
                pe.wait_ge(self.hn, self.c + t + 1)
                for g in range(2):
                    i = 2 * t + g
                    if i >= 4:
                        pe.wait_ge(self.ev, 2 * self.c + i - 3)
                    for k in range(4):
                        ins = pe.transpose(bank[4 + i % 4][:, k * n:(k + 1) * n],
                                           self.hnorm[0:n, t, (4 * g + k) * 128:(4 * g + k + 1) * 128],
                                           ident[0:n, 0:n])
                    ins.then_inc(self.tr, 1)

            def act(self, act, step, h_in=0):
                for t in range(NT):
                    self.act_tile(act, t)

            def dve(self, dve, step):
                self.dve_mean(dve, 0)
                for t in range(NT):
                    if t + 1 < NT:
                        self.dve_mean(dve, t + 1)
                    self.dve_scale(dve, t)
                    if t:
                        self.dve_uT(dve, t - 1)
                self.dve_uT(dve, NT - 1)

            def pool(self, pool):
                for t in range(NT):
                    self.pool_tile(pool, t)

            def pe(self, pe):
                for t in range(NT):
                    self.pe_tile(pe, t)

        class Experts:
            consts_in, logits, sub, exp, aff_ready, affT, pos, posT_done, onehot, picked, chosen = (
                sem("sel_" + x) for x in ("consts_in", "logits", "sub", "exp", "aff_ready", "affT", "pos", "posT_done",
                                          "onehot", "picked", "chosen"))
            sent = sem("moe_sent")

            def __init__(self, layer, base, gain, normed, resid):
                self.l, self.base, self.gain, self.normed, self.resid = layer, base, gain, normed, resid
                L = f"m{layer}_"
                self.once = layer + 1
                (self.idx_g, self.idx_s, self.gathered, self.scattered, self.xs_turned, self.xT_in,
                 self.silu, self.hidden0, self.hidden1, self.h_turned, self.hT_in, self.y) = (
                    sem(L + x) for x in ("idx_g", "idx_s", "gathered", "scattered", "xs_turned", "xT_in", "silu", "hidden0",
                    "hidden1", "h_turned", "hT_in", "y"))
                self.wr = sm(1056 + 128 * layer, KB * NE, k=KB)
                self.iota = sm(1312, CAP)
                self.tok = sm(1378 + NT * layer, NT)
                self.P = ar(0, NT * NE * CAP, t=NT, e=NE)
                self.aff = ar(5280, NT * NE, t=NT)
                self.a2 = ar(5360, NT * NE * 2, t=NT, e=NE)
                self.stat = ar(5520, 20)
                self.m8 = ar(5540, 8)[0:NE]
                self.posT = ar(5548, NT * NE, t=NT)
                self.work = ar(5628, PADS + T)[0:NE]
                self.mask = ar(6162, T)[0:NE]
                self.cum = ar(6690, T)[0:NE]
                self.pick = ar(7218, T)[0:NE]
                self.ones = ar(7746, T)[0:NE]
                self.idx = sm(1388, NE).bitcast(U32)[0:CAP]
                self.gate = sm(1404, NE)[0:CAP]
                self.idxg = sm(1420, 1).bitcast(U32)[0:CAP]
                self.idxs = sm(1421, 1).bitcast(U32)[0:CAP]
                self.xs = ar(0, D)[0:CAP]
                self.sg = ar(1024, D)[0:CAP]
                self.hid = ar(2048, D)[0:CAP]
                self.y_sb = ar(3072, D)[0:CAP]
                self.xT = ar(4096, KB * CAP, k=KB)
                self.hT = ar(4700, KB * CAP, k=KB)

            def consts(self, act):
                act.dma_start(self.wr, a["router_w"][self.l].rearrange("(k p) e -> p k e", p=128)).then_inc(self.consts_in, 16)
                act.dma_start(self.tok, a["c_token"][self.l]).then_inc(self.consts_in, 16)
                if self.l == 0:
                    act.dma_start(self.iota, a["c_iota"][:, :]).then_inc(self.consts_in, 16)

            VIEWS = [(NM, 0, 1), (128, 1, NT)]

            def select_pe(self, pe):
                pe.wait_ge(self.consts_in, 80)
                pe.wait_ge(outs[self.l].added, 2 * NT * self.once)
                pe.wait_ge(Norm.ev, 4 * NT * self.once)
                lg = bank[0]
                for t in range(NT):
                    n = rows_of(t)
                    c0, c1 = cols_of(t)
                    for k in range(KB):
                        ins = pe.matmul(lg[0:n, t * NE:(t + 1) * NE], uT[:, k, c0:c1], self.wr[:, k],
                                        start=(k == 0), stop=(k == KB - 1))
                ins.then_inc(self.logits, 1)
                pe.wait_ge(self.aff_ready, self.once)
                for t in range(NT):
                    n = rows_of(t)
                    ps = bank[1][0:NE, 0:NM] if t == 0 else bank[2][0:NE, 128 * (t - 1):128 * t]
                    ins = pe.transpose(ps, self.aff[0:n, t], ident[0:n, 0:n])
                ins.then_inc(self.affT, 1)
                pe.wait_ge(self.pos, self.once)
                for t in range(NT):
                    n = rows_of(t)
                    c0, c1 = cols_of(t)
                    ins = pe.transpose(bank[3][0:n, t * NE:(t + 1) * NE], self.pick[:, c0:c1], ident[0:NE, 0:NE])
                ins.then_inc(self.posT_done, 1)
                pe.wait_ge(self.onehot, self.once)
                for e in range(NE):
                    for t in range(NT):
                        n = rows_of(t)
                        ins = pe.matmul(bank[4][0:CAP, 2 * e:2 * e + 2], self.P[0:n, t, e], self.a2[0:n, t, e],
                                        start=(t == 0), stop=(t == NT - 1))
                ins.then_inc(self.picked, 1)

            def select_act(self, act):
                act.wait_ge(self.sub, self.once)
                for n, t0, t1 in self.VIEWS:
                    ins = act.activation(self.aff[0:n, t0:t1], self.aff[0:n, t0:t1], ACT.Exp)
                    ins.then_inc(self.exp, 1)

            def select_dve(self, dve, step):
                dve.wait_ge(self.consts_in, 80)
                dve.wait_ge(self.logits, self.once)
                lg = bank[0][:, 0:NT * NE].rearrange("p (t e) -> p t e", t=NT)
                for n, t0, t1 in self.VIEWS:
                    w = t1 - t0
                    step(dve.tensor_reduce(self.stat[0:n, t0:t1], lg[0:n, t0:t1], AX.X, ALU.max))
                    ins = dve.tensor_tensor(self.aff[0:n, t0:t1], lg[0:n, t0:t1],
                                            self.stat[0:n, t0:t1].unsqueeze(2).broadcast_to([n, w, NE]), ALU.subtract)
                    if t0:
                        ins.then_inc(self.sub, 1)
                    else:
                        step(ins)
                dve.memset(self.ones, 1.0)
                dve.memset(self.work[:, 0:PADS], 2.0)
                step(dve.tensor_copy(self.a2[:, :, :, 0], self.tok.unsqueeze(2).broadcast_to([128, NT, NE])))
                dve.wait_ge(self.exp, 2 * self.once)
                for n, t0, t1 in self.VIEWS:
                    w = t1 - t0
                    step(dve.tensor_reduce(self.stat[0:n, 5 + t0:5 + t1], self.aff[0:n, t0:t1], AX.X, ALU.add))
                    step(dve.reciprocal(self.stat[0:n, 10 + t0:10 + t1], self.stat[0:n, 5 + t0:5 + t1]))
                    step(dve.tensor_tensor(self.aff[0:n, t0:t1], self.aff[0:n, t0:t1],
                                           self.stat[0:n, 10 + t0:10 + t1].unsqueeze(2).broadcast_to([n, w, NE]),
                                           ALU.mult))
                    ins = dve.tensor_copy(self.a2[0:n, t0:t1, :, 1], self.aff[0:n, t0:t1])
                    if t0:
                        ins.then_inc(self.aff_ready, 1)
                    else:
                        step(ins)
                dve.wait_ge(self.affT, self.once)
                step(dve.tensor_copy(self.work[:, PADS:PADS + NM], bank[1][0:NE, 0:NM]))
                grid = self.work[:, PADS + NM:]
                src = bank[2][0:NE, :]
                if self.l:
                    for b in range(4):
                        src_b = src[:, 128 * b:128 * b + 128].rearrange("p (c r) -> p r c", r=GRID_H)
                        step(dve.tensor_copy(grid.rearrange("p (r c) -> p r c", r=GRID_H)[:, :, 16 * b:16 * b + 16], src_b))
                else:
                    step(dve.tensor_copy(grid, src))
                for r in range((PADS + CAP) // 8):
                    step(dve.max(self.m8, self.work))
                    step(dve.match_replace(self.work, self.m8, self.work, -1.0))
                step(dve.tensor_scalar(self.mask, self.work[:, PADS:], 0.0, None, ALU.is_lt))
                step(dve.tensor_tensor_scan(self.cum, self.ones, self.mask, 0.0, ALU.mult, ALU.add))
                step(dve.tensor_tensor(self.pick[:, 0:NM], self.cum[:, 0:NM], self.mask[:, 0:NM], ALU.mult))
                if self.l:
                    for b in range(4):
                        cut = lambda x: x[:, NM:].rearrange("p (r c) -> p c r", r=GRID_H)[:, 16 * b:16 * b + 16, :]
                        dst = self.pick[:, NM + 128 * b:NM + 128 * b + 128].rearrange("p (c r) -> p c r", r=GRID_H)
                        ins = dve.tensor_tensor(dst, cut(self.cum), cut(self.mask), ALU.mult)
                        if b < 3:
                            step(ins)
                else:
                    ins = dve.tensor_tensor(self.pick[:, NM:], self.cum[:, NM:], self.mask[:, NM:], ALU.mult)
                ins.then_inc(self.pos, 1)
                dve.wait_ge(self.posT_done, self.once)
                pt = bank[3][:, 0:NT * NE].rearrange("p (t e) -> p t e", t=NT)
                for t in range(NT):
                    n = rows_of(t)
                    step(dve.tensor_copy(self.posT[0:n, t], pt[0:n, t]))
                    ins = dve.tensor_tensor(self.P[0:n, t], self.posT[0:n, t].unsqueeze(2).broadcast_to([n, NE, CAP]),
                                            self.iota[0:n].unsqueeze(1).broadcast_to([n, NE, CAP]), ALU.is_equal)
                    if t == NT - 1:
                        ins.then_inc(self.onehot, 1)
                    else:
                        step(ins)
                dve.wait_ge(self.picked, self.once)
                ps = bank[4][0:CAP, 0:2 * NE].rearrange("p (e x) -> p e x", x=2)
                step(dve.tensor_copy(self.idx, ps[:, :, 0]))
                dve.tensor_copy(self.gate, ps[:, :, 1]).then_inc(self.chosen, 1)

            def loop(self, eng, body):
                body(eng, 0, False)
                with eng.Fori(1, NE - 1) as e:
                    body(eng, e, False)
                body(eng, NE - 1, True)

            def freed(self, eng, s, value):
                if not (isinstance(value, int) and value == 0):
                    eng.wait_ge(s, value)

            def units(self, j):
                return (self.base + j) % SLOTS, (self.base + j) // SLOTS

            def turn_xs(self, pe, e, half):
                pe.wait_ge(self.gathered, e * 16 + 16)
                self.freed(pe, self.xT_in, e * 2 + half)
                for k in range(4):
                    c = 128 * (4 * half + k)
                    ins = pe.transpose(bank[7][:, k * CAP:(k + 1) * CAP], self.xs[:, c:c + 128], ident[0:CAP, 0:CAP])
                ins.then_inc(self.xs_turned, 1)

            def pe_body(self, pe, e, last):
                def product(ps, lhs, j, ks):
                    s, _ = self.units(j)
                    for k in ks:
                        ins = pe.matmul(ps, lhs[:, k], ring[:, s, k], start=(k == 0), stop=(k == KB - 1))
                    return ins

                def arrived(j):
                    s, n = self.units(j)
                    pe.wait_ge(ring_in[s], (e + n + 1) * 16)

                def used(j):
                    return ring_used[self.units(j)[0]]

                def turn_hidden(half):
                    pe.wait_ge(self.hidden[half], e + 1)
                    self.freed(pe, self.hT_in, e * 2 + half)
                    for k in range(4):
                        ins = pe.transpose(bank[6][:, k * CAP:(k + 1) * CAP],
                                           self.hid[:, half * BLK + 128 * k:half * BLK + 128 * k + 128],
                                           ident[0:CAP, 0:CAP])
                    ins.then_inc(self.h_turned, 1)

                pe.wait_ge(self.xT_in, e * 2 + 2)
                self.freed(pe, self.hidden[0], e)
                arrived(0)
                product(bank[0][0:CAP, :], self.xT, 0, range(KB)).then_inc(used(0), 1)
                arrived(1)
                product(bank[1][0:CAP, :], self.xT, 1, range(KB)).then_inc(used(1), 1)
                self.freed(pe, self.hidden[1], e)
                arrived(2)
                product(bank[2][0:CAP, :], self.xT, 2, range(KB)).then_inc(used(2), 1)
                turn_hidden(0)
                arrived(3)
                product(bank[3][0:CAP, :], self.xT, 3, range(KB)).then_inc(used(3), 1)
                pe.wait_ge(self.hT_in, e * 2 + 1)
                self.freed(pe, self.y, e * 2)
                arrived(4)
                product(bank[4][0:CAP, :], self.hT, 4, range(4))
                turn_hidden(1)
                arrived(5)
                product(bank[5][0:CAP, :], self.hT, 5, range(4))
                if not last:
                    self.turn_xs(pe, e + 1, 0)
                pe.wait_ge(self.hT_in, e * 2 + 2)
                product(bank[4][0:CAP, :], self.hT, 4, range(4, KB)).then_inc(used(4), 1)
                if not last:
                    self.turn_xs(pe, e + 1, 1)
                product(bank[5][0:CAP, :], self.hT, 5, range(4, KB)).then_inc(used(5), 1)

            def act_body(self, act, e, last):
                for half in range(2):
                    s, n = self.units(2 * half)
                    act.wait_ge(ring_used[s], e + n + 1)
                    self.freed(act, self.hidden[half], e)
                    act.activation(self.sg[:, half * BLK:half * BLK + BLK], bank[2 * half][0:CAP, :],
                                   ACT.Silu).then_inc(self.silu, 1)
                for half in range(2):
                    act.wait_ge(self.h_turned, e * 2 + half + 1)
                    act.activation(self.hT[:, 4 * half:4 * half + 4],
                                   bank[6][:, 0:4 * CAP].rearrange("p (k c) -> p k c", k=4),
                                   ACT.Copy).then_inc(self.hT_in, 1)

            def xT_copy(self, dve, e):
                for half in range(2):
                    dve.wait_ge(self.xs_turned, e * 2 + half + 1)
                    g = gcol[:, self.gain, 4 * half:4 * half + 4]
                    dve.tensor_tensor(self.xT[:, 4 * half:4 * half + 4],
                                      bank[7][:, 0:4 * CAP].rearrange("p (k c) -> p k c", k=4),
                                      g.unsqueeze(2).broadcast_to([128, 4, CAP]), ALU.mult).then_inc(self.xT_in, 1)

            def dve_body(self, dve, e, last):
                for half in range(2):
                    s, n = self.units(2 * half + 1)
                    dve.wait_ge(ring_used[s], e + n + 1)
                    dve.wait_ge(self.silu, e * 2 + half + 1)
                    dve.tensor_tensor(self.hid[:, half * BLK:half * BLK + BLK], self.sg[:, half * BLK:half * BLK + BLK],
                                      bank[2 * half + 1][0:CAP, :], ALU.mult).then_inc(self.hidden[half], 1)
                if not last:
                    self.xT_copy(dve, e + 1)
                self.freed(dve, self.scattered, e * 16)
                for half in range(2):
                    s, n = self.units(4 + half)
                    dve.wait_ge(ring_used[s], e + n + 1)
                    dve.tensor_scalar(self.y_sb[:, half * BLK:half * BLK + BLK], bank[4 + half][0:CAP, :],
                                      self.gate[:, bass.ds(e, 1)], None, ALU.mult).then_inc(self.y, 1)

            def gather(self, pool, e, count):
                pool.tensor_copy(self.idxg, self.idx[:, bass.ds(e, 1)]).then_inc(self.idx_g, 1)
                pool.wait_ge(self.idx_g, count)
                pool.sem_inc(self.sent, 1)
                pool.indirect_dma_start(out=self.xs, out_offset=None, in_=self.normed,
                                        in_offset=bass.IndirectOffsetOnAxis(ap=self.idxg, axis=0)).then_inc(self.gathered, 16)

            def pool_body(self, pool, e, last):
                self.freed(pool, self.scattered, e * 16)
                pool.tensor_copy(self.idxs, self.idx[:, bass.ds(e, 1)]).then_inc(self.idx_s, 1)
                if not last:
                    pool.wait_ge(self.xs_turned, e * 2 + 2)
                    self.gather(pool, e + 1, e + 2)
                pool.wait_ge(self.idx_s, e + 1)
                pool.wait_ge(self.y, e * 2 + 2)
                pool.sem_inc(self.sent, 1)
                pool.indirect_dma_start(out=self.resid, out_offset=bass.IndirectOffsetOnAxis(ap=self.idxs, axis=0),
                                        in_=self.y_sb, in_offset=None, compute_op=ALU.add).then_inc(self.scattered, 16)

        ex = []
        for layer in range(2):
            x = Experts(layer, MOE0 if layer == 0 else MOE1, 1 + 2 * layer, hn_dram[layer], h_dram if layer == 0 else out)
            x.hidden = [x.hidden0, x.hidden1]
            ex.append(x)

        EV, at = {}, 0
        for nm, n in (("rows", 4 * T), ("v1", NT * NH * (HD + 1)), ("qk", 8 * T), ("rqk", 8 * T),
                      ("sgo", NT * BLK), ("sgr", NT * BLK), ("rv", NT * BLK), ("tmp", 1780)):
            EV[nm] = at
            at += n
        EVT = {"v1": ar(EV["v1"], NT * NH * (HD + 1), t=NT, h=NH), "qk": ar(EV["qk"], 8 * T, k=8),
               "rqk": ar(EV["rqk"], 8 * T, k=8), "sgo": ar(EV["sgo"], NT * BLK, t=NT),
               "sgr": ar(EV["sgr"], NT * BLK, t=NT), "rv": ar(EV["rv"], NT * BLK, t=NT)}
        lgam = sm(1516, 8)
        uflat = uT[:, :, :].rearrange("p k t -> p (k t)")

        class EvenIn:
            ORDER = ["mq", "mk", "mv", "mo", "rq", "rk", "rv", "rg"]

            def __init__(self):
                (self.consts_in, self.product, self.taken, self.raw, self.conv, self.gate_product,
                 self.gate_copied, self.gate_turned, self.rope, self.turned, self.turned_taken,
                 self.pad) = (
                    sem("ei_" + x) for x in ("consts_in", "product", "taken", "raw", "conv", "gate_product", "gate_copied",
                    "gate_turned", "rope", "turned", "turned_taken", "pad"))
                self.convw = sm(20, 2 * NH * CONV, f=2 * NH)
                self.wg = sm(60, KB * 16, k=KB)
                self.gtok = sm(188, NT * 16, t=NT)
                self.rows = [ar(EV["rows"] + i * T, T)[0:NH] for i in range(4)]
                self.gb = sm(268, 4)[0:NH]
                self.rawbuf = [ar(EV["tmp"] + i * (T + 4), T + 4) for i in range(2)]
                self.rope_a, self.rope_b, self.rope_o = (ar(EV["tmp"] + i * BLK, BLK) for i in range(3))
                self.cs = sm(280, NT * 128, t=NT)
                self.groups = []
                for u in range(8):
                    n = 4 if u < 2 else NT
                    self.groups += [(u, i) for i in range(n)]

            def consts(self, act):
                act.dma_start(self.convw, a["even_conv_w"][:, :, :]).then_inc(self.consts_in, 16)
                act.dma_start(self.wg, a["even_w_in"][:, 2048:2064].rearrange("(k p) c -> p k c", p=128)).then_inc(self.consts_in, 16)
                act.dma_start(self.gb, a["even_gate_b"].rearrange("(t h) -> h t", h=NH),
                              allow_slow_non_contiguous=True).then_inc(self.consts_in, 16)
                act.dma_start(self.cs, a["c_rope"][:, :, :]).then_inc(self.consts_in, 16)

            def pe(self, pe):
                pe.wait_ge(self.consts_in, 64)
                for t in range(NT):
                    n = rows_of(t)
                    c0, c1 = cols_of(t)
                    for k in range(KB):
                        ins = pe.matmul(bank[6][0:n, 16 * t:16 * t + 16], uT[:, k, c0:c1], self.wg[:, k],
                                        start=(k == 0), stop=(k == KB - 1))
                ins.then_inc(self.gate_product, 1)
                pe.wait_ge(self.gate_copied, 1)
                for i in range(4):
                    for t in range(NT):
                        n = rows_of(t)
                        ps = bank[4][0:NH, i * NM:(i + 1) * NM] if t == 0 else bank[i][0:NH, 128 * (t - 1):128 * t]
                        ins = pe.transpose(ps, self.gtok[0:n, t, 4 * i:4 * i + 4], ident[0:n, 0:n])
                ins.then_inc(self.gate_turned, 1)
                pe.wait_ge(self.gate_copied, 2)
                turn = 0
                for g, (u, i) in enumerate(self.groups):
                    if i == 0:
                        ring_wait(pe, u)
                    s = u % SLOTS
                    if g >= 4:
                        pe.wait_ge(self.taken, g - 3)
                    b = bank[g % 4]
                    if u < 2:
                        for k in range(KB):
                            pe.matmul(b[:, :], ring[:, s, k, 128 * i:128 * i + 128], uT[:, k, NM:T],
                                      start=(k == 0), stop=(k == KB - 1))
                        if g >= 2:
                            pe.wait_ge(self.taken, g - 1)
                        for k in range(KB):
                            ins = pe.matmul(bank[4 + g % 2][:, 0:NM], ring[:, s, k, 128 * i:128 * i + 128], uT[:, k, 0:NM],
                                            start=(k == 0), stop=(k == KB - 1))
                    else:
                        c0, c1 = cols_of(i)
                        for k in range(KB):
                            ins = pe.matmul(b[0:rows_of(i), :], uT[:, k, c0:c1], ring[:, s, k],
                                            start=(k == 0), stop=(k == KB - 1))
                    ins.then_inc(self.product, 1)
                    for u2, i2 in ([self.groups[g - 1]] if self.groups[g - 1][0] in (4, 5) and g else []):
                        n = rows_of(i2)
                        pe.wait_ge(self.rope, turn + 1)
                        if turn >= 2:
                            pe.wait_ge(self.turned_taken, turn - 1)
                        for h in range(NH):
                            ins2 = pe.transpose(bank[6 + turn % 2][:, h * n:(h + 1) * n],
                                                self.rope_o[0:n, 128 * h:128 * h + 128], ident[0:n, 0:n])
                        ins2.then_inc(self.turned, 1)
                        turn += 1
                    if i == (3 if u < 2 else NT - 1):
                        pe.wait_ge(self.product, g + 1)
                        pe.sem_inc(ring_used[s], 1)

            def act(self, act, step):
                for g, (u, i) in enumerate(self.groups):
                    n = rows_of(i)
                    b = bank[g % 4]
                    if u < 2:
                        f = 4 * u + i
                        act.wait_ge(self.product, g + 1)
                        if f >= 2:
                            act.wait_ge(self.conv, f - 1)
                        else:
                            act.wait_ge(self.pad, 1)
                        step(act.activation(self.rawbuf[f % 2][:, 2:2 + NM], bank[4 + g % 2][:, 0:NM], ACT.Copy))
                        act.activation(self.rawbuf[f % 2][:, 2 + NM:2 + T], b[:, :], ACT.Copy).then_inc(self.taken, 1)
                        if f >= 1:
                            self.silu_conv(act, f - 1)
                        if f == 7:
                            self.silu_conv(act, 7)
                    elif u in (4, 5):
                        if u == 4:
                            continue
                    else:
                        act.wait_ge(self.product, g + 1)
                        act.wait_ge(self.taken, g)
                        if u == 2:
                            dst = EVT["v1"][0:n, i, :, 0:HD]
                            act.activation(dst, b[0:n, :].rearrange("p (h e) -> p h e", h=NH), ACT.Copy).then_inc(self.taken, 1)
                        else:
                            dst, f = {3: (EVT["sgo"], ACT.Sigmoid), 6: (EVT["rv"], ACT.Copy), 7: (EVT["sgr"], ACT.Silu)}[u]
                            act.activation(dst[0:n, i], b[0:n, :], f).then_inc(self.taken, 1)

            def silu_conv(self, act, f):
                act.wait_ge(self.conv, f + 1)
                act.activation(EVT["qk"][:, f], EVT["qk"][:, f], ACT.Silu).then_inc(self.raw, 1)

            def dve(self, dve, step):
                for r in self.rawbuf:
                    step(dve.memset(r[:, 0:2], 0.0))
                    ins = dve.memset(r[:, T + 2:T + 4], 0.0)
                    if r is self.rawbuf[1]:
                        ins.then_inc(self.pad, 1)
                    else:
                        step(ins)
                step(dve.memset(EVT["v1"][:, :, :, HD:HD + 1], 1.0))
                dve.wait_ge(self.gate_product, 1)
                step(dve.tensor_copy(self.gtok[0:NM, 0], bank[6][0:NM, 0:16]))
                dve.tensor_copy(self.gtok[:, 1:NT], bank[6][:, 16:80].rearrange("p (t c) -> p t c", t=4)).then_inc(self.gate_copied, 1)
                dve.wait_ge(self.gate_turned, 1)
                for i in range(4):
                    gb = self.gb[:, i:i + 1]
                    step(dve.tensor_scalar(self.rows[i][:, 0:NM], bank[4][0:NH, i * NM:(i + 1) * NM], gb, None, ALU.add))
                    ins = dve.tensor_scalar(self.rows[i][:, NM:T], bank[i][0:NH, :], gb, None, ALU.add)
                    if i < 3:
                        step(ins)
                    else:
                        ins.then_inc(self.gate_copied, 1)
                turn = 0
                for g, (u, i) in enumerate(self.groups):
                    n = rows_of(i)
                    b = bank[g % 4]
                    if u < 2:
                        f = 4 * u + i
                        dve.wait_ge(self.taken, g + 1)
                        raw, acc = self.rawbuf[f % 2], EVT["qk"][:, f]
                        step(dve.tensor_scalar(acc, raw[:, 0:T], self.convw[:, f, 0:1], None, ALU.mult))
                        for w in range(1, CONV):
                            ins = dve.scalar_tensor_tensor(acc, raw[:, w:w + T], self.convw[:, f, w:w + 1], acc,
                                                           ALU.mult, ALU.add)
                            if w < CONV - 1:
                                step(ins)
                            else:
                                ins.then_inc(self.conv, 1)
                    elif u in (4, 5):
                        dve.wait_ge(self.product, g + 1)
                        dve.wait_ge(self.taken, g)
                        x = b[0:n, :].rearrange("p (h s e) -> p h s e", h=NH, s=2)
                        xv = lambda y: y[0:n].rearrange("p (h s e) -> p h s e", h=NH, s=2)
                        cos = self.cs[0:n, i, 0:64].unsqueeze(1).broadcast_to([n, NH, 64])
                        sin = self.cs[0:n, i, 64:128].unsqueeze(1).broadcast_to([n, NH, 64])
                        A, B, O = xv(self.rope_a), xv(self.rope_b), xv(self.rope_o)
                        if turn:
                            dve.wait_ge(self.turned, turn)
                        step(dve.tensor_tensor(A[:, :, 0], x[:, :, 0], cos, ALU.mult))
                        step(dve.tensor_tensor(A[:, :, 1], x[:, :, 1], cos, ALU.mult))
                        step(dve.tensor_tensor(B[:, :, 0], x[:, :, 1], sin, ALU.mult))
                        dve.tensor_tensor(B[:, :, 1], x[:, :, 0], sin, ALU.mult).then_inc(self.taken, 1)
                        dve.wait_ge(self.taken, g + 1)
                        step(dve.tensor_tensor(O[:, :, 0], A[:, :, 0], B[:, :, 0], ALU.subtract))
                        dve.tensor_tensor(O[:, :, 1], A[:, :, 1], B[:, :, 1], ALU.add).then_inc(self.rope, 1)
                        if turn:
                            self.copy_turned(dve, turn - 1)
                        turn += 1
                self.copy_turned(dve, turn - 1)

            def copy_turned(self, dve, turn):
                u, i = turn // NT, turn % NT
                n = rows_of(i)
                c0, c1 = cols_of(i)
                dve.wait_ge(self.turned, turn + 1)
                dve.tensor_copy(EVT["rqk"][:, 4 * u:4 * u + 4, c0:c1],
                                bank[6 + turn % 2][:, 0:4 * n].rearrange("p (h c) -> p h c", h=NH)).then_inc(self.turned_taken, 1)

        class Gates:

            def __init__(self, rows):
                (self.neg, self.soft, self.rows, self.m, self.turned, self.lneg, self.lsoft,
                 self.logit_in) = (
                    sem("g_" + x) for x in ("neg", "soft", "rows", "m", "turned", "lneg", "lsoft", "logit_in"))
                self.raw = rows
                self.logit, self.lg_e = sm(1500, 8), sm(1508, 8)
                z = [uT[0:NH, i] for i in range(7)]
                self.t, self.ones, self.zeros = z[0], z[1], z[2]
                self.F, self.em = z[3:5], z[5:7]
                self.Mx = [ar(EV["tmp"] + i * T, T)[0:NH] for i in range(2)]
                self.cols_sb = ar(EV["tmp"] + 2 * T, 2 * 2 * NT * NH, d=2, x=2, t=NT)

            def order(self, d, x):
                return x[:, NM:T] if d == 0 else x[:, T - 1:NM - 1:-1]

            def act(self, act, step):
                for d in range(2):
                    act.wait_ge(self.neg, d + 1)
                    step(act.activation(self.em[d], self.em[d], ACT.Exp))
                    act.activation(self.em[d], self.em[d], ACT.Ln, bias=1.0).then_inc(self.soft, 1)
                act.wait_ge(self.lneg, 1)
                step(act.activation(self.lg_e, self.lg_e, ACT.Exp))
                act.activation(self.lg_e, self.lg_e, ACT.Ln, bias=1.0).then_inc(self.lsoft, 1)
                act.wait_ge(self.m, 1)
                for d in range(2):
                    act.activation(self.em[d], self.em[d], ACT.Exp, scale=-1.0).then_inc(self.rows, 1)

            def dve(self, dve, step):
                step(dve.memset(self.ones, 1.0))
                step(dve.memset(self.zeros, 0.0))
                for d in range(2):
                    f = self.raw[2 * d + 1]
                    dve.scalar_tensor_tensor(self.em[d], f, -1.0, f, ALU.mult, ALU.min).then_inc(self.neg, 1)
                dve.wait_ge(self.logit_in, 16)
                dve.scalar_tensor_tensor(self.lg_e, self.logit, -1.0, self.logit, ALU.mult, ALU.min).then_inc(self.lneg, 1)
                dve.wait_ge(self.lsoft, 1)
                step(dve.scalar_tensor_tensor(lgam, self.logit, 0.0, self.lg_e, ALU.min, ALU.subtract))
                for d in range(2):
                    i, f = self.raw[2 * d], self.raw[2 * d + 1]
                    F, M = self.F[d], self.Mx[d]
                    dve.wait_ge(self.soft, d + 1)
                    step(dve.scalar_tensor_tensor(self.t, f, 0.0, self.em[d], ALU.min, ALU.subtract))
                    step(dve.tensor_tensor_scan(F[:, 0:NM], self.ones[:, 0:NM], self.t[:, 0:NM], 0.0, ALU.mult, ALU.add))
                    step(dve.tensor_tensor_scan(self.order(d, F), self.ones[:, NM:T], self.order(d, self.t),
                                                F[:, NM - 1:NM], ALU.mult, ALU.add))
                    step(dve.tensor_tensor(i, i, F, ALU.subtract))
                    step(dve.tensor_tensor_scan(M[:, 0:NM], self.zeros[:, 0:NM], i[:, 0:NM], 0.0, ALU.add, ALU.max))
                    step(dve.tensor_tensor_scan(self.order(d, M), self.zeros[:, NM:T], self.order(d, i),
                                                M[:, NM - 1:NM], ALU.add, ALU.max))
                    ins = dve.tensor_tensor(self.em[d], F, M, ALU.add)
                    if d:
                        ins.then_inc(self.m, 1)
                    else:
                        step(ins)
                dve.wait_ge(self.turned, 1)
                ps = bank[0][:, 0:2 * 2 * NT * NH].rearrange("p (d x t h) -> p d x t h", d=2, x=2, t=NT)
                for d in range(2):
                    for x in range(2):
                        step(dve.tensor_copy(self.cols_sb[0:NM, d, x, 0], ps[0:NM, d, x, 0]))
                        step(dve.tensor_copy(self.cols_sb[:, d, x, 1:NT], ps[:, d, x, 1:NT]))

            def pe(self, pe):
                pe.wait_ge(self.rows, 2)
                for d in range(2):
                    for x, row in enumerate((self.raw[2 * d], self.em[d])):
                        for t in range(NT):
                            n = rows_of(t)
                            c0, c1 = cols_of(t)
                            o = ((d * 2 + x) * NT + t) * NH
                            ins = pe.transpose(bank[0][0:n, o:o + NH], row[:, c0:c1], ident[0:NH, 0:NH])
                ins.then_inc(self.turned, 1)

            def a_col(self, d, t, h):
                return self.cols_sb[0:rows_of(t), d, 0, t, h:h + 1]

            def em_col(self, d, t0, t1, n, h):
                return self.cols_sb[0:n, d, 1, t0:t1, h]

        def qcols(kt, d):
            return (128 * kt, NR) if d == 0 else (0, 128 * kt + 128)

        PACK = [[0, 512, 896, 1152], [0, 128, 384, 768]]
        TRI = 1280

        class HeadNorm:

            def __init__(self, k, gate):
                self.sq, self.ms, self.rs, self.done = (sem(f"hn{k}_{x}") for x in ("sq", "ms", "rs", "done"))
                self.gate = gate
                self.buf = [ar(EV["tmp"] + 2 * T + 80, NT * HD, t=NT), ar(EV["rows"], NT * HD, t=NT)]
                self.junk = ar(EV["rows"] + 640, HD)
                self.ss, self.mean, self.rstd = (sm(1524 + 5 * i, 5) for i in range(3))

            def act(self, act, h):
                for t in range(NT):
                    n = rows_of(t)
                    if NT * h + t:
                        act.wait_ge(self.sq, NT * h + t)
                    act.activation(self.junk[0:n], self.buf[h % 2][0:n, t], ACT.Square,
                                   accum_out=self.ss[0:n, t:t + 1]).then_inc(self.sq, 1)

            def dve_mean(self, dve, h):
                dve.wait_ge(self.sq, NT * (h + 1))
                if h:
                    dve.wait_ge(self.rs, 2 * h)
                for n, t0, t1 in ((NM, 0, 1), (128, 1, NT)):
                    dve.tensor_scalar(self.mean[0:n, t0:t1], self.ss[0:n, t0:t1], 1.0 / HD, EPS, ALU.mult,
                                      ALU.add).then_inc(self.ms, 1)

            def pool(self, pool, h):
                for i, (n, t0, t1) in enumerate(((NM, 0, 1), (128, 1, NT))):
                    pool.wait_ge(self.ms, 2 * h + i + 1)
                    if h:
                        pool.wait_ge(self.done, h)
                    pool.tensor_tensor(self.rstd[0:n, t0:t1], self.mean[0:n, t0:t1],
                                       minus_half[0:n, 0:1].broadcast_to([n, t1 - t0]), ALU.pow).then_inc(self.rs, 1)

            def dve_apply(self, dve, h):
                dve.wait_ge(self.rs, 2 * h + 2)
                for t in range(NT):
                    n = rows_of(t)
                    g = self.gate[0:n, t, HD * h:HD * h + HD]
                    ins = dve.scalar_tensor_tensor(g, self.buf[h % 2][0:n, t], self.rstd[0:n, t:t + 1], g,
                                                   ALU.mult, ALU.mult)
                ins.then_inc(self.done, 1)

        OUT_AT = [(6, 2 * (HD + 1)), (6, 0), (6, HD + 1), (7, 0), (7, HD + 1)]

        class MLSTM:

            def __init__(self, gates):
                (self.mbc, self.diag, self.dexp, self.sprod, self.sd, self.oprod, self.comb,
                 self.pre, self.pre_d, self.pre_e, self.pre_sd, self.masks_in) = (
                    sem("ml_" + x) for x in ("mbc", "diag", "dexp", "sprod", "sd", "oprod", "comb", "pre", "pre_d", "pre_e", "pre_sd",
                    "masks_in"))
                self.g = gates
                self.D = [uflat[:, d * TRI:(d + 1) * TRI] for d in range(2)]
                self.Dm = [uflat[0:NM, 2 * TRI + d * NR:2 * TRI + (d + 1) * NR] for d in range(2)]
                self.Dmm = uflat[0:NM, 2 * TRI + 2 * NR:2 * TRI + 2 * NR + 2 * NH * NM].rearrange("p (d h q) -> p d h q", d=2, h=NH)
                self.sel = sm(280, NH * 128, h=NH)[0:NH]
                self.far = sm(800, 256, d=2)
                self.dn = sm(1540, 5)
                self.rd = sm(1545, 5)
                self.norm = HeadNorm(0, EVT["sgo"])

            def consts(self, act):
                act.dma_start(self.sel, a["c_sel"][:, :, :]).then_inc(self.masks_in, 16)
                act.dma_start(self.far, a["c_far"][:, :, :]).then_inc(self.masks_in, 16)

            def q(self, h):
                return EVT["qk"][:, h]

            def k(self, h):
                return EVT["qk"][:, NH + h]

            def pe(self, pe):
                pe.wait_ge(self.masks_in, 32)
                for h in range(NH):
                    pe.matmul(bank[7][0:NM, 128 + NM * h:128 + NM * h + NM], self.k(h)[:, 0:NM], self.q(h)[:, 0:NM],
                              start=True, stop=True)
                for d in range(2):
                    for h in range(NH):
                        o = NM * (NH * d + h)
                        ins = pe.matmul(bank[7][0:NM, o:o + NM], self.sel[:, h, 0:NM], self.g.Mx[d][:, 0:NM],
                                        start=True, stop=True)
                ins.then_inc(self.pre, 1)

                def scores(h):
                    if h:
                        pe.wait_ge(self.sd, 2 * h)
                    for kt in range(4):
                        pe.matmul(bank[kt][:, :], self.k(h)[:, NM + 128 * kt:NM + 128 * kt + 128], self.q(h)[:, NM:T],
                                  start=True, stop=True)
                    pe.matmul(bank[4][0:NM, :], self.k(h)[:, 0:NM], self.q(h)[:, NM:T], start=True,
                              stop=True).then_inc(self.sprod, 1)

                def maxima(s):
                    h, d = s // 2, s % 2
                    if s:
                        pe.wait_ge(self.dexp, s)
                    pe.matmul(bank[5][:, :], self.sel[:, h], self.g.Mx[d][:, NM:T], start=True, stop=True).then_inc(self.mbc, 1)

                scores(0)
                maxima(0)
                pe.wait_ge(self.pre_sd, 2)
                for s in range(2 * NH):
                    h, d = s // 2, s % 2
                    if s < 2 * NH - 1:
                        maxima(s + 1)
                    pe.wait_ge(self.sd, s + 1)
                    if d and h < NH - 1:
                        scores(h + 1)
                    if s:
                        pe.wait_ge(self.comb, s)
                    for t in range(1, NT):
                        qt = t - 1
                        bk, o = OUT_AT[t]
                        ps = bank[bk][:, o:o + HD + 1]
                        pe.matmul(ps, self.Dm[d][:, 128 * qt:128 * qt + 128], EVT["v1"][0:NM, 0, h], start=True, stop=False)
                        kts = range(0, qt + 1) if d == 0 else range(qt, 4)
                        for kt in kts:
                            c = PACK[d][kt] + 128 * qt - qcols(kt, d)[0]
                            ins = pe.matmul(ps, self.D[d][:, c:c + 128], EVT["v1"][:, kt + 1, h], start=False,
                                            stop=(kt == kts[-1]))
                    bk, o = OUT_AT[0]
                    pe.matmul(bank[bk][0:NM, o:o + HD + 1], self.Dmm[:, d, h], EVT["v1"][0:NM, 0, h], start=True,
                              stop=True).then_inc(self.oprod, 1)

            def act(self, act, step):
                act.wait_ge(self.pre_d, 1)
                act.activation(self.Dmm, self.Dmm, ACT.Exp, scale=-1.0).then_inc(self.pre_e, 1)
                for s in range(2 * NH):
                    h, d = s // 2, s % 2
                    act.wait_ge(self.diag, s + 1)
                    for kt in range(4):
                        c0, c1 = qcols(kt, d)
                        o = PACK[d][kt]
                        if d == 0:
                            c0, o = c0 + 128, o + 128
                        else:
                            c1 -= 128
                        if c1 > c0:
                            act.activation(self.D[d][:, o:o + c1 - c0], bank[5][:, c0:c1], ACT.Exp,
                                           bias=self.g.a_col(d, kt + 1, h), scale=-1.0)
                    act.activation(self.Dm[d], bank[5][0:NM, :], ACT.Exp, bias=self.g.a_col(d, 0, h), scale=-1.0)
                    for kt in range(4):
                        o = PACK[d][kt] + (0 if d == 0 else 128 * kt)
                        ins = act.activation(self.D[d][:, o:o + 128], self.D[d][:, o:o + 128], ACT.Exp, scale=-1.0)
                    ins.then_inc(self.dexp, 1)
                    if d == 0 and h:
                        self.squares(act, h - 1)
                self.squares(act, NH - 1)

            def squares(self, act, h):
                act.wait_ge(self.comb, 2 * h + 2)
                self.norm.act(act, h)

            def dve(self, dve, step):
                def diag(s):
                    h, d = s // 2, s % 2
                    dve.wait_ge(self.mbc, s + 1)
                    if s >= 2:
                        dve.wait_ge(self.oprod, s - 1)
                    for kt in range(4):
                        o = PACK[d][kt] + (0 if d == 0 else 128 * kt)
                        ins = dve.scalar_tensor_tensor(self.D[d][:, o:o + 128], bank[5][:, 128 * kt:128 * kt + 128],
                                                       self.g.a_col(d, kt + 1, h), self.far[:, d], ALU.subtract, ALU.max)
                    ins.then_inc(self.diag, 1)

                def weigh(s):
                    h, d = s // 2, s % 2
                    dve.wait_ge(self.sprod, h + 1)
                    dve.wait_ge(self.dexp, s + 1)
                    for kt in range(4):
                        c0, c1 = qcols(kt, d)
                        o = PACK[d][kt]
                        x = self.D[d][:, o:o + c1 - c0]
                        dve.scalar_tensor_tensor(x, bank[kt][:, c0:c1], HEAD_SCALE, x, ALU.mult, ALU.mult)
                    dve.scalar_tensor_tensor(self.Dm[d], bank[4][0:NM, :], HEAD_SCALE, self.Dm[d], ALU.mult,
                                             ALU.mult).then_inc(self.sd, 1)

                def combine(s):
                    h, d = s // 2, s % 2
                    hm = self.norm.buf[h % 2]
                    dve.wait_ge(self.oprod, s + 1)
                    if d == 0 and h >= 2:
                        dve.wait_ge(self.norm.done, h - 1)
                    for (n, t0, t1, bk, o) in ((NM, 0, 1, 6, 2 * (HD + 1)), (128, 1, 3, 6, 0), (128, 3, 5, 7, 0)):
                        den = bank[bk][0:n, o + HD:o + HD + (HD + 1) * (t1 - t0 - 1) + 1:HD + 1]
                        step(dve.scalar_tensor_tensor(self.dn[0:n, t0:t1], den, -1.0, self.g.em_col(d, t0, t1, n, h),
                                                      ALU.mult, ALU.max))
                        step(dve.tensor_tensor(self.dn[0:n, t0:t1], den, self.dn[0:n, t0:t1], ALU.max))
                        step(dve.reciprocal(self.rd[0:n, t0:t1], self.dn[0:n, t0:t1]))
                    for t in range(NT):
                        n = rows_of(t)
                        bk, o = OUT_AT[t]
                        num = bank[bk][0:n, o:o + HD]
                        if d == 0:
                            ins = dve.tensor_scalar(hm[0:n, t], num, self.rd[0:n, t:t + 1], None, ALU.mult)
                        else:
                            ins = dve.scalar_tensor_tensor(hm[0:n, t], num, self.rd[0:n, t:t + 1], hm[0:n, t],
                                                           ALU.mult, ALU.add)
                    ins.then_inc(self.comb, 1)
                    dve.wait_ge(self.comb, s + 1)

                dve.wait_ge(self.pre, 1)
                for d in range(2):
                    for h in range(NH):
                        o = NM * (NH * d + h)
                        ins = dve.scalar_tensor_tensor(self.Dmm[:, d, h], bank[7][0:NM, o:o + NM], self.g.a_col(d, 0, h),
                                                       self.far[0:NM, 0, 0:NM], ALU.subtract, ALU.max)
                ins.then_inc(self.pre_d, 1)
                dve.wait_ge(self.pre_e, 1)
                for d in range(2):
                    dve.scalar_tensor_tensor(self.Dmm[:, d], bank[7][0:NM, 128:128 + NH * NM].rearrange("p (h q) -> p h q", h=NH),
                                             HEAD_SCALE, self.Dmm[:, d], ALU.mult, ALU.mult).then_inc(self.pre_sd, 1)
                diag(0)
                for s in range(2 * NH):
                    h, d = s // 2, s % 2
                    weigh(s)
                    if s < 2 * NH - 1:
                        diag(s + 1)
                    if s:
                        combine(s - 1)
                    if d and h:
                        self.norm.dve_mean(dve, h - 1)
                        self.norm.dve_apply(dve, h - 1)
                combine(2 * NH - 1)
                self.norm.dve_mean(dve, NH - 1)
                self.norm.dve_apply(dve, NH - 1)

            def pool(self, pool):
                for h in range(NH):
                    self.norm.pool(pool, h)

        class Retention:

            def __init__(self):
                (self.consts_in, self.pre, self.table, self.sprod, self.sd, self.oprod, self.comb,
                 self.mm, self.mexp, self.msd) = (
                    sem("re_" + x) for x in ("consts_in", "pre", "table", "sprod", "sd", "oprod", "comb", "mm", "mexp", "msd"))
                self.SD = uflat[:, 0:4 * NR].rearrange("p (k q) -> p k q", k=4)
                self.SDm = uflat[0:NM, 4 * NR:5 * NR]
                self.E = uflat[:, 5 * NR:5 * NR + 896]
                self.ED = uflat[:, 5 * NR + 896:5 * NR + 1024]
                self.Em = uflat[0:NM, 6 * NR + 512:7 * NR + 512]
                self.mmE = sm(280, NH * 2 * NM, h=NH, d=2)[0:NM]
                self.mm = sm(420, NH * NM, h=NH)[0:NM]
                c = EV["v1"]
                self.DF, self.DB = ar(c, NR), ar(c + NR, NR)
                self.MF, self.MB = ar(c + 2 * NR, 128), ar(c + 2 * NR + 128, 128)
                self.dm = ar(c + 2 * NR + 256, 2 * NR, d=2)[0:NM]
                self.Em2 = ar(EV["rows"] + 768, NR)[0:NM]
                self.norm = HeadNorm(1, EVT["sgr"])

            def consts(self, act):
                for dst, n in ((self.DF, "c_df"), (self.DB, "c_db"), (self.MF, "c_mf"), (self.MB, "c_mb")):
                    act.dma_start(dst, a[n][:, :]).then_inc(self.consts_in, 16)
                act.dma_start(self.dm, a["c_dm"][:, :, :]).then_inc(self.consts_in, 16)

            def q(self, h):
                return EVT["rqk"][:, h]

            def k(self, h):
                return EVT["rqk"][:, NH + h]

            def lg(self, d, h, n=128):
                return lgam[0:n, NH * d + h:NH * d + h + 1]

            def pe(self, pe):
                for h in range(NH):
                    ins = pe.matmul(bank[7][0:NM, NM * h:NM * h + NM], self.k(h)[:, 0:NM], self.q(h)[:, 0:NM],
                                    start=True, stop=True)
                ins.then_inc(self.pre, 1)

                def scores(h):
                    if h:
                        pe.wait_ge(self.sd, h)
                    for kt in range(4):
                        pe.matmul(bank[kt][:, :], self.k(h)[:, NM + 128 * kt:NM + 128 * kt + 128], self.q(h)[:, NM:T],
                                  start=True, stop=True)
                    pe.matmul(bank[4][0:NM, :], self.k(h)[:, 0:NM], self.q(h)[:, NM:T], start=True,
                              stop=True).then_inc(self.sprod, 1)

                scores(0)
                pe.wait_ge(self.msd, 1)
                for h in range(NH):
                    pe.wait_ge(self.sd, h + 1)
                    if h < NH - 1:
                        scores(h + 1)
                    if h:
                        pe.wait_ge(self.comb, h)
                    v = lambda t, n: EVT["rv"][0:n, t, HD * h:HD * h + HD]
                    for t in range(1, NT):
                        qt = t - 1
                        bk, o = OUT_AT[t]
                        ps = bank[bk][:, o:o + HD]
                        pe.matmul(ps, self.SDm[:, 128 * qt:128 * qt + 128], v(0, NM), start=True, stop=False)
                        for kt in range(4):
                            pe.matmul(ps, self.SD[:, kt, 128 * qt:128 * qt + 128], v(kt + 1, 128), start=False, stop=(kt == 3))
                    bk, o = OUT_AT[0]
                    pe.matmul(bank[bk][0:NM, o:o + HD], self.mm[:, h], v(0, NM), start=True, stop=True).then_inc(self.oprod, 1)

            def act(self, act, step):
                act.wait_ge(self.consts_in, 80)
                for h in range(NH):
                    for d in range(2):
                        ins = act.activation(self.mmE[:, h, d], self.DF[0:NM, 0:NM], ACT.Exp, scale=self.lg(d, h, NM))
                ins.then_inc(self.mexp, 1)
                for h in range(NH):
                    if h:
                        act.wait_ge(self.sd, h)
                    act.activation(self.E[:, 384:896], self.DF, ACT.Exp, scale=self.lg(0, h))
                    act.activation(self.E[:, 0:384], self.DB[:, 0:384], ACT.Exp, scale=self.lg(1, h))
                    act.activation(self.ED, self.DB[:, 384:512], ACT.Exp, scale=self.lg(1, h))
                    act.activation(self.Em, self.dm[:, 0], ACT.Exp, scale=self.lg(0, h, NM))
                    act.activation(self.Em2, self.dm[:, 1], ACT.Exp, scale=self.lg(1, h, NM)).then_inc(self.table, 1)
                    if h:
                        act.wait_ge(self.comb, h)
                        self.norm.act(act, h - 1)
                act.wait_ge(self.comb, NH)
                self.norm.act(act, NH - 1)

            def dve(self, dve, step):
                dve.wait_ge(self.consts_in, 80)
                dve.wait_ge(self.mexp, 1)
                dve.wait_ge(self.pre, 1)
                for h in range(NH):
                    step(dve.tensor_tensor(self.mm[:, h], self.mmE[:, h, 0], self.mmE[:, h, 1], ALU.add))
                    step(dve.tensor_tensor(self.mm[:, h], self.mm[:, h], self.MF[0:NM, 0:NM], ALU.mult))
                dve.scalar_tensor_tensor(self.mm, bank[7][0:NM, 0:NH * NM].rearrange("p (h q) -> p h q", h=NH),
                                         HEAD_SCALE, self.mm, ALU.mult, ALU.mult).then_inc(self.msd, 1)
                for h in range(NH):
                    dve.wait_ge(self.table, h + 1)
                    diag = self.E[:, 384:512]
                    step(dve.tensor_tensor(diag, diag, self.MF, ALU.mult))
                    step(dve.tensor_tensor(self.ED, self.ED, self.MB, ALU.mult))
                    step(dve.tensor_tensor(diag, diag, self.ED, ALU.add))
                    step(dve.tensor_tensor(self.Em, self.Em, self.Em2, ALU.add))
                    dve.wait_ge(self.sprod, h + 1)
                    if h:
                        dve.wait_ge(self.oprod, h)
                    for kt in range(4):
                        dve.scalar_tensor_tensor(self.SD[:, kt], bank[kt][:, :], HEAD_SCALE,
                                                 self.E[:, 384 - 128 * kt:896 - 128 * kt], ALU.mult, ALU.mult)
                    dve.scalar_tensor_tensor(self.SDm, bank[4][0:NM, :], HEAD_SCALE, self.Em, ALU.mult,
                                             ALU.mult).then_inc(self.sd, 1)
                    if h:
                        self.norm.dve_mean(dve, h - 1)
                        self.norm.dve_apply(dve, h - 1)
                    dve.wait_ge(self.oprod, h + 1)
                    hm = self.norm.buf[h % 2]
                    for t in range(NT):
                        n = rows_of(t)
                        bk, o = OUT_AT[t]
                        ins = dve.tensor_copy(hm[0:n, t], bank[bk][0:n, o:o + HD])
                    ins.then_inc(self.comb, 1)
                self.norm.dve_mean(dve, NH - 1)
                self.norm.dve_apply(dve, NH - 1)

            def pool(self, pool):
                for h in range(NH):
                    self.norm.pool(pool, h)

        class Project:

            turned, copied, h_in, product, added = (sem("pr_" + x) for x in ("turned", "copied", "h_in", "product", "added"))

            def __init__(self, layer, mix, mixT, gain, base):
                self.mix, self.mixT, self.gain, self.base = mix, mixT, gain, base
                self.c = 2 * NT * layer
                self.h_count = 16 * NT * (layer + 1)

            def turn_pe(self, pe):
                for t in range(NT):
                    n = rows_of(t)
                    for g in range(2):
                        i = 2 * t + g
                        if i >= 4:
                            pe.wait_ge(self.copied, self.c + i - 3)
                        for k in range(4):
                            ins = pe.transpose(bank[i % 4][:, k * n:(k + 1) * n], self.mix(t, 4 * g + k), ident[0:n, 0:n])
                        ins.then_inc(self.turned, 1)

            def turn_dve(self, dve, step):
                for t in range(NT):
                    n = rows_of(t)
                    c0, c1 = cols_of(t)
                    for g in range(2):
                        i = 2 * t + g
                        dve.wait_ge(self.turned, self.c + i + 1)
                        ps = bank[i % 4][:, 0:4 * n].rearrange("p (k c) -> p k c", k=4)
                        dst = self.mixT[:, 4 * g:4 * g + 4, c0:c1]
                        if self.gain is None:
                            ins = dve.tensor_copy(dst, ps)
                        else:
                            ins = dve.tensor_tensor(dst, ps, gcol[:, self.gain, 4 * g:4 * g + 4].unsqueeze(2)
                                                    .broadcast_to([128, 4, n]), ALU.mult)
                        ins.then_inc(self.copied, 1)

            def pe(self, pe, norm):
                for half in range(2):
                    u = self.base + half
                    ring_wait(pe, u)
                    for t in range(NT):
                        g = NT * half + t
                        c0, c1 = cols_of(t)
                        if g >= 4:
                            pe.wait_ge(self.added, self.c + g - 3)
                        for k in range(KB):
                            ins = pe.matmul(bank[g % 4][0:rows_of(t), :], self.mixT[:, k, c0:c1], ring[:, u % SLOTS, k],
                                            start=(k == 0), stop=(k == KB - 1))
                        ins.then_inc(self.product, 1)
                        if half and t:
                            norm.pe_tile(pe, t - 1)
                    pe.wait_ge(self.product, self.c + NT * half + NT)
                    pe.sem_inc(ring_used[u % SLOTS], 1)
                norm.pe_tile(pe, NT - 1)

            def act(self, act, norm):
                for t in range(NT):
                    act.wait_ge(self.added, self.c + NT + t + 1)
                    norm.act_tile(act, t)

            def dve(self, dve, norm):
                dve.wait_ge(self.h_in, self.h_count)
                for half in range(2):
                    for t in range(NT):
                        g = NT * half + t
                        n = rows_of(t)
                        x = H[0:n, t, BLK * half:BLK * half + BLK]
                        dve.wait_ge(self.product, self.c + g + 1)
                        dve.tensor_tensor(x, bank[g % 4][0:n, :], x, ALU.add).then_inc(self.added, 1)
                        if half:
                            norm.dve_mean(dve, t)
                            if t == NT - 1:
                                norm.dve_uT(dve, t - 1)
                            dve.wait_ge(self.added, self.c + g + 1)
                            norm.dve_scale(dve, t)
                            if 0 < t < NT - 1:
                                norm.dve_uT(dve, t - 1)
                norm.dve_uT(dve, NT - 1)
        OD_Q, OD_K, OD_V, OD_VS, OD_ATT = 0, 4224, 8448, 13568, 16640
        qT, kT = ar(OD_Q, 8 * T, k=8), ar(OD_K, 8 * T, k=8)
        vtok = ar(OD_V, NT * D, t=NT)
        vmid = ar(OD_VS, 3 * D, t=3)
        att = ar(OD_ATT, NT * D, t=NT)

        class OddIn:

            def __init__(self):
                (self.product, self.taken, self.sq, self.ms, self.rs, self.qn, self.turned,
                 self.copied, self.vmid) = (
                    sem("oi_" + x) for x in ("product", "taken", "sq", "ms", "rs", "qn", "turned", "copied", "vmid"))
                self.junk = ar(OD_ATT, BLK)
                self.qn_sb = [ar(OD_ATT + BLK * (i + 1), BLK) for i in range(2)]
                self.ss, self.mean, self.rstd = (sm(20 + 8 * i, 8) for i in range(3))
                self.groups = [(u, t) for u in range(6) for t in range(NT)]

            def pe(self, pe):
                def turn(g):
                    n = rows_of(self.groups[g][1])
                    pe.wait_ge(self.qn, g + 1)
                    if g >= 2:
                        pe.wait_ge(self.copied, g - 1)
                    for k in range(4):
                        ins = pe.transpose(bank[4 + g % 2][:, k * n:(k + 1) * n],
                                           self.qn_sb[g % 2][0:n, 128 * k:128 * k + 128], ident[0:n, 0:n])
                    ins.then_inc(self.turned, 1)

                for g, (j, t) in enumerate(self.groups):
                    u = ODD + j
                    if t == 0:
                        ring_wait(pe, u)
                    if g >= 4:
                        pe.wait_ge(self.taken, g - 3)
                    c0, c1 = cols_of(t)
                    for k in range(KB):
                        ins = pe.matmul(bank[g % 4][0:rows_of(t), :], uT[:, k, c0:c1], ring[:, u % SLOTS, k],
                                        start=(k == 0), stop=(k == KB - 1))
                    ins.then_inc(self.product, 1)
                    if 1 <= g <= 4 * NT:
                        turn(g - 1)
                    if t == NT - 1:
                        pe.wait_ge(self.product, g + 1)
                        pe.sem_inc(ring_used[u % SLOTS], 1)

            def act(self, act, step):
                for g, (j, t) in enumerate(self.groups):
                    n = rows_of(t)
                    act.wait_ge(self.product, g + 1)
                    if j < 4:
                        if g:
                            act.wait_ge(self.ms, g)
                        act.activation(self.junk[0:n], bank[g % 4][0:n, :], ACT.Square).then_inc(self.sq, 1)
                    else:
                        act.wait_ge(self.taken, g)
                        act.activation(vtok[0:n, t, BLK * (j - 4):BLK * (j - 3)], bank[g % 4][0:n, :],
                                       ACT.Copy).then_inc(self.taken, 1)
                act.wait_ge(self.taken, 6 * NT)
                for i in range(3):
                    act.dma_start(vmid[0:64, i], vtok[64:128, i + 1]).then_inc(self.vmid, 16)
                    act.dma_start(vmid[64:128, i], vtok[0:64, i + 2]).then_inc(self.vmid, 16)
                act.wait_ge(self.vmid, 96)

            def dve(self, dve, step):
                step(dve.tensor_scalar(gcol[:, 5, 0:1], gcol[:, 5, 0:1], float(AD) ** -0.5, None, ALU.mult))
                for g, (j, t) in enumerate(self.groups[:4 * NT]):
                    n = rows_of(t)
                    dve.wait_ge(self.sq, g + 1)
                    step(dve.tensor_reduce(self.ss[0:n], self.junk[0:n].rearrange("p (h e) -> p h e", e=AD), AX.X, ALU.add))
                    dve.tensor_scalar(self.mean[0:n], self.ss[0:n], 1.0 / AD, EPS, ALU.mult, ALU.add).then_inc(self.ms, 1)
                    if g:
                        self.copy(dve, g - 1)
                    dve.wait_ge(self.rs, g + 1)
                    dve.tensor_tensor(self.qn_sb[g % 2][0:n].rearrange("p (h e) -> p h e", e=AD),
                                      bank[g % 4][0:n, :].rearrange("p (h e) -> p h e", e=AD),
                                      self.rstd[0:n].unsqueeze(2).broadcast_to([n, 8, AD]), ALU.mult).then_inc(self.taken, 1)
                    dve.wait_ge(self.taken, g + 1)
                    dve.sem_inc(self.qn, 1)
                self.copy(dve, 4 * NT - 1)

            def copy(self, dve, g):
                j, t = self.groups[g]
                c0, c1 = cols_of(t)
                dst = (qT if j < 2 else kT)[:, 4 * (j % 2):4 * (j % 2) + 4, c0:c1]
                dve.wait_ge(self.turned, g + 1)
                dve.tensor_scalar(dst, bank[4 + g % 2][:, 0:4 * (c1 - c0)].rearrange("p (k c) -> p k c", k=4),
                                  gcol[:, 5, j // 2:j // 2 + 1], None, ALU.mult).then_inc(self.copied, 1)

            def pool(self, pool):
                for g, (j, t) in enumerate(self.groups[:4 * NT]):
                    n = rows_of(t)
                    pool.wait_ge(self.ms, g + 1)
                    if g:
                        pool.wait_ge(self.taken, g)
                    pool.tensor_tensor(self.rstd[0:n], self.mean[0:n], minus_half[0:n, 0:1].broadcast_to([n, 8]),
                                       ALU.pow).then_inc(self.rs, 1)

        class Attention:
            KEY0 = [0, 64, 192, 256]
            TABLE = [0, 1, 1, 2]
            W = NM + 256

            def __init__(self):
                (self.product, self.neg, self.exp, self.turned, self.copied, self.pv, self.comb,
                 self.m_s, self.m_sub, self.m_exp, self.m_p, self.m_t, self.m_pt, self.m_o,
                 self.m_done) = (
                    sem("at_" + x) for x in ("product", "neg", "exp", "turned", "copied", "pv", "comb", "m_s", "m_sub", "m_exp", "m_p",
                    "m_t", "m_pt", "m_o", "m_done"))
                self.bias = [uflat[:, 816 * i:816 * i + 816] for i in range(2)]
                self.bias_in = [sem(f"at_bias_in{i}") for i in range(2)]
                o = 1632
                self.P = [uflat[:, o + self.W * i:o + self.W * (i + 1)] for i in range(2)]
                o += 2 * self.W
                self.PT = [uflat[:, o + 384 * i:o + 384 * i + 256] for i in range(2)]
                self.PTm = [uflat[0:NM, o + 384 * i + 256:o + 384 * i + 384] for i in range(2)]
                self.mn = sm(20, 2)
                self.sum = sm(24, 8, b=2)
                self.rinv = sm(32, 4)
                self.mp = sm(40, AH * NM, h=AH)[0:NM]
                self.mpT = sm(300, AH * NM, h=AH)[0:NM]
                self.ms_ = sm(560, 3 * AH, x=3)[0:NM]

            def slot(self, h):
                return h // 2 + 8 * (h % 2)

            def values(self, b):
                t = lambda i: vtok[:, i + 1]
                return [(t(0), t(1)), (vmid[:, 0], vmid[:, 1]), (vmid[:, 1], vmid[:, 2]), (t(2), t(3))][b]

            def load_bias(self, act, h):
                act.dma_start(self.bias[h % 2], a["rpb_tiles"][h]).then_inc(self.bias_in[h % 2], 16)

            def act(self, act, step):
                self.load_bias(act, 0)
                self.load_bias(act, 1)
                act.wait_ge(self.m_sub, 2)
                act.activation(self.mp, self.mp, ACT.Exp).then_inc(self.m_exp, 1)
                for s in range(4 * AH):
                    h, b = s // 4, s % 4
                    act.wait_ge(self.neg, s + 1)
                    if b == 0 and h >= 2:
                        act.wait_ge(self.comb, h - 1)
                    act.activation(self.P[s % 2], self.P[s % 2], ACT.Exp, bias=self.mn[:, s % 2:s % 2 + 1], scale=-1.0,
                                   accum_out=self.sum[:, h % 2, b:b + 1]).then_inc(self.exp, 1)
                    if b == 3 and h + 2 < AH:
                        self.load_bias(act, h + 2)

            def dve(self, dve, step):
                dve.wait_ge(self.m_s, 1)
                bc = lambda x: x.unsqueeze(2).broadcast_to([NM, x.shape[1], NM])
                for i in range(2):
                    ps = bank[4 * i][0:NM, 0:8 * NM].rearrange("p (h k) -> p h k", h=8)
                    mx = self.ms_[:, 0, 8 * i:8 * i + 8]
                    step(dve.tensor_reduce(mx, ps, AX.X, ALU.max))
                    dve.tensor_tensor(self.mp[:, 8 * i:8 * i + 8], ps, bc(mx), ALU.subtract).then_inc(self.m_sub, 1)
                dve.wait_ge(self.m_exp, 1)
                step(dve.tensor_reduce(self.ms_[:, 1], self.mp, AX.X, ALU.add))
                step(dve.reciprocal(self.ms_[:, 2], self.ms_[:, 1]))
                dve.tensor_tensor(self.mp, self.mp, bc(self.ms_[:, 2]), ALU.mult).then_inc(self.m_p, 1)
                dve.wait_ge(self.m_t, 1)
                dve.tensor_copy(self.mpT, bank[1][0:NM, 0:AH * NM].rearrange("p (h k) -> p h k", h=AH)).then_inc(self.m_pt, 1)
                dve.wait_ge(self.m_o, 1)
                for i in range(2):
                    dve.tensor_copy(att[0:NM, 0, BLK * i:BLK * i + BLK], bank[2 + i][0:NM, :]).then_inc(self.m_done, 1)

                def scores(s):
                    h, b = s // 4, s % 4
                    dve.wait_ge(self.bias_in[h % 2], 16 * (h // 2 + 1))
                    dve.wait_ge(self.product, s + 1)
                    if s >= 2:
                        dve.wait_ge(self.turned, s - 1)
                    t = self.TABLE[b]
                    dve.tensor_tensor_reduce(self.P[s % 2], bank[s % 2][:, 0:self.W], self.bias[h % 2][:, self.W * t:self.W * (t + 1)],
                                             -1.0, 3e38, ALU.add, ALU.min, self.mn[:, s % 2:s % 2 + 1]).then_inc(self.neg, 1)

                def combine(h):
                    dve.wait_ge(self.exp, 4 * h + 4)
                    step(dve.reciprocal(self.rinv, self.sum[:, h % 2]))
                    dve.wait_ge(self.pv, 4 * h + 4)
                    dve.tensor_tensor(att[:, 1:NT, AD * h:AD * h + AD],
                                      bank[4 + h % 2][:, 0:4 * AD].rearrange("p (b e) -> p b e", b=4),
                                      self.rinv.unsqueeze(2).broadcast_to([128, 4, AD]), ALU.mult).then_inc(self.comb, 1)

                scores(0)
                for s in range(4 * AH):
                    if s + 1 < 4 * AH:
                        scores(s + 1)
                    dve.wait_ge(self.turned, s + 1)
                    if s >= 2:
                        dve.wait_ge(self.pv, s - 1)
                    dve.tensor_copy(self.PT[s % 2], bank[2 + s % 2][:, 0:256])
                    dve.tensor_copy(self.PTm[s % 2], bank[2 + s % 2][0:NM, 256:384]).then_inc(self.copied, 1)
                    if s % 4 == 1 and s > 4:
                        combine(s // 4 - 1)
                combine(AH - 1)

            def pe(self, pe):
                def head(x, h, c0, c1):
                    return x[AD * (h % 2):AD * (h % 2) + AD, h // 2, c0:c1]

                for h in range(AH):
                    ins = pe.matmul(bank[4 * (h % 2)][0:NM, NM * (h // 2):NM * (h // 2) + NM], head(qT, h, 0, NM),
                                    head(kT, h, 0, NM), start=True, stop=True)
                ins.then_inc(self.m_s, 1)
                pe.wait_ge(self.m_p, 1)
                for h in range(AH):
                    ins = pe.transpose(bank[1][0:NM, NM * h:NM * h + NM], self.mp[:, self.slot(h)], ident[0:NM, 0:NM])
                ins.then_inc(self.m_t, 1)
                pe.wait_ge(self.m_pt, 1)
                for h in range(AH):
                    ins = pe.matmul(bank[2 + h // 8][0:NM, AD * (h % 8):AD * (h % 8) + AD], self.mpT[:, h],
                                    vtok[0:NM, 0, AD * h:AD * h + AD], start=True, stop=True)
                ins.then_inc(self.m_o, 1)
                pe.wait_ge(self.m_done, 2)

                def scores(s):
                    h, b = s // 4, s % 4
                    q = head(qT, h, NM + 128 * b, NM + 128 * b + 128)
                    k0 = NM + self.KEY0[b]
                    pe.matmul(bank[s % 2][:, 0:NM], q, head(kT, h, 0, NM), start=True, stop=True)
                    pe.matmul(bank[s % 2][:, NM:self.W], q, head(kT, h, k0, k0 + 256), start=True, stop=True).then_inc(self.product, 1)

                def values(s):
                    h, b = s // 4, s % 4
                    pe.wait_ge(self.copied, s + 1)
                    if b == 0 and h >= 2:
                        pe.wait_ge(self.comb, h - 1)
                    o = bank[4 + h % 2][:, AD * b:AD * b + AD]
                    v0, v1 = self.values(b)
                    hs = slice(AD * h, AD * h + AD)
                    pe.matmul(o, self.PT[s % 2][:, 0:128], v0[:, hs], start=True, stop=False)
                    pe.matmul(o, self.PT[s % 2][:, 128:256], v1[:, hs], start=False, stop=False)
                    pe.matmul(o, self.PTm[s % 2], vtok[0:NM, 0, hs], start=False, stop=True).then_inc(self.pv, 1)

                scores(0)
                scores(1)
                for s in range(4 * AH):
                    pe.wait_ge(self.exp, s + 1)
                    if s >= 2:
                        pe.wait_ge(self.copied, s - 1)
                    P, ps = self.P[s % 2], bank[2 + s % 2]
                    pe.transpose(ps[:, 0:128], P[:, NM:NM + 128], ident[:, :])
                    pe.transpose(ps[:, 128:256], P[:, NM + 128:self.W], ident[:, :])
                    pe.transpose(ps[0:NM, 256:384], P[:, 0:NM], ident[:, :]).then_inc(self.turned, 1)
                    if s + 2 < 4 * AH:
                        scores(s + 2)
                    if s:
                        values(s - 1)
                values(4 * AH - 1)

        def store_tile(eng, x, dram, layer, t, s):
            if t == 0:
                eng.dma_start(dram[0:NM, :], x[0:NM, 0]).then_inc(s, 16)
            elif layer:
                c0, c1 = cols_of(t)
                eng.dma_start(dram[c0:c1, :], x[:, t]).then_inc(s, 16)
            else:
                by_row = dram[NM:T, :].rearrange("(c r) d -> r c d", r=GRID_H)
                for i in range(2):
                    eng.dma_start(by_row[2 * (t - 1) + i], x[GRID_W * i:GRID_W * (i + 1), t]).then_inc(s, 16)

        def store_tiles(eng, norm, h, hn, layer, s):
            for t in range(NT):
                eng.wait_ge(norm.hn, norm.c + t + 1)
                store_tile(eng, H, h, layer, t, s)
                store_tile(eng, norm.hnorm, hn, layer, t, s)

        def load_h(eng, s):
            for t in range(NT):
                c0, c1 = cols_of(t)
                eng.dma_start(H[0:rows_of(t), t], h_dram[c0:c1, :]).then_inc(s, 16)

        def load_x(eng, s):
            for t in range(NT):
                src = a["meta_tokens"] if t == 0 else a["x"][0, 128 * (t - 1):128 * t, :]
                eng.dma_start(H[0:rows_of(t), t], src).then_inc(s, 16)

        norms = [Norm(i, i) for i in range(4)]
        stored = [sem(f"stored{i}") for i in range(2)]
        even_in = EvenIn()
        gates = Gates(even_in.rows)
        mlstm, ret = MLSTM(gates), Retention()

        def even_mix(t, k):
            src = EVT["sgo"] if k < 4 else EVT["sgr"]
            return src[0:rows_of(t), t, 128 * (k % 4):128 * (k % 4) + 128]

        even_out = Project(0, even_mix, EVT["qk"], 4, EVEN + 8)
        odd_in, attn = OddIn(), Attention()
        odd_out = Project(1, lambda t, k: att[0:rows_of(t), t, 128 * k:128 * k + 128], ar(0, 8 * T, k=8), None, ODD + 6)
        outs = [even_out, odd_out]
        block = ctx.enter_context(nc.Block())

        @block.sync
        def _(sp):
            stream_even(sp)
            stream_moe(sp, 0, MOE0)
            stream_odd(sp)
            stream_moe(sp, 1, MOE1)

        @block.scalar
        def _(act):
            step = Chain(act, act_step)
            load_x(act, norms[0].in_)
            act.dma_start(ident[:, :], a["c_ident"][:, :]).then_inc(consts_in, 16)
            act.dma_start(minus_half, a["c_mhalf"][:, :]).then_inc(consts_in, 16)
            for i, (n, l) in enumerate([("attn_norm_g", 0), ("ffn_norm_g", 0), ("attn_norm_g", 1), ("ffn_norm_g", 1)]):
                act.dma_start(gcol[:, i], a[n][l].rearrange("(k p) -> p k", p=128),
                              allow_slow_non_contiguous=True).then_inc(consts_in, 16)
            for i, n in enumerate(("even_m_norm_g", "even_r_norm_g")):
                act.dma_start(gcol[:, 4, 4 * i:4 * i + 4], a[n].rearrange("(k p) -> p k", p=128),
                              allow_slow_non_contiguous=True).then_inc(consts_in, 16)
            for i, n in enumerate(("odd_q_norm_g", "odd_k_norm_g")):
                for j in range(2):
                    act.dma_start(gcol[AD * j:AD * j + AD, 5, i:i + 1], a[n].rearrange("(p o) -> p o", o=1),
                                  allow_slow_non_contiguous=True).then_inc(consts_in, 16)
            even_in.consts(act)
            act.dma_start(gates.logit, a["even_ret_decay_logit"].rearrange("d h -> (d h)").unsqueeze(0)
                          .broadcast_to([128, 8])).then_inc(gates.logit_in, 16)
            ex[0].consts(act)
            ex[1].consts(act)
            act.wait_ge(consts_in, 192)
            for layer in range(2):
                n_in, n_ffn = norms[2 * layer], norms[2 * layer + 1]
                if layer:
                    fenced(act)
                    load_h(act, n_in.in_)
                act.wait_ge(n_in.in_, 16 * NT)
                fenced(act)
                n_in.act(act, step)
                fenced(act)
                if layer == 0:
                    even_in.act(act, step)
                    fenced(act)
                    mlstm.consts(act)
                    gates.act(act, step)
                    fenced(act)
                    mlstm.act(act, step)
                    fenced(act)
                    ret.consts(act)
                    ret.act(act, step)
                    fenced(act)
                    fenced(act)
                    load_x(act, even_out.h_in)
                else:
                    odd_in.act(act, step)
                    fenced(act)
                    attn.act(act, step)
                    fenced(act)
                    fenced(act)
                    load_h(act, odd_out.h_in)
                outs[layer].act(act, n_ffn)
                store_tiles(act, n_ffn, ex[layer].resid, ex[layer].normed, layer, stored[layer])
                ex[layer].select_act(act)
                act.wait_ge(stored[layer], 32 * STORES[layer])
                fenced(act)
                ex[layer].loop(act, ex[layer].act_body)

        @block.vector
        def _(dve):
            step = Chain(dve, dve_step)
            for layer in range(2):
                if layer:
                    fenced(dve)
                fenced(dve)
                norms[2 * layer].dve(dve, step)
                fenced(dve)
                if layer == 0:
                    even_in.dve(dve, step)
                    fenced(dve)
                    gates.dve(dve, step)
                    fenced(dve)
                    mlstm.dve(dve, step)
                    fenced(dve)
                    ret.dve(dve, step)
                else:
                    odd_in.dve(dve, step)
                    fenced(dve)
                    attn.dve(dve, step)
                fenced(dve)
                outs[layer].turn_dve(dve, step)
                fenced(dve)
                outs[layer].dve(dve, norms[2 * layer + 1])
                ex[layer].select_dve(dve, step)
                fenced(dve)
                ex[layer].xT_copy(dve, 0)
                ex[layer].loop(dve, ex[layer].dve_body)

        @block.gpsimd
        def _(pool):
            for layer in range(2):
                if layer:
                    fenced(pool)
                fenced(pool)
                norms[2 * layer].pool(pool)
                fenced(pool)
                if layer == 0:
                    fenced(pool)
                    fenced(pool)
                    mlstm.pool(pool)
                    fenced(pool)
                    ret.pool(pool)
                else:
                    odd_in.pool(pool)
                    fenced(pool)
                fenced(pool)
                fenced(pool)
                norms[2 * layer + 1].pool(pool)
                fenced(pool)
                ex[layer].gather(pool, 0, 1)
                ex[layer].loop(pool, ex[layer].pool_body)
                pool.wait_ge(ex[layer].scattered, 16 * NE)

        @block.tensor
        def _(pe):
            for layer in range(2):
                if layer:
                    fenced(pe)
                fenced(pe)
                norms[2 * layer].pe(pe)
                fenced(pe)
                if layer == 0:
                    even_in.pe(pe)
                    fenced(pe)
                    gates.pe(pe)
                    fenced(pe)
                    mlstm.pe(pe)
                    fenced(pe)
                    ret.pe(pe)
                else:
                    odd_in.pe(pe)
                    fenced(pe)
                    attn.pe(pe)
                fenced(pe)
                outs[layer].turn_pe(pe)
                fenced(pe)
                outs[layer].pe(pe, norms[2 * layer + 1])
                ex[layer].select_pe(pe)
                fenced(pe)
                ex[layer].turn_xs(pe, 0, 0)
                ex[layer].turn_xs(pe, 0, 1)
                ex[layer].loop(pe, ex[layer].pe_body)


def constants():
    f = np.float32
    c = {}
    c["c_ident"] = np.eye(128, dtype=f)
    c["c_mhalf"] = np.full((128, 1), -0.5, f)
    c["c_iota"] = np.broadcast_to(np.arange(1, CAP + 1, dtype=f), (128, CAP)).copy()
    p = np.arange(128)
    tok = np.zeros((2, 128, NT), f)
    tok[:, :, 0] = p
    for b in range(4):
        tok[0, :, b + 1] = NM + (p % GRID_W) * GRID_H + 2 * b + p // GRID_W
        tok[1, :, b + 1] = NM + 128 * b + p
    c["c_token"] = tok
    half = HD // 2
    inv = (f(10000.0) ** (-np.arange(half, dtype=f) / f(half))).astype(f)
    ang = np.arange(T, dtype=f)[:, None] * inv[None, :]
    cs = np.concatenate([np.cos(ang), np.sin(ang)], -1).astype(f)
    rope = np.zeros((128, NT, HD), f)
    rope[:NM, 0] = cs[:NM]
    rope[:, 1:] = cs[NM:].reshape(4, 128, HD).transpose(1, 0, 2)
    c["c_rope"] = rope
    k, q = p[:, None], p[None, :]
    c["c_mf"] = (q >= k).astype(f)
    c["c_mb"] = (q <= k).astype(f)
    c["c_far"] = np.stack([np.where(q >= k, 0, FAR), np.where(q <= k, 0, FAR)], 1).astype(f)
    c["c_sel"] = np.broadcast_to(np.eye(NH, dtype=f)[:, :, None], (NH, NH, 128)).copy()
    j = np.arange(NR)[None, :]
    c["c_df"] = np.maximum(j - k, 0).astype(f)
    c["c_db"] = np.maximum(k - (j - 384), 0).astype(f)
    m = np.arange(NM)[:, None]
    c["c_dm"] = np.stack([NM + j - m, T - 1 - j - m], 1).astype(f)
    return c


def bias_tiles(rpb):
    p = np.arange(128)
    c, r = p[:, None] // GRID_H, p[:, None] % GRID_H
    kk = np.arange(256)[None, :]
    parts = []
    for q0, k0 in ((0, 0), (16, 8), (48, 32)):
        qc, kc, kr = q0 + c, k0 + kk // GRID_H, kk % GRID_H
        start = np.clip(qc - 8, 0, GRID_W - 16)
        seen = (kc >= start) & (kc < start + 16)
        t = rpb[:, kr - r + 7, np.clip(kc - qc, -15, 15) + 15]
        t[:, ~seen] = -FAR
        parts += [np.zeros((AH, 128, NM), np.float32), t]
    return np.concatenate(parts, -1)


INPUTS = ["x", "meta_tokens", "attn_norm_g", "ffn_norm_g", "even_w_in", "even_conv_w", "even_gate_b",
          "even_m_norm_g", "even_ret_decay_logit", "even_r_norm_g", "even_w_out", "odd_w_in", "odd_q_norm_g",
          "odd_k_norm_g", "odd_w_out", "router_w", "expert_w_gate", "expert_w_up", "expert_w_down"]


def kernel(**inputs):
    from concourse import bacc
    from concourse.bass_utils import run_bass_kernel_spmd

    arrays = {n: np.ascontiguousarray(inputs[n]) for n in INPUTS}
    for n in ("even_w_in", "even_conv_w", "even_gate_b", "even_m_norm_g", "even_ret_decay_logit", "even_r_norm_g",
              "even_w_out", "odd_w_in", "odd_q_norm_g", "odd_k_norm_g", "odd_w_out"):
        arrays[n] = arrays[n][0]
    arrays["even_conv_w"] = np.ascontiguousarray(arrays["even_conv_w"].reshape(CONV, 2 * NH, 128).transpose(2, 1, 0))
    arrays["rpb_tiles"] = bias_tiles(np.asarray(inputs["odd_rpb"])[0])
    arrays |= constants()
    nc = bacc.Bacc("TRN2", target_bir_lowering=False, num_devices=1)
    a = {n: nc.dram_tensor(f"in_{n}", v.shape, mybir.dt.from_np(v.dtype), kind="ExternalInput").ap()
         for n, v in arrays.items()}
    out = nc.dram_tensor("out_h", (T, D), F32, kind="ExternalOutput").ap()
    trunk(nc, a, out)
    r = run_bass_kernel_spmd(nc, [{f"in_{n}": v for n, v in arrays.items()}], core_ids=[0])
    return r.results[0]["out_h"][NM:].reshape(GRID_W, GRID_H, D).transpose(1, 0, 2).reshape(1, NR, D)
```

```python
from contextlib import ExitStack

import numpy as np

import concourse.bass as bass
from concourse import mybir

ALU = mybir.AluOpType
ACT = mybir.ActivationFunctionType
AX = mybir.AxisListType
F32 = mybir.dt.float32
F32R = mybir.dt.float32r
U32 = mybir.dt.uint32

D = 1024
KB = D // 128
NM = 16
NR = 512
T = NM + NR
NT = 5
GRID_W, GRID_H = 64, 8
EPS = 1e-6
BLK = 512
SLOTS = 6
HD = 128
NH = 4
CONV = 5
AH, AD = 16, 64
NE = 16
CAP = 2 * T // NE
FAR = 1e30
HEAD_SCALE = float(HD) ** -0.5
BAND = [(0, 192), (64, 256), (192, 256), (320, 192)]
BIAS_AT = [0, 208, 208, 480]
BIAS_N = 688
ARENA = 22600
PADS = 6


def rows_of(t):
    return NM if t == 0 else 128


def cols_of(t):
    return (0, NM) if t == 0 else (NM + 128 * (t - 1), NM + 128 * t)


def trunk(nc, a, out, upto=99, dbg=None):
    ctx = ExitStack()
    with ctx:
        def sb(name, shape, dt=F32):
            return ctx.enter_context(nc.sbuf_tensor(name, shape, dt))

        def sem(name):
            return ctx.enter_context(nc.semaphore(name))

        h_dram = nc.dram_tensor("h_mid", [T, D], F32, kind="Internal").ap()
        hn_dram = [nc.dram_tensor(f"h_normed{i}", [T, D], F32, kind="Internal").ap() for i in range(2)]

        SPACES = [("ring", [128, SLOTS, KB, BLK]),
                  ("small", [128, 1600]),
                  ("uT", [128, KB, T]),
                  ("arena", [128, ARENA])]
        with ExitStack() as first:
            ring_rounded = [first.enter_context(nc.sbuf_tensor(f"ring{i}_r", [128, KB, BLK], F32R)) for i in range(SLOTS)]
            rounded = {n: first.enter_context(nc.sbuf_tensor(n + "_r", shape, F32R)) for n, shape in SPACES[1:]}
        ring, small, uT, arena = (sb(n, shape) for n, shape in SPACES)
        ident = sb("ident", [128, 128])
        gcol = sb("gcol", [128, 6, KB])
        bank = [ctx.enter_context(nc.psum_tensor(f"bank{i}", [128, 512], F32)) for i in range(8)]

        minus_half = small[:, 1599:1600]
        H = arena[:, ARENA - NT * D:ARENA].rearrange("p (t d) -> p t d", t=NT)

        def ar(off, n, **kw):
            assert off + n <= ARENA, (off, n)
            v = arena[:, off:off + n]
            if kw:
                names = " ".join(kw)
                v = v.rearrange(f"p ({names} z) -> p {names} z", **kw)
            return v

        def sm(off, n, **kw):
            v = small[:, off:off + n]
            if kw:
                names = " ".join(kw)
                v = v.rearrange(f"p ({names} z) -> p {names} z", **kw)
            return v

        ring_in = [sem(f"ring_in{i}") for i in range(SLOTS)]
        ring_used = [sem(f"ring_used{i}") for i in range(SLOTS)]
        fence = sem("fence")
        consts_in = sem("consts_in")
        dve_step = sem("dve_step")
        act_step = sem("act_step")
        pool_step = sem("pool_step")

        class Chain:

            def __init__(self, eng, s):
                self.eng, self.s, self.n = eng, s, 0

            def __call__(self, ins):
                self.n += 1
                ins.then_inc(self.s, 1)
                self.eng.wait_ge(self.s, self.n)

        fences = {}

        def fenced(eng):
            fences[eng] = fences.get(eng, 0) + 1
            eng.drain().then_inc(fence, 1)
            eng.wait_ge(fence, 4 * fences[eng])

        def high(x):
            if x.tensor.name != "ring":
                return bass.AP(rounded[x.tensor.name], x.offset, x.ap)
            slot, offset = divmod(x.offset, KB * BLK)
            return bass.AP(ring_rounded[slot], offset, [(KB * BLK, 128)] + list(x.ap[1:]))

        def part(x):
            return high(x).bitcast(F32)

        def product3(pe, ps, still, moving, ks, start, stop, order=((0, 0), (0, 1), (1, 0)), before_last=None):
            for i, (a_, b_) in enumerate(order):
                if i == 2 and before_last:
                    before_last()
                for k in ks:
                    first, last = i == 0 and k == ks[0], i == 2 and k == ks[-1]
                    ins = pe.matmul(ps, high(still[a_](k)), high(moving[b_](k)), start=start and first, stop=stop and last)
            return ins

        EVEN_UNITS, ODD_UNITS = 10, 8
        mixer_slots = [[m % 3 for m in range(EVEN_UNITS)], [(1, 2, 0)[m % 3] for m in range(ODD_UNITS)]]
        HIGH_SLOTS, TOKEN_SLOT = (3, 4), 5
        moe_slots = [[1, 5, 2, 0, 3, 4], [0, 5, 1, 2, 3, 4]]
        seen_in, seen_used = [0] * SLOTS, [0] * SLOTS
        mixer_units, moe_base = [], []
        for layer in range(2):
            units = []
            for m, s in enumerate(mixer_slots[layer]):
                units.append((s, seen_in[s], seen_used[s], HIGH_SLOTS[m % 2], seen_used[HIGH_SLOTS[m % 2]]))
                seen_in[s] += 1
                seen_used[s] += 1
                seen_used[HIGH_SLOTS[m % 2]] += 1
            mixer_units.append(units)
            seen_used[TOKEN_SLOT] += 1
            moe_base.append((list(seen_in), list(seen_used)))
            seen_in = [n + NE for n in seen_in]
            seen_used = [n + NE for n in seen_used]
        MOE_UNITS = 6
        even_cols = [0, 512, 1024, 1536, 2064, 2576, 3088, 3600]

        def block_of(w, c):
            return w[:, c:c + BLK].rearrange("(k p) c -> p k c", p=128)

        def stream_mixer(sp, layer, sources, tokens):
            for m, src in enumerate(sources):
                s, _, used, _, _ = mixer_units[layer][m]
                if used:
                    sp.wait_ge(ring_used[s], used)
                if m == layer:
                    sp.wait_ge(tokens, 16 * NT)
                sp.dma_start(ring[:, s], src).then_inc(ring_in[s], 16)

        def stream_moe(sp, layer):
            names = ["expert_w_gate", "expert_w_up", "expert_w_gate", "expert_w_up", "expert_w_down", "expert_w_down"]
            half = [0, 0, 1, 1, 0, 1]
            with sp.Fori(0, NE) as e:
                for j in range(MOE_UNITS):
                    s = moe_slots[layer][j]
                    w = a[names[j]][layer].rearrange("e (k p) c -> e p k c", p=128)
                    sp.wait_ge(ring_used[s], e + moe_base[layer][1][s])
                    sp.dma_start(ring[:, s], w[bass.ds(e, 1), :, :, BLK * half[j]:BLK * (half[j] + 1)]
                                 .rearrange("e p k c -> p (e k) c")).then_inc(ring_in[s], 16)

        token_meta = sm(920, KB * NM, k=KB)

        class TokenHigh:

            def cols(self, c0, c1):
                return token_meta[:, :, c0:c1] if c0 < NM else ring[:, TOKEN_SLOT, :, c0 - NM:c1 - NM]

        uH = TokenHigh()

        class Halves:
            hi, lo = sem("block_high"), sem("block_low")

            def __init__(self, layer):
                self.l, self.before = layer, EVEN_UNITS * layer

            def act(self, act, m):
                s, fills, _, h, used = mixer_units[self.l][m]
                act.wait_ge(ring_in[s], 16 * (fills + 1))
                if used:
                    act.wait_ge(ring_used[h], used)
                act.activation(high(ring[:, h]), ring[:, s], ACT.Copy).then_inc(self.hi, 1)

            def dve(self, dve, m):
                s, _, _, h, _ = mixer_units[self.l][m]
                dve.wait_ge(self.hi, self.before + m + 1)
                dve.tensor_tensor(high(ring[:, s]), ring[:, s], part(ring[:, h]), ALU.subtract).then_inc(self.lo, 1)

            def ready(self, pe, m):
                pe.wait_ge(self.lo, self.before + m + 1)

            def weights(self, m, c0=0, c1=BLK):
                s, _, _, h, _ = mixer_units[self.l][m]
                return (lambda k: ring[:, h, k, c0:c1]), (lambda k: ring[:, s, k, c0:c1])

            def used(self, pe, m):
                s, _, _, h, _ = mixer_units[self.l][m]
                pe.sem_inc(ring_used[s], 1)
                pe.sem_inc(ring_used[h], 1)

        def tokens(c0, c1):
            return (lambda k: uH.cols(c0, c1)[:, k]), (lambda k: uT[:, k, c0:c1])

        halves = [Halves(i) for i in range(2)]

        STORES = [1 + 2 * (NT - 1), NT]

        class Norm:
            sq, ms, rs, hn, tr, ev, hi = (sem("n_" + x) for x in ("squares", "mean", "rstd", "normed", "turned", "uT", "uT_high"))

            def __init__(self, k, gain, dram=None, real_rows=None, meta_rows=None):
                self.c, self.gain, self.dram = NT * k, gain, dram
                self.in_ = sem(f"n{k}_h_in")
                self.ss = small[:, 0:5]
                self.mean = small[:, 5:10]
                self.rstd = small[:, 10:15]
                self.hnorm = ar(8916, NT * D, t=NT)
                self.junk = ar(8916 + NT * D, D)

            def act_tile(self, act, t):
                n = rows_of(t)
                if t:
                    act.wait_ge(self.sq, self.c + t)
                act.activation(self.junk[0:n], H[0:n, t], ACT.Square,
                               accum_out=self.ss[0:n, t:t + 1]).then_inc(self.sq, 1)

            def dve_mean(self, dve, t):
                n = rows_of(t)
                dve.wait_ge(self.sq, self.c + t + 1)
                dve.tensor_scalar(self.mean[0:n, t:t + 1], self.ss[0:n, t:t + 1], 1.0 / D, EPS,
                                  ALU.mult, ALU.add).then_inc(self.ms, 1)

            def dve_scale(self, dve, t):
                n = rows_of(t)
                dve.wait_ge(self.rs, self.c + t + 1)
                dve.tensor_scalar(self.hnorm[0:n, t], H[0:n, t], self.rstd[0:n, t:t + 1], None,
                                  ALU.mult).then_inc(self.hn, 1)

            def dve_uT(self, dve, t):
                n = rows_of(t)
                c0, c1 = cols_of(t)
                for g in range(2):
                    dve.wait_ge(self.tr, 2 * self.c + 2 * t + g + 1)
                    ps = bank[4 + (2 * t + g) % 4][:, 0:4 * n].rearrange("p (k c) -> p k c", k=4)
                    dve.tensor_tensor(uT[:, 4 * g:4 * g + 4, c0:c1], ps,
                                      gcol[:, self.gain, 4 * g:4 * g + 4].unsqueeze(2).broadcast_to([128, 4, n]),
                                      ALU.mult).then_inc(self.ev, 1)

            def pool_tile(self, pool, t):
                n = rows_of(t)
                pool.wait_ge(self.ms, self.c + t + 1)
                pool.tensor_tensor(self.rstd[0:n, t:t + 1], self.mean[0:n, t:t + 1], minus_half[0:n, 0:1],
                                   ALU.pow).then_inc(self.rs, 1)

            def pe_tile(self, pe, t):
                n = rows_of(t)
                pe.wait_ge(self.hn, self.c + t + 1)
                for g in range(2):
                    i = 2 * t + g
                    if i >= 4:
                        pe.wait_ge(self.ev, 2 * self.c + i - 3)
                    for k in range(4):
                        ins = pe.transpose(bank[4 + i % 4][:, k * n:(k + 1) * n],
                                           self.hnorm[0:n, t, (4 * g + k) * 128:(4 * g + k + 1) * 128],
                                           ident[0:n, 0:n])
                    ins.then_inc(self.tr, 1)

            def act(self, act, step, h_in=0):
                for t in range(NT):
                    self.act_tile(act, t)
                for t in range(NT):
                    c0, c1 = cols_of(t)
                    act.wait_ge(self.ev, 2 * (self.c + t + 1))
                    act.activation(high(uH.cols(c0, c1)), uT[:, :, c0:c1], ACT.Copy).then_inc(self.hi, 1)

            def dve_low(self, dve, t):
                c0, c1 = cols_of(t)
                dve.wait_ge(self.hi, self.c // 2 + t + 1)
                dve.tensor_tensor(high(uT[:, :, c0:c1]), uT[:, :, c0:c1], part(uH.cols(c0, c1)), ALU.subtract)

            def dve(self, dve, step):
                self.dve_mean(dve, 0)
                for t in range(NT):
                    if t + 1 < NT:
                        self.dve_mean(dve, t + 1)
                    self.dve_scale(dve, t)
                    if t:
                        self.dve_uT(dve, t - 1)
                    if t > 1:
                        self.dve_low(dve, t - 2)
                self.dve_uT(dve, NT - 1)
                self.dve_low(dve, NT - 2)
                self.dve_low(dve, NT - 1)

            def pool(self, pool):
                for t in range(NT):
                    self.pool_tile(pool, t)

            def pe(self, pe):
                for t in range(NT):
                    self.pe_tile(pe, t)

        class Experts:
            consts_in, logits, sub, exp, aff_ready, affT, pos, posT_done, onehot, picked, chosen = (
                sem("sel_" + x) for x in ("consts_in", "logits", "sub", "exp", "aff_ready", "affT", "pos", "posT_done",
                                          "onehot", "picked", "chosen"))
            sent = sem("moe_sent")
            w_hi, w_lo, x_hi, x_lo, h_hi, h_lo = (sem("moe_" + x) for x in ("w_high", "w_low", "x_high", "x_low", "h_high", "h_low"))
            HIGH_OF = [0, 1, 2, 0, 3, 2]
            BEFORE = [(3, 0), (1, 0), (5, 0), (0, 1), (4, 0), (2, 1)]

            def __init__(self, layer, gain, normed, resid):
                self.l, self.gain, self.normed, self.resid = layer, gain, normed, resid
                L = f"m{layer}_"
                self.once = layer + 1
                (self.idx_g, self.idx_s, self.gathered, self.scattered, self.xs_turned, self.xT_in,
                 self.silu, self.hidden0, self.hidden1, self.h_turned, self.y) = (
                    sem(L + x) for x in ("idx_g", "idx_s", "gathered", "scattered", "xs_turned", "xT_in", "silu", "hidden0",
                    "hidden1", "h_turned", "y"))
                self.wr = sm(1056 + 128 * layer, KB * NE, k=KB)
                self.iota = sm(1312, CAP)
                self.tok = sm(1378 + NT * layer, NT)
                self.P = ar(0, NT * NE * CAP, t=NT, e=NE)
                self.aff = ar(5280, NT * NE, t=NT)
                self.a2 = ar(5360, NT * NE * 2, t=NT, e=NE)
                self.stat = ar(5520, 20)
                self.m8 = ar(5540, 8)[0:NE]
                self.posT = ar(5548, NT * NE, t=NT)
                self.work = ar(5628, PADS + T)[0:NE]
                self.mask = ar(6162, T)[0:NE]
                self.cum = ar(6690, T)[0:NE]
                self.pick = ar(7218, T)[0:NE]
                self.ones = ar(7746, T)[0:NE]
                self.idx = sm(1388, NE).bitcast(U32)[0:CAP]
                self.gate = sm(1404, NE)[0:CAP]
                self.idxg = sm(1420, 1).bitcast(U32)[0:CAP]
                self.idxs = sm(1421, 1).bitcast(U32)[0:CAP]
                self.xs = ar(0, D)[0:CAP]
                self.sg = ar(1024, D)[0:CAP]
                self.hid = ar(2048, D)[0:CAP]
                self.y_sb = ar(3072, D)[0:CAP]
                self.xT, self.xTh, self.hTh, self.hTl = (ar(4096 + i * KB * CAP, KB * CAP, k=KB) for i in range(4))
                self.wh = [ar(4096 + 4 * KB * CAP + i * KB * BLK, KB * BLK, k=KB) for i in range(4)]

            def consts(self, act):
                act.dma_start(self.wr, a["router_w"][self.l].rearrange("(k p) e -> p k e", p=128)).then_inc(self.consts_in, 16)
                act.dma_start(self.tok, a["c_token"][self.l]).then_inc(self.consts_in, 16)
                if self.l == 0:
                    act.dma_start(self.iota, a["c_iota"][:, :]).then_inc(self.consts_in, 16)

            VIEWS = [(NM, 0, 1), (128, 1, NT)]

            def select_pe(self, pe):
                pe.wait_ge(self.consts_in, 80)
                pe.wait_ge(outs[self.l].added, 2 * NT * self.once)
                pe.wait_ge(Norm.ev, 4 * NT * self.once)
                lg = bank[0]
                for t in range(NT):
                    n = rows_of(t)
                    c0, c1 = cols_of(t)
                    for k in range(KB):
                        ins = pe.matmul(lg[0:n, t * NE:(t + 1) * NE], uT[:, k, c0:c1], self.wr[:, k],
                                        start=(k == 0), stop=(k == KB - 1))
                ins.then_inc(self.logits, 1)
                pe.wait_ge(self.aff_ready, self.once)
                for t in range(NT):
                    n = rows_of(t)
                    ps = bank[1][0:NE, 0:NM] if t == 0 else bank[2][0:NE, 128 * (t - 1):128 * t]
                    ins = pe.transpose(ps, self.aff[0:n, t], ident[0:n, 0:n])
                ins.then_inc(self.affT, 1)
                pe.wait_ge(self.pos, self.once)
                for t in range(NT):
                    n = rows_of(t)
                    c0, c1 = cols_of(t)
                    ins = pe.transpose(bank[3][0:n, t * NE:(t + 1) * NE], self.pick[:, c0:c1], ident[0:NE, 0:NE])
                ins.then_inc(self.posT_done, 1)
                pe.wait_ge(self.onehot, self.once)
                for e in range(NE):
                    for t in range(NT):
                        n = rows_of(t)
                        ins = pe.matmul(bank[4][0:CAP, 2 * e:2 * e + 2], self.P[0:n, t, e], self.a2[0:n, t, e],
                                        start=(t == 0), stop=(t == NT - 1))
                ins.then_inc(self.picked, 1)

            def select_act(self, act):
                act.wait_ge(self.sub, self.once)
                for n, t0, t1 in self.VIEWS:
                    ins = act.activation(self.aff[0:n, t0:t1], self.aff[0:n, t0:t1], ACT.Exp)
                    ins.then_inc(self.exp, 1)

            def select_dve(self, dve, step):
                dve.wait_ge(self.consts_in, 80)
                dve.wait_ge(self.logits, self.once)
                lg = bank[0][:, 0:NT * NE].rearrange("p (t e) -> p t e", t=NT)
                for n, t0, t1 in self.VIEWS:
                    w = t1 - t0
                    step(dve.tensor_reduce(self.stat[0:n, t0:t1], lg[0:n, t0:t1], AX.X, ALU.max))
                    ins = dve.tensor_tensor(self.aff[0:n, t0:t1], lg[0:n, t0:t1],
                                            self.stat[0:n, t0:t1].unsqueeze(2).broadcast_to([n, w, NE]), ALU.subtract)
                    if t0:
                        ins.then_inc(self.sub, 1)
                    else:
                        step(ins)
                dve.memset(self.ones, 1.0)
                dve.memset(self.work[:, 0:PADS], 2.0)
                step(dve.tensor_copy(self.a2[:, :, :, 0], self.tok.unsqueeze(2).broadcast_to([128, NT, NE])))
                dve.wait_ge(self.exp, 2 * self.once)
                for n, t0, t1 in self.VIEWS:
                    w = t1 - t0
                    step(dve.tensor_reduce(self.stat[0:n, 5 + t0:5 + t1], self.aff[0:n, t0:t1], AX.X, ALU.add))
                    step(dve.reciprocal(self.stat[0:n, 10 + t0:10 + t1], self.stat[0:n, 5 + t0:5 + t1]))
                    step(dve.tensor_tensor(self.aff[0:n, t0:t1], self.aff[0:n, t0:t1],
                                           self.stat[0:n, 10 + t0:10 + t1].unsqueeze(2).broadcast_to([n, w, NE]),
                                           ALU.mult))
                    ins = dve.tensor_copy(self.a2[0:n, t0:t1, :, 1], self.aff[0:n, t0:t1])
                    if t0:
                        ins.then_inc(self.aff_ready, 1)
                    else:
                        step(ins)
                dve.wait_ge(self.affT, self.once)
                step(dve.tensor_copy(self.work[:, PADS:PADS + NM], bank[1][0:NE, 0:NM]))
                grid = self.work[:, PADS + NM:]
                src = bank[2][0:NE, :]
                if self.l:
                    for b in range(4):
                        src_b = src[:, 128 * b:128 * b + 128].rearrange("p (c r) -> p r c", r=GRID_H)
                        step(dve.tensor_copy(grid.rearrange("p (r c) -> p r c", r=GRID_H)[:, :, 16 * b:16 * b + 16], src_b))
                else:
                    step(dve.tensor_copy(grid, src))
                for r in range((PADS + CAP) // 8):
                    step(dve.max(self.m8, self.work))
                    step(dve.match_replace(self.work, self.m8, self.work, -1.0))
                step(dve.tensor_scalar(self.mask, self.work[:, PADS:], 0.0, None, ALU.is_lt))
                step(dve.tensor_tensor_scan(self.cum, self.ones, self.mask, 0.0, ALU.mult, ALU.add))
                step(dve.tensor_tensor(self.pick[:, 0:NM], self.cum[:, 0:NM], self.mask[:, 0:NM], ALU.mult))
                if self.l:
                    for b in range(4):
                        cut = lambda x: x[:, NM:].rearrange("p (r c) -> p c r", r=GRID_H)[:, 16 * b:16 * b + 16, :]
                        dst = self.pick[:, NM + 128 * b:NM + 128 * b + 128].rearrange("p (c r) -> p c r", r=GRID_H)
                        ins = dve.tensor_tensor(dst, cut(self.cum), cut(self.mask), ALU.mult)
                        if b < 3:
                            step(ins)
                else:
                    ins = dve.tensor_tensor(self.pick[:, NM:], self.cum[:, NM:], self.mask[:, NM:], ALU.mult)
                ins.then_inc(self.pos, 1)
                dve.wait_ge(self.posT_done, self.once)
                pt = bank[3][:, 0:NT * NE].rearrange("p (t e) -> p t e", t=NT)
                for t in range(NT):
                    n = rows_of(t)
                    step(dve.tensor_copy(self.posT[0:n, t], pt[0:n, t]))
                    ins = dve.tensor_tensor(self.P[0:n, t], self.posT[0:n, t].unsqueeze(2).broadcast_to([n, NE, CAP]),
                                            self.iota[0:n].unsqueeze(1).broadcast_to([n, NE, CAP]), ALU.is_equal)
                    if t == NT - 1:
                        ins.then_inc(self.onehot, 1)
                    else:
                        step(ins)
                dve.wait_ge(self.picked, self.once)
                ps = bank[4][0:CAP, 0:2 * NE].rearrange("p (e x) -> p e x", x=2)
                step(dve.tensor_copy(self.idx, ps[:, :, 0]))
                dve.tensor_copy(self.gate, ps[:, :, 1]).then_inc(self.chosen, 1)

            def loop(self, eng, body):
                body(eng, 0, False)
                with eng.Fori(1, NE - 1) as e:
                    body(eng, e, False)
                body(eng, NE - 1, True)

            def freed(self, eng, s, value):
                if not (isinstance(value, int) and value == 0):
                    eng.wait_ge(s, value)

            def units(self, j):
                s = moe_slots[self.l][j]
                return s, moe_base[self.l][0][s], moe_base[self.l][1][s]

            def turn_xs(self, pe, e, half):
                pe.wait_ge(self.gathered, e * 16 + 16)
                self.freed(pe, self.xT_in, e * 2 + half)
                for k in range(4):
                    c = 128 * (4 * half + k)
                    ins = pe.transpose(bank[7][:, k * CAP:(k + 1) * CAP], self.xs[:, c:c + 128], ident[0:CAP, 0:CAP])
                ins.then_inc(self.xs_turned, 1)

            def nth(self, e, per_expert, i):
                return e * per_expert + (self.l * NE * per_expert + i)

            def pe_body(self, pe, e, last):
                def weights(j):
                    s, _, _ = self.units(j)
                    return (lambda k: self.wh[self.HIGH_OF[j]][:, k]), (lambda k: ring[:, s, k])

                x = (lambda k: self.xTh[:, k]), (lambda k: self.xT[:, k])
                hid = (lambda k: self.hTh[:, k]), (lambda k: self.hTl[:, k])

                def product(b, lhs, j, ks=range(KB)):
                    pe.wait_ge(self.w_hi, self.nth(e, MOE_UNITS, j + 1))
                    low = lambda: pe.wait_ge(self.w_lo, self.nth(e, MOE_UNITS, j + 1))
                    return product3(pe, bank[b][0:CAP, :], lhs, weights(j), ks, ks[0] == 0, ks[-1] == KB - 1,
                                    order=((0, 0), (1, 0), (0, 1)), before_last=low)

                def used(j):
                    return ring_used[self.units(j)[0]]

                def turn_hidden(half):
                    pe.wait_ge(self.hidden[half], e + 1)
                    if self.l or half or not (isinstance(e, int) and e == 0):
                        pe.wait_ge(self.h_lo, self.nth(e, 2, half))
                    for k in range(4):
                        ins = pe.transpose(bank[6][:, k * CAP:(k + 1) * CAP],
                                           self.hid[:, half * BLK + 128 * k:half * BLK + 128 * k + 128],
                                           ident[0:CAP, 0:CAP])
                    ins.then_inc(self.h_turned, 1)

                pe.wait_ge(self.x_lo, self.nth(e, 2, 2))
                self.freed(pe, self.hidden[0], e)
                product(0, x, 0).then_inc(used(0), 1)
                product(1, x, 1).then_inc(used(1), 1)
                self.freed(pe, self.hidden[1], e)
                product(2, x, 2).then_inc(used(2), 1)
                turn_hidden(0)
                product(3, x, 3).then_inc(used(3), 1)
                pe.wait_ge(self.h_lo, self.nth(e, 2, 1))
                self.freed(pe, self.y, e * 2)
                product(4, hid, 4, range(4))
                turn_hidden(1)
                if not last:
                    self.turn_xs(pe, e + 1, 0)
                product(5, hid, 5, range(4))
                pe.wait_ge(self.h_lo, self.nth(e, 2, 2))
                product(4, hid, 4, range(4, KB)).then_inc(used(4), 1)
                if not last:
                    self.turn_xs(pe, e + 1, 1)
                product(5, hid, 5, range(4, KB)).then_inc(used(5), 1)

            def high_part(self, act, e, j):
                s, fills, _ = self.units(j)
                other, same = self.BEFORE[j]
                act.wait_ge(ring_in[s], (e + fills + 1) * 16)
                s2, _, uses = self.units(other)
                act.wait_ge(ring_used[s2], e + uses + same)
                act.activation(high(self.wh[self.HIGH_OF[j]]), ring[:, s], ACT.Copy).then_inc(self.w_hi, 1)

            def low_part(self, dve, e, j):
                s, _, _ = self.units(j)
                dve.wait_ge(self.w_hi, self.nth(e, MOE_UNITS, j + 1))
                dve.tensor_tensor(high(ring[:, s]), ring[:, s], part(self.wh[self.HIGH_OF[j]]),
                                  ALU.subtract).then_inc(self.w_lo, 1)

            def x_high(self, act, e):
                for half in range(2):
                    act.wait_ge(self.xT_in, e * 2 + half + 1)
                    act.activation(high(self.xTh[:, 4 * half:4 * half + 4]), self.xT[:, 4 * half:4 * half + 4],
                                   ACT.Copy).then_inc(self.x_hi, 1)

            def x_low(self, dve, e):
                for half in range(2):
                    x, xh = self.xT[:, 4 * half:4 * half + 4], self.xTh[:, 4 * half:4 * half + 4]
                    dve.wait_ge(self.x_hi, self.nth(e, 2, half + 1))
                    dve.tensor_tensor(high(x), x, part(xh), ALU.subtract).then_inc(self.x_lo, 1)

            def act_body(self, act, e, last):
                def silu(half):
                    s, _, n = self.units(2 * half)
                    act.wait_ge(ring_used[s], e + n + 1)
                    self.freed(act, self.hidden[half], e)
                    act.activation(self.sg[:, half * BLK:half * BLK + BLK], bank[2 * half][0:CAP, :],
                                   ACT.Silu).then_inc(self.silu, 1)

                def hidden_high(half):
                    act.wait_ge(self.h_turned, e * 2 + half + 1)
                    act.activation(high(self.hTh[:, 4 * half:4 * half + 4]),
                                   bank[6][:, 0:4 * CAP].rearrange("p (k c) -> p k c", k=4),
                                   ACT.Copy).then_inc(self.h_hi, 1)

                self.high_part(act, e, 2)
                silu(0)
                self.high_part(act, e, 3)
                self.high_part(act, e, 4)
                silu(1)
                hidden_high(0)
                self.high_part(act, e, 5)
                hidden_high(1)
                if not last:
                    self.x_high(act, e + 1)
                    self.high_part(act, e + 1, 0)
                    self.high_part(act, e + 1, 1)

            def xT_copy(self, dve, e):
                for half in range(2):
                    dve.wait_ge(self.xs_turned, e * 2 + half + 1)
                    g = gcol[:, self.gain, 4 * half:4 * half + 4]
                    dve.tensor_tensor(self.xT[:, 4 * half:4 * half + 4],
                                      bank[7][:, 0:4 * CAP].rearrange("p (k c) -> p k c", k=4),
                                      g.unsqueeze(2).broadcast_to([128, 4, CAP]), ALU.mult).then_inc(self.xT_in, 1)

            def dve_body(self, dve, e, last):
                def hidden_values(half):
                    s, _, n = self.units(2 * half + 1)
                    dve.wait_ge(ring_used[s], e + n + 1)
                    dve.wait_ge(self.silu, e * 2 + half + 1)
                    dve.tensor_tensor(self.hid[:, half * BLK:half * BLK + BLK], self.sg[:, half * BLK:half * BLK + BLK],
                                      bank[2 * half + 1][0:CAP, :], ALU.mult).then_inc(self.hidden[half], 1)

                def hidden_low(half):
                    dve.wait_ge(self.h_hi, self.nth(e, 2, half + 1))
                    dve.tensor_tensor(high(self.hTl[:, 4 * half:4 * half + 4]),
                                      bank[6][:, 0:4 * CAP].rearrange("p (k c) -> p k c", k=4),
                                      part(self.hTh[:, 4 * half:4 * half + 4]), ALU.subtract).then_inc(self.h_lo, 1)

                self.low_part(dve, e, 2)
                self.low_part(dve, e, 3)
                hidden_values(0)
                self.low_part(dve, e, 4)
                hidden_low(0)
                self.low_part(dve, e, 5)
                hidden_values(1)
                hidden_low(1)
                if not last:
                    self.xT_copy(dve, e + 1)
                    self.x_low(dve, e + 1)
                self.freed(dve, self.scattered, e * 16)
                for half in range(2):
                    if not last:
                        self.low_part(dve, e + 1, half)
                    s, _, n = self.units(4 + half)
                    dve.wait_ge(ring_used[s], e + n + 1)
                    dve.tensor_scalar(self.y_sb[:, half * BLK:half * BLK + BLK], bank[4 + half][0:CAP, :],
                                      self.gate[:, bass.ds(e, 1)], None, ALU.mult).then_inc(self.y, 1)

            def gather(self, pool, e, count):
                pool.tensor_copy(self.idxg, self.idx[:, bass.ds(e, 1)]).then_inc(self.idx_g, 1)
                pool.wait_ge(self.idx_g, count)
                pool.sem_inc(self.sent, 1)
                pool.indirect_dma_start(out=self.xs, out_offset=None, in_=self.normed,
                                        in_offset=bass.IndirectOffsetOnAxis(ap=self.idxg, axis=0)).then_inc(self.gathered, 16)

            def pool_body(self, pool, e, last):
                self.freed(pool, self.scattered, e * 16)
                pool.tensor_copy(self.idxs, self.idx[:, bass.ds(e, 1)]).then_inc(self.idx_s, 1)
                if not last:
                    pool.wait_ge(self.xs_turned, e * 2 + 2)
                    self.gather(pool, e + 1, e + 2)
                pool.wait_ge(self.idx_s, e + 1)
                pool.wait_ge(self.y, e * 2 + 2)
                pool.sem_inc(self.sent, 1)
                pool.indirect_dma_start(out=self.resid, out_offset=bass.IndirectOffsetOnAxis(ap=self.idxs, axis=0),
                                        in_=self.y_sb, in_offset=None, compute_op=ALU.add).then_inc(self.scattered, 16)

        ex = []
        for layer in range(2):
            x = Experts(layer, 1 + 2 * layer, hn_dram[layer], h_dram if layer == 0 else out)
            x.hidden = [x.hidden0, x.hidden1]
            ex.append(x)

        EV, at = {}, 0
        for nm, n in (("rows", 4 * T), ("v1", NT * NH * (HD + 1)), ("qk", 8 * T), ("rqk", 8 * T),
                      ("sgo", NT * BLK), ("sgr", NT * BLK), ("rv", NT * BLK), ("tmp", 1780)):
            EV[nm] = at
            at += n
        EVT = {"v1": ar(EV["v1"], NT * NH * (HD + 1), t=NT, h=NH), "qk": ar(EV["qk"], 8 * T, k=8),
               "rqk": ar(EV["rqk"], 8 * T, k=8), "sgo": ar(EV["sgo"], NT * BLK, t=NT),
               "sgr": ar(EV["sgr"], NT * BLK, t=NT), "rv": ar(EV["rv"], NT * BLK, t=NT)}
        lgam = sm(1516, 8)
        uflat = uT[:, :, :].rearrange("p k t -> p (k t)")

        class EvenIn:
            ORDER = ["mq", "mk", "mv", "mo", "rq", "rk", "rv", "rg"]

            def __init__(self):
                (self.consts_in, self.product, self.taken, self.raw, self.conv, self.gate_product,
                 self.gate_copied, self.gate_turned, self.rope, self.turned, self.turned_taken,
                 self.pad) = (
                    sem("ei_" + x) for x in ("consts_in", "product", "taken", "raw", "conv", "gate_product", "gate_copied",
                    "gate_turned", "rope", "turned", "turned_taken", "pad"))
                self.convw = sm(20, 2 * NH * CONV, f=2 * NH)
                self.wg = sm(60, KB * 16, k=KB)
                self.gtok = sm(188, NT * 16, t=NT)
                self.rows = [ar(EV["rows"] + i * T, T)[0:NH] for i in range(4)]
                self.gb = sm(268, 4)[0:NH]
                self.rawbuf = [ar(EV["tmp"] + i * (T + 4), T + 4) for i in range(2)]
                self.rope_a, self.rope_b, self.rope_o = (ar(EV["tmp"] + i * BLK, BLK) for i in range(3))
                self.cs = sm(280, NT * 128, t=NT)
                self.groups = []
                for u in range(8):
                    n = 4 if u < 2 else NT
                    self.groups += [(u, i) for i in range(n)]

            def consts(self, act):
                act.dma_start(self.convw, a["even_conv_w"][:, :, :]).then_inc(self.consts_in, 16)
                act.dma_start(self.wg, a["even_w_in"][:, 2048:2064].rearrange("(k p) c -> p k c", p=128)).then_inc(self.consts_in, 16)
                act.dma_start(self.gb, a["even_gate_b"].rearrange("(t h) -> h t", h=NH),
                              allow_slow_non_contiguous=True).then_inc(self.consts_in, 16)
                act.dma_start(self.cs, a["c_rope"][:, :, :]).then_inc(self.consts_in, 16)

            def pe(self, pe):
                pe.wait_ge(self.consts_in, 64)
                for t in range(NT):
                    n = rows_of(t)
                    c0, c1 = cols_of(t)
                    for i, x in enumerate(tokens(c0, c1)):
                        for k in range(KB):
                            ins = pe.matmul(bank[6][0:n, 16 * t:16 * t + 16], part(x(k)), self.wg[:, k],
                                            start=(i == 0 and k == 0), stop=(i == 1 and k == KB - 1))
                ins.then_inc(self.gate_product, 1)
                pe.wait_ge(self.gate_copied, 1)
                for i in range(4):
                    for t in range(NT):
                        n = rows_of(t)
                        ps = bank[4][0:NH, i * NM:(i + 1) * NM] if t == 0 else bank[i][0:NH, 128 * (t - 1):128 * t]
                        ins = pe.transpose(ps, self.gtok[0:n, t, 4 * i:4 * i + 4], ident[0:n, 0:n])
                ins.then_inc(self.gate_turned, 1)
                pe.wait_ge(self.gate_copied, 2)
                turn = 0
                for g, (u, i) in enumerate(self.groups):
                    if i == 0:
                        halves[0].ready(pe, u)
                    if g >= 4:
                        pe.wait_ge(self.taken, g - 3)
                    b = bank[g % 4]
                    if u < 2:
                        w = halves[0].weights(u, 128 * i, 128 * i + 128)
                        product3(pe, b[:, :], w, tokens(NM, T), range(KB), True, True)
                        if g >= 2:
                            pe.wait_ge(self.taken, g - 1)
                        ins = product3(pe, bank[4 + g % 2][:, 0:NM], w, tokens(0, NM), range(KB), True, True)
                    else:
                        c0, c1 = cols_of(i)
                        ins = product3(pe, b[0:rows_of(i), :], tokens(c0, c1), halves[0].weights(u), range(KB), True, True)
                    ins.then_inc(self.product, 1)
                    for u2, i2 in ([self.groups[g - 1]] if self.groups[g - 1][0] in (4, 5) and g else []):
                        n = rows_of(i2)
                        pe.wait_ge(self.rope, turn + 1)
                        if turn >= 2:
                            pe.wait_ge(self.turned_taken, turn - 1)
                        for h in range(NH):
                            ins2 = pe.transpose(bank[6 + turn % 2][:, h * n:(h + 1) * n],
                                                self.rope_o[0:n, 128 * h:128 * h + 128], ident[0:n, 0:n])
                        ins2.then_inc(self.turned, 1)
                        turn += 1
                    if i == (3 if u < 2 else NT - 1):
                        pe.wait_ge(self.product, g + 1)
                        halves[0].used(pe, u)
                pe.sem_inc(ring_used[TOKEN_SLOT], 1)

            def act(self, act, step):
                halves[0].act(act, 0)
                for g, (u, i) in enumerate(self.groups):
                    n = rows_of(i)
                    b = bank[g % 4]
                    if i == 1:
                        halves[0].act(act, u + 1)
                    if u < 2:
                        f = 4 * u + i
                        act.wait_ge(self.product, g + 1)
                        if f >= 2:
                            act.wait_ge(self.conv, f - 1)
                        else:
                            act.wait_ge(self.pad, 1)
                        step(act.activation(self.rawbuf[f % 2][:, 2:2 + NM], bank[4 + g % 2][:, 0:NM], ACT.Copy))
                        act.activation(self.rawbuf[f % 2][:, 2 + NM:2 + T], b[:, :], ACT.Copy).then_inc(self.taken, 1)
                        if f >= 1:
                            self.silu_conv(act, f - 1)
                        if f == 7:
                            self.silu_conv(act, 7)
                    elif u in (4, 5):
                        if u == 4:
                            continue
                    else:
                        act.wait_ge(self.product, g + 1)
                        act.wait_ge(self.taken, g)
                        if u == 2:
                            dst = EVT["v1"][0:n, i, :, 0:HD]
                            act.activation(dst, b[0:n, :].rearrange("p (h e) -> p h e", h=NH), ACT.Copy).then_inc(self.taken, 1)
                        else:
                            dst, f = {3: (EVT["sgo"], ACT.Sigmoid), 6: (EVT["rv"], ACT.Copy), 7: (EVT["sgr"], ACT.Silu)}[u]
                            act.activation(dst[0:n, i], b[0:n, :], f).then_inc(self.taken, 1)

            def silu_conv(self, act, f):
                act.wait_ge(self.conv, f + 1)
                act.activation(EVT["qk"][:, f], EVT["qk"][:, f], ACT.Silu).then_inc(self.raw, 1)

            def dve(self, dve, step):
                for r in self.rawbuf:
                    step(dve.memset(r[:, 0:2], 0.0))
                    ins = dve.memset(r[:, T + 2:T + 4], 0.0)
                    if r is self.rawbuf[1]:
                        ins.then_inc(self.pad, 1)
                    else:
                        step(ins)
                step(dve.memset(EVT["v1"][:, :, :, HD:HD + 1], 1.0))
                halves[0].dve(dve, 0)
                dve.wait_ge(self.gate_product, 1)
                step(dve.tensor_copy(self.gtok[0:NM, 0], bank[6][0:NM, 0:16]))
                dve.tensor_copy(self.gtok[:, 1:NT], bank[6][:, 16:80].rearrange("p (t c) -> p t c", t=4)).then_inc(self.gate_copied, 1)
                dve.wait_ge(self.gate_turned, 1)
                for i in range(4):
                    gb = self.gb[:, i:i + 1]
                    step(dve.tensor_scalar(self.rows[i][:, 0:NM], bank[4][0:NH, i * NM:(i + 1) * NM], gb, None, ALU.add))
                    ins = dve.tensor_scalar(self.rows[i][:, NM:T], bank[i][0:NH, :], gb, None, ALU.add)
                    if i < 3:
                        step(ins)
                    else:
                        ins.then_inc(self.gate_copied, 1)
                turn = 0
                for g, (u, i) in enumerate(self.groups):
                    n = rows_of(i)
                    b = bank[g % 4]
                    if i == 2:
                        halves[0].dve(dve, u + 1)
                    if u < 2:
                        f = 4 * u + i
                        dve.wait_ge(self.taken, g + 1)
                        raw, acc = self.rawbuf[f % 2], EVT["qk"][:, f]
                        step(dve.tensor_scalar(acc, raw[:, 0:T], self.convw[:, f, 0:1], None, ALU.mult))
                        for w in range(1, CONV):
                            ins = dve.scalar_tensor_tensor(acc, raw[:, w:w + T], self.convw[:, f, w:w + 1], acc,
                                                           ALU.mult, ALU.add)
                            if w < CONV - 1:
                                step(ins)
                            else:
                                ins.then_inc(self.conv, 1)
                    elif u in (4, 5):
                        dve.wait_ge(self.product, g + 1)
                        dve.wait_ge(self.taken, g)
                        x = b[0:n, :].rearrange("p (h s e) -> p h s e", h=NH, s=2)
                        xv = lambda y: y[0:n].rearrange("p (h s e) -> p h s e", h=NH, s=2)
                        cos = self.cs[0:n, i, 0:64].unsqueeze(1).broadcast_to([n, NH, 64])
                        sin = self.cs[0:n, i, 64:128].unsqueeze(1).broadcast_to([n, NH, 64])
                        A, B, O = xv(self.rope_a), xv(self.rope_b), xv(self.rope_o)
                        if turn:
                            dve.wait_ge(self.turned, turn)
                        step(dve.tensor_tensor(A[:, :, 0], x[:, :, 0], cos, ALU.mult))
                        step(dve.tensor_tensor(A[:, :, 1], x[:, :, 1], cos, ALU.mult))
                        step(dve.tensor_tensor(B[:, :, 0], x[:, :, 1], sin, ALU.mult))
                        dve.tensor_tensor(B[:, :, 1], x[:, :, 0], sin, ALU.mult).then_inc(self.taken, 1)
                        dve.wait_ge(self.taken, g + 1)
                        step(dve.tensor_tensor(O[:, :, 0], A[:, :, 0], B[:, :, 0], ALU.subtract))
                        dve.tensor_tensor(O[:, :, 1], A[:, :, 1], B[:, :, 1], ALU.add).then_inc(self.rope, 1)
                        if turn:
                            self.copy_turned(dve, turn - 1)
                        turn += 1
                self.copy_turned(dve, turn - 1)

            def copy_turned(self, dve, turn):
                u, i = turn // NT, turn % NT
                n = rows_of(i)
                c0, c1 = cols_of(i)
                dve.wait_ge(self.turned, turn + 1)
                dve.tensor_copy(EVT["rqk"][:, 4 * u:4 * u + 4, c0:c1],
                                bank[6 + turn % 2][:, 0:4 * n].rearrange("p (h c) -> p h c", h=NH)).then_inc(self.turned_taken, 1)

        class Gates:

            def __init__(self, rows):
                (self.neg, self.soft, self.rows, self.m, self.turned, self.lneg, self.lsoft,
                 self.logit_in) = (
                    sem("g_" + x) for x in ("neg", "soft", "rows", "m", "turned", "lneg", "lsoft", "logit_in"))
                self.raw = rows
                self.logit, self.lg_e = sm(1500, 8), sm(1508, 8)
                z = [uT[0:NH, i] for i in range(7)]
                self.t, self.ones, self.zeros = z[0], z[1], z[2]
                self.F, self.em = z[3:5], z[5:7]
                self.Mx = [ar(EV["tmp"] + i * T, T)[0:NH] for i in range(2)]
                self.cols_sb = ar(EV["tmp"] + 2 * T, 2 * 2 * NT * NH, d=2, x=2, t=NT)

            def order(self, d, x):
                return x[:, NM:T] if d == 0 else x[:, T - 1:NM - 1:-1]

            def act(self, act, step):
                for d in range(2):
                    act.wait_ge(self.neg, d + 1)
                    step(act.activation(self.em[d], self.em[d], ACT.Exp))
                    act.activation(self.em[d], self.em[d], ACT.Ln, bias=1.0).then_inc(self.soft, 1)
                act.wait_ge(self.lneg, 1)
                step(act.activation(self.lg_e, self.lg_e, ACT.Exp))
                act.activation(self.lg_e, self.lg_e, ACT.Ln, bias=1.0).then_inc(self.lsoft, 1)
                act.wait_ge(self.m, 1)
                for d in range(2):
                    act.activation(self.em[d], self.em[d], ACT.Exp, scale=-1.0).then_inc(self.rows, 1)
                halves[0].act(act, 9)

            def dve(self, dve, step):
                step(dve.memset(self.ones, 1.0))
                step(dve.memset(self.zeros, 0.0))
                for d in range(2):
                    f = self.raw[2 * d + 1]
                    dve.scalar_tensor_tensor(self.em[d], f, -1.0, f, ALU.mult, ALU.min).then_inc(self.neg, 1)
                dve.wait_ge(self.logit_in, 16)
                dve.scalar_tensor_tensor(self.lg_e, self.logit, -1.0, self.logit, ALU.mult, ALU.min).then_inc(self.lneg, 1)
                dve.wait_ge(self.lsoft, 1)
                step(dve.scalar_tensor_tensor(lgam, self.logit, 0.0, self.lg_e, ALU.min, ALU.subtract))
                for d in range(2):
                    i, f = self.raw[2 * d], self.raw[2 * d + 1]
                    F, M = self.F[d], self.Mx[d]
                    dve.wait_ge(self.soft, d + 1)
                    step(dve.scalar_tensor_tensor(self.t, f, 0.0, self.em[d], ALU.min, ALU.subtract))
                    step(dve.tensor_tensor_scan(F[:, 0:NM], self.ones[:, 0:NM], self.t[:, 0:NM], 0.0, ALU.mult, ALU.add))
                    step(dve.tensor_tensor_scan(self.order(d, F), self.ones[:, NM:T], self.order(d, self.t),
                                                F[:, NM - 1:NM], ALU.mult, ALU.add))
                    step(dve.tensor_tensor(i, i, F, ALU.subtract))
                    step(dve.tensor_tensor_scan(M[:, 0:NM], self.zeros[:, 0:NM], i[:, 0:NM], 0.0, ALU.add, ALU.max))
                    step(dve.tensor_tensor_scan(self.order(d, M), self.zeros[:, NM:T], self.order(d, i),
                                                M[:, NM - 1:NM], ALU.add, ALU.max))
                    ins = dve.tensor_tensor(self.em[d], F, M, ALU.add)
                    if d:
                        ins.then_inc(self.m, 1)
                    else:
                        step(ins)
                dve.wait_ge(self.turned, 1)
                ps = bank[0][:, 0:2 * 2 * NT * NH].rearrange("p (d x t h) -> p d x t h", d=2, x=2, t=NT)
                for d in range(2):
                    for x in range(2):
                        step(dve.tensor_copy(self.cols_sb[0:NM, d, x, 0], ps[0:NM, d, x, 0]))
                        step(dve.tensor_copy(self.cols_sb[:, d, x, 1:NT], ps[:, d, x, 1:NT]))
                halves[0].dve(dve, 9)

            def pe(self, pe):
                pe.wait_ge(self.rows, 2)
                for d in range(2):
                    for x, row in enumerate((self.raw[2 * d], self.em[d])):
                        for t in range(NT):
                            n = rows_of(t)
                            c0, c1 = cols_of(t)
                            o = ((d * 2 + x) * NT + t) * NH
                            ins = pe.transpose(bank[0][0:n, o:o + NH], row[:, c0:c1], ident[0:NH, 0:NH])
                ins.then_inc(self.turned, 1)

            def a_col(self, d, t, h):
                return self.cols_sb[0:rows_of(t), d, 0, t, h:h + 1]

            def em_col(self, d, t0, t1, n, h):
                return self.cols_sb[0:n, d, 1, t0:t1, h]

        def qcols(kt, d):
            return (128 * kt, NR) if d == 0 else (0, 128 * kt + 128)

        PACK = [[0, 512, 896, 1152], [0, 128, 384, 768]]
        TRI = 1280

        class HeadNorm:

            def __init__(self, k, gate):
                self.sq, self.ms, self.rs, self.done = (sem(f"hn{k}_{x}") for x in ("sq", "ms", "rs", "done"))
                self.gate = gate
                self.buf = [ar(EV["tmp"] + 2 * T + 80, NT * HD, t=NT), ar(EV["rows"], NT * HD, t=NT)]
                self.junk = ar(EV["rows"] + 640, HD)
                self.ss, self.mean, self.rstd = (sm(1524 + 5 * i, 5) for i in range(3))

            def act(self, act, h):
                for t in range(NT):
                    n = rows_of(t)
                    if NT * h + t:
                        act.wait_ge(self.sq, NT * h + t)
                    act.activation(self.junk[0:n], self.buf[h % 2][0:n, t], ACT.Square,
                                   accum_out=self.ss[0:n, t:t + 1]).then_inc(self.sq, 1)

            def dve_mean(self, dve, h):
                dve.wait_ge(self.sq, NT * (h + 1))
                if h:
                    dve.wait_ge(self.rs, 2 * h)
                for n, t0, t1 in ((NM, 0, 1), (128, 1, NT)):
                    dve.tensor_scalar(self.mean[0:n, t0:t1], self.ss[0:n, t0:t1], 1.0 / HD, EPS, ALU.mult,
                                      ALU.add).then_inc(self.ms, 1)

            def pool(self, pool, h):
                for i, (n, t0, t1) in enumerate(((NM, 0, 1), (128, 1, NT))):
                    pool.wait_ge(self.ms, 2 * h + i + 1)
                    if h:
                        pool.wait_ge(self.done, h)
                    pool.tensor_tensor(self.rstd[0:n, t0:t1], self.mean[0:n, t0:t1],
                                       minus_half[0:n, 0:1].broadcast_to([n, t1 - t0]), ALU.pow).then_inc(self.rs, 1)

            def dve_apply(self, dve, h):
                dve.wait_ge(self.rs, 2 * h + 2)
                for t in range(NT):
                    n = rows_of(t)
                    g = self.gate[0:n, t, HD * h:HD * h + HD]
                    ins = dve.scalar_tensor_tensor(g, self.buf[h % 2][0:n, t], self.rstd[0:n, t:t + 1], g,
                                                   ALU.mult, ALU.mult)
                ins.then_inc(self.done, 1)

        OUT_AT = [(6, 2 * (HD + 1)), (6, 0), (6, HD + 1), (7, 0), (7, HD + 1)]

        class MLSTM:

            def __init__(self, gates):
                (self.mbc, self.diag, self.dexp, self.sprod, self.sd, self.oprod, self.comb,
                 self.pre, self.pre_d, self.pre_e, self.pre_sd, self.masks_in) = (
                    sem("ml_" + x) for x in ("mbc", "diag", "dexp", "sprod", "sd", "oprod", "comb", "pre", "pre_d", "pre_e", "pre_sd",
                    "masks_in"))
                self.g = gates
                self.D = [uflat[:, d * TRI:(d + 1) * TRI] for d in range(2)]
                self.Dm = [uflat[0:NM, 2 * TRI + d * NR:2 * TRI + (d + 1) * NR] for d in range(2)]
                self.Dmm = uflat[0:NM, 2 * TRI + 2 * NR:2 * TRI + 2 * NR + 2 * NH * NM].rearrange("p (d h q) -> p d h q", d=2, h=NH)
                self.sel = sm(280, NH * 128, h=NH)[0:NH]
                self.far = sm(800, 256, d=2)
                self.dn = sm(1540, 5)
                self.rd = sm(1545, 5)
                self.norm = HeadNorm(0, EVT["sgo"])

            def consts(self, act):
                act.dma_start(self.sel, a["c_sel"][:, :, :]).then_inc(self.masks_in, 16)
                act.dma_start(self.far, a["c_far"][:, :, :]).then_inc(self.masks_in, 16)

            def q(self, h):
                return EVT["qk"][:, h]

            def k(self, h):
                return EVT["qk"][:, NH + h]

            def pe(self, pe):
                pe.wait_ge(self.masks_in, 32)
                for h in range(NH):
                    pe.matmul(bank[7][0:NM, 128 + NM * h:128 + NM * h + NM], self.k(h)[:, 0:NM], self.q(h)[:, 0:NM],
                              start=True, stop=True)
                for d in range(2):
                    for h in range(NH):
                        o = NM * (NH * d + h)
                        ins = pe.matmul(bank[7][0:NM, o:o + NM], self.sel[:, h, 0:NM], self.g.Mx[d][:, 0:NM],
                                        start=True, stop=True)
                ins.then_inc(self.pre, 1)

                def scores(h):
                    if h:
                        pe.wait_ge(self.sd, 2 * h)
                    for kt in range(4):
                        pe.matmul(bank[kt][:, :], self.k(h)[:, NM + 128 * kt:NM + 128 * kt + 128], self.q(h)[:, NM:T],
                                  start=True, stop=True)
                    pe.matmul(bank[4][0:NM, :], self.k(h)[:, 0:NM], self.q(h)[:, NM:T], start=True,
                              stop=True).then_inc(self.sprod, 1)

                def maxima(s):
                    h, d = s // 2, s % 2
                    if s:
                        pe.wait_ge(self.dexp, s)
                    pe.matmul(bank[5][:, :], self.sel[:, h], self.g.Mx[d][:, NM:T], start=True, stop=True).then_inc(self.mbc, 1)

                scores(0)
                maxima(0)
                pe.wait_ge(self.pre_sd, 2)
                for s in range(2 * NH):
                    h, d = s // 2, s % 2
                    if s < 2 * NH - 1:
                        maxima(s + 1)
                    pe.wait_ge(self.sd, s + 1)
                    if d and h < NH - 1:
                        scores(h + 1)
                    if s:
                        pe.wait_ge(self.comb, s)
                    for t in range(1, NT):
                        qt = t - 1
                        bk, o = OUT_AT[t]
                        ps = bank[bk][:, o:o + HD + 1]
                        pe.matmul(ps, self.Dm[d][:, 128 * qt:128 * qt + 128], EVT["v1"][0:NM, 0, h], start=True, stop=False)
                        kts = range(0, qt + 1) if d == 0 else range(qt, 4)
                        for kt in kts:
                            c = PACK[d][kt] + 128 * qt - qcols(kt, d)[0]
                            ins = pe.matmul(ps, self.D[d][:, c:c + 128], EVT["v1"][:, kt + 1, h], start=False,
                                            stop=(kt == kts[-1]))
                    bk, o = OUT_AT[0]
                    pe.matmul(bank[bk][0:NM, o:o + HD + 1], self.Dmm[:, d, h], EVT["v1"][0:NM, 0, h], start=True,
                              stop=True).then_inc(self.oprod, 1)

            def act(self, act, step):
                act.wait_ge(self.pre_d, 1)
                act.activation(self.Dmm, self.Dmm, ACT.Exp, scale=-1.0).then_inc(self.pre_e, 1)
                for s in range(2 * NH):
                    h, d = s // 2, s % 2
                    act.wait_ge(self.diag, s + 1)
                    for kt in range(4):
                        c0, c1 = qcols(kt, d)
                        o = PACK[d][kt]
                        if d == 0:
                            c0, o = c0 + 128, o + 128
                        else:
                            c1 -= 128
                        if c1 > c0:
                            act.activation(self.D[d][:, o:o + c1 - c0], bank[5][:, c0:c1], ACT.Exp,
                                           bias=self.g.a_col(d, kt + 1, h), scale=-1.0)
                    act.activation(self.Dm[d], bank[5][0:NM, :], ACT.Exp, bias=self.g.a_col(d, 0, h), scale=-1.0)
                    for kt in range(4):
                        o = PACK[d][kt] + (0 if d == 0 else 128 * kt)
                        ins = act.activation(self.D[d][:, o:o + 128], self.D[d][:, o:o + 128], ACT.Exp, scale=-1.0)
                    ins.then_inc(self.dexp, 1)
                    if d == 0 and h:
                        self.squares(act, h - 1)
                self.squares(act, NH - 1)

            def squares(self, act, h):
                act.wait_ge(self.comb, 2 * h + 2)
                self.norm.act(act, h)

            def dve(self, dve, step):
                def diag(s):
                    h, d = s // 2, s % 2
                    dve.wait_ge(self.mbc, s + 1)
                    if s >= 2:
                        dve.wait_ge(self.oprod, s - 1)
                    for kt in range(4):
                        o = PACK[d][kt] + (0 if d == 0 else 128 * kt)
                        ins = dve.scalar_tensor_tensor(self.D[d][:, o:o + 128], bank[5][:, 128 * kt:128 * kt + 128],
                                                       self.g.a_col(d, kt + 1, h), self.far[:, d], ALU.subtract, ALU.max)
                    ins.then_inc(self.diag, 1)

                def weigh(s):
                    h, d = s // 2, s % 2
                    dve.wait_ge(self.sprod, h + 1)
                    dve.wait_ge(self.dexp, s + 1)
                    for kt in range(4):
                        c0, c1 = qcols(kt, d)
                        o = PACK[d][kt]
                        x = self.D[d][:, o:o + c1 - c0]
                        dve.scalar_tensor_tensor(x, bank[kt][:, c0:c1], HEAD_SCALE, x, ALU.mult, ALU.mult)
                    dve.scalar_tensor_tensor(self.Dm[d], bank[4][0:NM, :], HEAD_SCALE, self.Dm[d], ALU.mult,
                                             ALU.mult).then_inc(self.sd, 1)

                def combine(s):
                    h, d = s // 2, s % 2
                    hm = self.norm.buf[h % 2]
                    dve.wait_ge(self.oprod, s + 1)
                    if d == 0 and h >= 2:
                        dve.wait_ge(self.norm.done, h - 1)
                    for (n, t0, t1, bk, o) in ((NM, 0, 1, 6, 2 * (HD + 1)), (128, 1, 3, 6, 0), (128, 3, 5, 7, 0)):
                        den = bank[bk][0:n, o + HD:o + HD + (HD + 1) * (t1 - t0 - 1) + 1:HD + 1]
                        step(dve.scalar_tensor_tensor(self.dn[0:n, t0:t1], den, -1.0, self.g.em_col(d, t0, t1, n, h),
                                                      ALU.mult, ALU.max))
                        step(dve.tensor_tensor(self.dn[0:n, t0:t1], den, self.dn[0:n, t0:t1], ALU.max))
                        step(dve.reciprocal(self.rd[0:n, t0:t1], self.dn[0:n, t0:t1]))
                    for t in range(NT):
                        n = rows_of(t)
                        bk, o = OUT_AT[t]
                        num = bank[bk][0:n, o:o + HD]
                        if d == 0:
                            ins = dve.tensor_scalar(hm[0:n, t], num, self.rd[0:n, t:t + 1], None, ALU.mult)
                        else:
                            ins = dve.scalar_tensor_tensor(hm[0:n, t], num, self.rd[0:n, t:t + 1], hm[0:n, t],
                                                           ALU.mult, ALU.add)
                    ins.then_inc(self.comb, 1)
                    dve.wait_ge(self.comb, s + 1)

                dve.wait_ge(self.pre, 1)
                for d in range(2):
                    for h in range(NH):
                        o = NM * (NH * d + h)
                        ins = dve.scalar_tensor_tensor(self.Dmm[:, d, h], bank[7][0:NM, o:o + NM], self.g.a_col(d, 0, h),
                                                       self.far[0:NM, 0, 0:NM], ALU.subtract, ALU.max)
                ins.then_inc(self.pre_d, 1)
                dve.wait_ge(self.pre_e, 1)
                for d in range(2):
                    dve.scalar_tensor_tensor(self.Dmm[:, d], bank[7][0:NM, 128:128 + NH * NM].rearrange("p (h q) -> p h q", h=NH),
                                             HEAD_SCALE, self.Dmm[:, d], ALU.mult, ALU.mult).then_inc(self.pre_sd, 1)
                diag(0)
                for s in range(2 * NH):
                    h, d = s // 2, s % 2
                    weigh(s)
                    if s < 2 * NH - 1:
                        diag(s + 1)
                    if s:
                        combine(s - 1)
                    if d and h:
                        self.norm.dve_mean(dve, h - 1)
                        self.norm.dve_apply(dve, h - 1)
                combine(2 * NH - 1)
                self.norm.dve_mean(dve, NH - 1)
                self.norm.dve_apply(dve, NH - 1)

            def pool(self, pool):
                for h in range(NH):
                    self.norm.pool(pool, h)

        class Retention:

            def __init__(self):
                (self.consts_in, self.pre, self.table, self.sprod, self.sd, self.oprod, self.comb,
                 self.mm, self.mexp, self.msd) = (
                    sem("re_" + x) for x in ("consts_in", "pre", "table", "sprod", "sd", "oprod", "comb", "mm", "mexp", "msd"))
                self.SD = uflat[:, 0:4 * NR].rearrange("p (k q) -> p k q", k=4)
                self.SDm = uflat[0:NM, 4 * NR:5 * NR]
                self.E = uflat[:, 5 * NR:5 * NR + 896]
                self.ED = uflat[:, 5 * NR + 896:5 * NR + 1024]
                self.Em = uflat[0:NM, 6 * NR + 512:7 * NR + 512]
                self.mmE = sm(280, NH * 2 * NM, h=NH, d=2)[0:NM]
                self.mm = sm(420, NH * NM, h=NH)[0:NM]
                c = EV["v1"]
                self.DF, self.DB = ar(c, NR), ar(c + NR, NR)
                self.MF, self.MB = ar(c + 2 * NR, 128), ar(c + 2 * NR + 128, 128)
                self.dm = ar(c + 2 * NR + 256, 2 * NR, d=2)[0:NM]
                self.Em2 = ar(EV["rows"] + 768, NR)[0:NM]
                self.norm = HeadNorm(1, EVT["sgr"])

            def consts(self, act):
                for dst, n in ((self.DF, "c_df"), (self.DB, "c_db"), (self.MF, "c_mf"), (self.MB, "c_mb")):
                    act.dma_start(dst, a[n][:, :]).then_inc(self.consts_in, 16)
                act.dma_start(self.dm, a["c_dm"][:, :, :]).then_inc(self.consts_in, 16)

            def q(self, h):
                return EVT["rqk"][:, h]

            def k(self, h):
                return EVT["rqk"][:, NH + h]

            def lg(self, d, h, n=128):
                return lgam[0:n, NH * d + h:NH * d + h + 1]

            def pe(self, pe):
                for h in range(NH):
                    ins = pe.matmul(bank[7][0:NM, NM * h:NM * h + NM], self.k(h)[:, 0:NM], self.q(h)[:, 0:NM],
                                    start=True, stop=True)
                ins.then_inc(self.pre, 1)

                def scores(h):
                    if h:
                        pe.wait_ge(self.sd, h)
                    for kt in range(4):
                        pe.matmul(bank[kt][:, :], self.k(h)[:, NM + 128 * kt:NM + 128 * kt + 128], self.q(h)[:, NM:T],
                                  start=True, stop=True)
                    pe.matmul(bank[4][0:NM, :], self.k(h)[:, 0:NM], self.q(h)[:, NM:T], start=True,
                              stop=True).then_inc(self.sprod, 1)

                scores(0)
                pe.wait_ge(self.msd, 1)
                for h in range(NH):
                    pe.wait_ge(self.sd, h + 1)
                    if h < NH - 1:
                        scores(h + 1)
                    if h:
                        pe.wait_ge(self.comb, h)
                    v = lambda t, n: EVT["rv"][0:n, t, HD * h:HD * h + HD]
                    for t in range(1, NT):
                        qt = t - 1
                        bk, o = OUT_AT[t]
                        ps = bank[bk][:, o:o + HD]
                        pe.matmul(ps, self.SDm[:, 128 * qt:128 * qt + 128], v(0, NM), start=True, stop=False)
                        for kt in range(4):
                            pe.matmul(ps, self.SD[:, kt, 128 * qt:128 * qt + 128], v(kt + 1, 128), start=False, stop=(kt == 3))
                    bk, o = OUT_AT[0]
                    pe.matmul(bank[bk][0:NM, o:o + HD], self.mm[:, h], v(0, NM), start=True, stop=True).then_inc(self.oprod, 1)

            def act(self, act, step):
                act.wait_ge(self.consts_in, 80)
                for h in range(NH):
                    for d in range(2):
                        ins = act.activation(self.mmE[:, h, d], self.DF[0:NM, 0:NM], ACT.Exp, scale=self.lg(d, h, NM))
                ins.then_inc(self.mexp, 1)
                for h in range(NH):
                    if h:
                        act.wait_ge(self.sd, h)
                    act.activation(self.E[:, 384:896], self.DF, ACT.Exp, scale=self.lg(0, h))
                    act.activation(self.E[:, 0:384], self.DB[:, 0:384], ACT.Exp, scale=self.lg(1, h))
                    act.activation(self.ED, self.DB[:, 384:512], ACT.Exp, scale=self.lg(1, h))
                    act.activation(self.Em, self.dm[:, 0], ACT.Exp, scale=self.lg(0, h, NM))
                    act.activation(self.Em2, self.dm[:, 1], ACT.Exp, scale=self.lg(1, h, NM)).then_inc(self.table, 1)
                    if h:
                        act.wait_ge(self.comb, h)
                        self.norm.act(act, h - 1)
                act.wait_ge(self.comb, NH)
                self.norm.act(act, NH - 1)

            def dve(self, dve, step):
                dve.wait_ge(self.consts_in, 80)
                dve.wait_ge(self.mexp, 1)
                dve.wait_ge(self.pre, 1)
                for h in range(NH):
                    step(dve.tensor_tensor(self.mm[:, h], self.mmE[:, h, 0], self.mmE[:, h, 1], ALU.add))
                    step(dve.tensor_tensor(self.mm[:, h], self.mm[:, h], self.MF[0:NM, 0:NM], ALU.mult))
                dve.scalar_tensor_tensor(self.mm, bank[7][0:NM, 0:NH * NM].rearrange("p (h q) -> p h q", h=NH),
                                         HEAD_SCALE, self.mm, ALU.mult, ALU.mult).then_inc(self.msd, 1)
                for h in range(NH):
                    dve.wait_ge(self.table, h + 1)
                    diag = self.E[:, 384:512]
                    step(dve.tensor_tensor(diag, diag, self.MF, ALU.mult))
                    step(dve.tensor_tensor(self.ED, self.ED, self.MB, ALU.mult))
                    step(dve.tensor_tensor(diag, diag, self.ED, ALU.add))
                    step(dve.tensor_tensor(self.Em, self.Em, self.Em2, ALU.add))
                    dve.wait_ge(self.sprod, h + 1)
                    if h:
                        dve.wait_ge(self.oprod, h)
                    for kt in range(4):
                        dve.scalar_tensor_tensor(self.SD[:, kt], bank[kt][:, :], HEAD_SCALE,
                                                 self.E[:, 384 - 128 * kt:896 - 128 * kt], ALU.mult, ALU.mult)
                    dve.scalar_tensor_tensor(self.SDm, bank[4][0:NM, :], HEAD_SCALE, self.Em, ALU.mult,
                                             ALU.mult).then_inc(self.sd, 1)
                    if h:
                        self.norm.dve_mean(dve, h - 1)
                        self.norm.dve_apply(dve, h - 1)
                    dve.wait_ge(self.oprod, h + 1)
                    hm = self.norm.buf[h % 2]
                    for t in range(NT):
                        n = rows_of(t)
                        bk, o = OUT_AT[t]
                        ins = dve.tensor_copy(hm[0:n, t], bank[bk][0:n, o:o + HD])
                    ins.then_inc(self.comb, 1)
                self.norm.dve_mean(dve, NH - 1)
                self.norm.dve_apply(dve, NH - 1)

            def pool(self, pool):
                for h in range(NH):
                    self.norm.pool(pool, h)

        class Project:

            turned, copied, high, h_in, product, added = (
                sem("pr_" + x) for x in ("turned", "copied", "high", "h_in", "product", "added"))

            def __init__(self, layer, mix, mixT, mixH, gain, base):
                self.mix, self.mixT, self.mixH, self.gain, self.base = mix, mixT, mixH, gain, base
                self.halves = halves[layer]
                self.c = 2 * NT * layer
                self.h_count = 16 * NT * (layer + 1)

            def turn_pe(self, pe):
                for t in range(NT):
                    n = rows_of(t)
                    for g in range(2):
                        i = 2 * t + g
                        if i >= 4:
                            pe.wait_ge(self.copied, self.c + i - 3)
                        for k in range(4):
                            ins = pe.transpose(bank[i % 4][:, k * n:(k + 1) * n], self.mix(t, 4 * g + k), ident[0:n, 0:n])
                        ins.then_inc(self.turned, 1)

            def turn_dve(self, dve, step):
                for t in range(NT):
                    n = rows_of(t)
                    c0, c1 = cols_of(t)
                    for g in range(2):
                        i = 2 * t + g
                        dve.wait_ge(self.turned, self.c + i + 1)
                        ps = bank[i % 4][:, 0:4 * n].rearrange("p (k c) -> p k c", k=4)
                        dst = self.mixT[:, 4 * g:4 * g + 4, c0:c1]
                        if self.gain is None:
                            ins = dve.tensor_copy(dst, ps)
                        else:
                            ins = dve.tensor_tensor(dst, ps, gcol[:, self.gain, 4 * g:4 * g + 4].unsqueeze(2)
                                                    .broadcast_to([128, 4, n]), ALU.mult)
                        ins.then_inc(self.copied, 1)
                    if t:
                        self.turn_low(dve, t - 1)
                self.turn_low(dve, NT - 1)

            def turn_low(self, dve, t):
                c0, c1 = cols_of(t)
                dve.wait_ge(self.high, self.c // 2 + t + 1)
                dve.tensor_tensor(high(self.mixT[:, :, c0:c1]), self.mixT[:, :, c0:c1], part(self.mixH[:, :, c0:c1]),
                                  ALU.subtract)

            def turn_act(self, act):
                for t in range(NT):
                    c0, c1 = cols_of(t)
                    act.wait_ge(self.copied, self.c + 2 * t + 2)
                    act.activation(high(self.mixH[:, :, c0:c1]), self.mixT[:, :, c0:c1], ACT.Copy).then_inc(self.high, 1)

            def pe(self, pe, norm):
                for half in range(2):
                    u = self.base + half
                    self.halves.ready(pe, u)
                    for t in range(NT):
                        g = NT * half + t
                        c0, c1 = cols_of(t)
                        if g >= 4:
                            pe.wait_ge(self.added, self.c + g - 3)
                        mix = (lambda k: self.mixH[:, k, c0:c1]), (lambda k: self.mixT[:, k, c0:c1])
                        product3(pe, bank[g % 4][0:rows_of(t), :], mix, self.halves.weights(u), range(KB), True,
                                 True).then_inc(self.product, 1)
                        if half and t:
                            norm.pe_tile(pe, t - 1)
                    pe.wait_ge(self.product, self.c + NT * half + NT)
                    self.halves.used(pe, u)
                norm.pe_tile(pe, NT - 1)

            def act(self, act, norm):
                for t in range(NT):
                    act.wait_ge(self.added, self.c + NT + t + 1)
                    norm.act_tile(act, t)

            def dve(self, dve, norm):
                dve.wait_ge(self.h_in, self.h_count)
                for half in range(2):
                    for t in range(NT):
                        g = NT * half + t
                        n = rows_of(t)
                        x = H[0:n, t, BLK * half:BLK * half + BLK]
                        dve.wait_ge(self.product, self.c + g + 1)
                        dve.tensor_tensor(x, bank[g % 4][0:n, :], x, ALU.add).then_inc(self.added, 1)
                        if half:
                            norm.dve_mean(dve, t)
                            if t == NT - 1:
                                norm.dve_uT(dve, t - 1)
                            dve.wait_ge(self.added, self.c + g + 1)
                            norm.dve_scale(dve, t)
                            if 0 < t < NT - 1:
                                norm.dve_uT(dve, t - 1)
                norm.dve_uT(dve, NT - 1)
        OD_Q, OD_K, OD_V, OD_VS, OD_ATT = 0, 4224, 8448, 13568, 16640
        qT, kT = ar(OD_Q, 8 * T, k=8), ar(OD_K, 8 * T, k=8)
        vtok = ar(OD_V, NT * D, t=NT)
        vmid = ar(OD_VS, 3 * D, t=3)
        att = ar(OD_ATT, NT * D, t=NT)

        class OddIn:

            def __init__(self):
                (self.product, self.taken, self.sq, self.ms, self.rs, self.qn, self.turned,
                 self.copied, self.vmid) = (
                    sem("oi_" + x) for x in ("product", "taken", "sq", "ms", "rs", "qn", "turned", "copied", "vmid"))
                self.junk = ar(OD_ATT, BLK)
                self.qn_sb = [ar(OD_ATT + BLK * (i + 1), BLK) for i in range(2)]
                self.ss, self.mean, self.rstd = (sm(20 + 8 * i, 8) for i in range(3))
                self.groups = [(u, t) for u in range(6) for t in range(NT)]

            def pe(self, pe):
                def turn(g):
                    n = rows_of(self.groups[g][1])
                    pe.wait_ge(self.qn, g + 1)
                    if g >= 2:
                        pe.wait_ge(self.copied, g - 1)
                    for k in range(4):
                        ins = pe.transpose(bank[4 + g % 2][:, k * n:(k + 1) * n],
                                           self.qn_sb[g % 2][0:n, 128 * k:128 * k + 128], ident[0:n, 0:n])
                    ins.then_inc(self.turned, 1)

                for g, (j, t) in enumerate(self.groups):
                    if t == 0:
                        halves[1].ready(pe, j)
                    if g >= 4:
                        pe.wait_ge(self.taken, g - 3)
                    c0, c1 = cols_of(t)
                    product3(pe, bank[g % 4][0:rows_of(t), :], tokens(c0, c1), halves[1].weights(j), range(KB), True,
                             True).then_inc(self.product, 1)
                    if 1 <= g <= 4 * NT:
                        turn(g - 1)
                    if t == NT - 1:
                        pe.wait_ge(self.product, g + 1)
                        halves[1].used(pe, j)
                pe.sem_inc(ring_used[TOKEN_SLOT], 1)

            def act(self, act, step):
                halves[1].act(act, 0)
                for g, (j, t) in enumerate(self.groups):
                    n = rows_of(t)
                    if t == 1:
                        halves[1].act(act, j + 1)
                    act.wait_ge(self.product, g + 1)
                    if j < 4:
                        if g:
                            act.wait_ge(self.ms, g)
                        act.activation(self.junk[0:n], bank[g % 4][0:n, :], ACT.Square).then_inc(self.sq, 1)
                    else:
                        act.wait_ge(self.taken, g)
                        act.activation(vtok[0:n, t, BLK * (j - 4):BLK * (j - 3)], bank[g % 4][0:n, :],
                                       ACT.Copy).then_inc(self.taken, 1)
                act.wait_ge(self.taken, 6 * NT)
                for i in range(3):
                    act.dma_start(vmid[0:64, i], vtok[64:128, i + 1]).then_inc(self.vmid, 16)
                    act.dma_start(vmid[64:128, i], vtok[0:64, i + 2]).then_inc(self.vmid, 16)
                act.wait_ge(self.vmid, 96)

            def dve(self, dve, step):
                step(dve.tensor_scalar(gcol[:, 5, 0:1], gcol[:, 5, 0:1], float(AD) ** -0.5, None, ALU.mult))
                halves[1].dve(dve, 0)
                for g, (j, t) in enumerate(self.groups[:4 * NT]):
                    n = rows_of(t)
                    if t == 2:
                        halves[1].dve(dve, j + 1)
                    dve.wait_ge(self.sq, g + 1)
                    step(dve.tensor_reduce(self.ss[0:n], self.junk[0:n].rearrange("p (h e) -> p h e", e=AD), AX.X, ALU.add))
                    dve.tensor_scalar(self.mean[0:n], self.ss[0:n], 1.0 / AD, EPS, ALU.mult, ALU.add).then_inc(self.ms, 1)
                    if g:
                        self.copy(dve, g - 1)
                    dve.wait_ge(self.rs, g + 1)
                    dve.tensor_tensor(self.qn_sb[g % 2][0:n].rearrange("p (h e) -> p h e", e=AD),
                                      bank[g % 4][0:n, :].rearrange("p (h e) -> p h e", e=AD),
                                      self.rstd[0:n].unsqueeze(2).broadcast_to([n, 8, AD]), ALU.mult).then_inc(self.taken, 1)
                    dve.wait_ge(self.taken, g + 1)
                    dve.sem_inc(self.qn, 1)
                self.copy(dve, 4 * NT - 1)
                halves[1].dve(dve, 5)
                halves[1].dve(dve, 6)

            def copy(self, dve, g):
                j, t = self.groups[g]
                c0, c1 = cols_of(t)
                dst = (qT if j < 2 else kT)[:, 4 * (j % 2):4 * (j % 2) + 4, c0:c1]
                dve.wait_ge(self.turned, g + 1)
                dve.tensor_scalar(dst, bank[4 + g % 2][:, 0:4 * (c1 - c0)].rearrange("p (k c) -> p k c", k=4),
                                  gcol[:, 5, j // 2:j // 2 + 1], None, ALU.mult).then_inc(self.copied, 1)

            def pool(self, pool):
                for g, (j, t) in enumerate(self.groups[:4 * NT]):
                    n = rows_of(t)
                    pool.wait_ge(self.ms, g + 1)
                    if g:
                        pool.wait_ge(self.taken, g)
                    pool.tensor_tensor(self.rstd[0:n], self.mean[0:n], minus_half[0:n, 0:1].broadcast_to([n, 8]),
                                       ALU.pow).then_inc(self.rs, 1)

        class Attention:
            KEY0 = [0, 64, 192, 256]
            TABLE = [0, 1, 1, 2]
            W = NM + 256

            def __init__(self):
                (self.product, self.neg, self.exp, self.turned, self.copied, self.pv, self.comb,
                 self.m_s, self.m_sub, self.m_exp, self.m_p, self.m_t, self.m_pt, self.m_o,
                 self.m_done) = (
                    sem("at_" + x) for x in ("product", "neg", "exp", "turned", "copied", "pv", "comb", "m_s", "m_sub", "m_exp", "m_p",
                    "m_t", "m_pt", "m_o", "m_done"))
                self.bias = [uflat[:, 816 * i:816 * i + 816] for i in range(2)]
                self.bias_in = [sem(f"at_bias_in{i}") for i in range(2)]
                o = 1632
                self.P = [uflat[:, o + self.W * i:o + self.W * (i + 1)] for i in range(2)]
                o += 2 * self.W
                self.PT = [uflat[:, o + 384 * i:o + 384 * i + 256] for i in range(2)]
                self.PTm = [uflat[0:NM, o + 384 * i + 256:o + 384 * i + 384] for i in range(2)]
                self.mn = sm(20, 2)
                self.sum = sm(24, 8, b=2)
                self.rinv = sm(32, 4)
                self.mp = sm(40, AH * NM, h=AH)[0:NM]
                self.mpT = sm(300, AH * NM, h=AH)[0:NM]
                self.ms_ = sm(560, 3 * AH, x=3)[0:NM]

            def slot(self, h):
                return h // 2 + 8 * (h % 2)

            def values(self, b):
                t = lambda i: vtok[:, i + 1]
                return [(t(0), t(1)), (vmid[:, 0], vmid[:, 1]), (vmid[:, 1], vmid[:, 2]), (t(2), t(3))][b]

            def load_bias(self, act, h):
                act.dma_start(self.bias[h % 2], a["rpb_tiles"][h]).then_inc(self.bias_in[h % 2], 16)

            def act(self, act, step):
                self.load_bias(act, 0)
                self.load_bias(act, 1)
                act.wait_ge(self.m_sub, 2)
                act.activation(self.mp, self.mp, ACT.Exp).then_inc(self.m_exp, 1)
                halves[1].act(act, 7)
                for s in range(4 * AH):
                    h, b = s // 4, s % 4
                    act.wait_ge(self.neg, s + 1)
                    if b == 0 and h >= 2:
                        act.wait_ge(self.comb, h - 1)
                    act.activation(self.P[s % 2], self.P[s % 2], ACT.Exp, bias=self.mn[:, s % 2:s % 2 + 1], scale=-1.0,
                                   accum_out=self.sum[:, h % 2, b:b + 1]).then_inc(self.exp, 1)
                    if b == 3 and h + 2 < AH:
                        self.load_bias(act, h + 2)

            def dve(self, dve, step):
                dve.wait_ge(self.m_s, 1)
                bc = lambda x: x.unsqueeze(2).broadcast_to([NM, x.shape[1], NM])
                for i in range(2):
                    ps = bank[4 * i][0:NM, 0:8 * NM].rearrange("p (h k) -> p h k", h=8)
                    mx = self.ms_[:, 0, 8 * i:8 * i + 8]
                    step(dve.tensor_reduce(mx, ps, AX.X, ALU.max))
                    dve.tensor_tensor(self.mp[:, 8 * i:8 * i + 8], ps, bc(mx), ALU.subtract).then_inc(self.m_sub, 1)
                dve.wait_ge(self.m_exp, 1)
                step(dve.tensor_reduce(self.ms_[:, 1], self.mp, AX.X, ALU.add))
                step(dve.reciprocal(self.ms_[:, 2], self.ms_[:, 1]))
                dve.tensor_tensor(self.mp, self.mp, bc(self.ms_[:, 2]), ALU.mult).then_inc(self.m_p, 1)
                dve.wait_ge(self.m_t, 1)
                dve.tensor_copy(self.mpT, bank[1][0:NM, 0:AH * NM].rearrange("p (h k) -> p h k", h=AH)).then_inc(self.m_pt, 1)
                dve.wait_ge(self.m_o, 1)
                for i in range(2):
                    dve.tensor_copy(att[0:NM, 0, BLK * i:BLK * i + BLK], bank[2 + i][0:NM, :]).then_inc(self.m_done, 1)

                def scores(s):
                    h, b = s // 4, s % 4
                    dve.wait_ge(self.bias_in[h % 2], 16 * (h // 2 + 1))
                    dve.wait_ge(self.product, s + 1)
                    if s >= 2:
                        dve.wait_ge(self.turned, s - 1)
                    t = self.TABLE[b]
                    dve.tensor_tensor_reduce(self.P[s % 2], bank[s % 2][:, 0:self.W], self.bias[h % 2][:, self.W * t:self.W * (t + 1)],
                                             -1.0, 3e38, ALU.add, ALU.min, self.mn[:, s % 2:s % 2 + 1]).then_inc(self.neg, 1)

                def combine(h):
                    dve.wait_ge(self.exp, 4 * h + 4)
                    step(dve.reciprocal(self.rinv, self.sum[:, h % 2]))
                    dve.wait_ge(self.pv, 4 * h + 4)
                    dve.tensor_tensor(att[:, 1:NT, AD * h:AD * h + AD],
                                      bank[4 + h % 2][:, 0:4 * AD].rearrange("p (b e) -> p b e", b=4),
                                      self.rinv.unsqueeze(2).broadcast_to([128, 4, AD]), ALU.mult).then_inc(self.comb, 1)

                scores(0)
                halves[1].dve(dve, 7)
                for s in range(4 * AH):
                    if s + 1 < 4 * AH:
                        scores(s + 1)
                    dve.wait_ge(self.turned, s + 1)
                    if s >= 2:
                        dve.wait_ge(self.pv, s - 1)
                    dve.tensor_copy(self.PT[s % 2], bank[2 + s % 2][:, 0:256])
                    dve.tensor_copy(self.PTm[s % 2], bank[2 + s % 2][0:NM, 256:384]).then_inc(self.copied, 1)
                    if s % 4 == 1 and s > 4:
                        combine(s // 4 - 1)
                combine(AH - 1)

            def pe(self, pe):
                def head(x, h, c0, c1):
                    return x[AD * (h % 2):AD * (h % 2) + AD, h // 2, c0:c1]

                for h in range(AH):
                    ins = pe.matmul(bank[4 * (h % 2)][0:NM, NM * (h // 2):NM * (h // 2) + NM], head(qT, h, 0, NM),
                                    head(kT, h, 0, NM), start=True, stop=True)
                ins.then_inc(self.m_s, 1)
                pe.wait_ge(self.m_p, 1)
                for h in range(AH):
                    ins = pe.transpose(bank[1][0:NM, NM * h:NM * h + NM], self.mp[:, self.slot(h)], ident[0:NM, 0:NM])
                ins.then_inc(self.m_t, 1)
                pe.wait_ge(self.m_pt, 1)
                for h in range(AH):
                    ins = pe.matmul(bank[2 + h // 8][0:NM, AD * (h % 8):AD * (h % 8) + AD], self.mpT[:, h],
                                    vtok[0:NM, 0, AD * h:AD * h + AD], start=True, stop=True)
                ins.then_inc(self.m_o, 1)
                pe.wait_ge(self.m_done, 2)

                def scores(s):
                    h, b = s // 4, s % 4
                    q = head(qT, h, NM + 128 * b, NM + 128 * b + 128)
                    k0 = NM + self.KEY0[b]
                    pe.matmul(bank[s % 2][:, 0:NM], q, head(kT, h, 0, NM), start=True, stop=True)
                    pe.matmul(bank[s % 2][:, NM:self.W], q, head(kT, h, k0, k0 + 256), start=True, stop=True).then_inc(self.product, 1)

                def values(s):
                    h, b = s // 4, s % 4
                    pe.wait_ge(self.copied, s + 1)
                    if b == 0 and h >= 2:
                        pe.wait_ge(self.comb, h - 1)
                    o = bank[4 + h % 2][:, AD * b:AD * b + AD]
                    v0, v1 = self.values(b)
                    hs = slice(AD * h, AD * h + AD)
                    pe.matmul(o, self.PT[s % 2][:, 0:128], v0[:, hs], start=True, stop=False)
                    pe.matmul(o, self.PT[s % 2][:, 128:256], v1[:, hs], start=False, stop=False)
                    pe.matmul(o, self.PTm[s % 2], vtok[0:NM, 0, hs], start=False, stop=True).then_inc(self.pv, 1)

                scores(0)
                scores(1)
                for s in range(4 * AH):
                    pe.wait_ge(self.exp, s + 1)
                    if s >= 2:
                        pe.wait_ge(self.copied, s - 1)
                    P, ps = self.P[s % 2], bank[2 + s % 2]
                    pe.transpose(ps[:, 0:128], P[:, NM:NM + 128], ident[:, :])
                    pe.transpose(ps[:, 128:256], P[:, NM + 128:self.W], ident[:, :])
                    pe.transpose(ps[0:NM, 256:384], P[:, 0:NM], ident[:, :]).then_inc(self.turned, 1)
                    if s + 2 < 4 * AH:
                        scores(s + 2)
                    if s:
                        values(s - 1)
                values(4 * AH - 1)

        def store_tile(eng, x, dram, layer, t, s):
            if t == 0:
                eng.dma_start(dram[0:NM, :], x[0:NM, 0]).then_inc(s, 16)
            elif layer:
                c0, c1 = cols_of(t)
                eng.dma_start(dram[c0:c1, :], x[:, t]).then_inc(s, 16)
            else:
                by_row = dram[NM:T, :].rearrange("(c r) d -> r c d", r=GRID_H)
                for i in range(2):
                    eng.dma_start(by_row[2 * (t - 1) + i], x[GRID_W * i:GRID_W * (i + 1), t]).then_inc(s, 16)

        def store_tiles(eng, norm, h, hn, layer, s):
            for t in range(NT):
                eng.wait_ge(norm.hn, norm.c + t + 1)
                store_tile(eng, H, h, layer, t, s)
                store_tile(eng, norm.hnorm, hn, layer, t, s)

        def load_h(eng, s):
            for t in range(NT):
                c0, c1 = cols_of(t)
                eng.dma_start(H[0:rows_of(t), t], h_dram[c0:c1, :]).then_inc(s, 16)

        def load_x(eng, s):
            for t in range(NT):
                src = a["meta_tokens"] if t == 0 else a["x"][0, 128 * (t - 1):128 * t, :]
                eng.dma_start(H[0:rows_of(t), t], src).then_inc(s, 16)

        norms = [Norm(i, i) for i in range(4)]
        stored = [sem(f"stored{i}") for i in range(2)]
        even_in = EvenIn()
        gates = Gates(even_in.rows)
        mlstm, ret = MLSTM(gates), Retention()

        def even_mix(t, k):
            src = EVT["sgo"] if k < 4 else EVT["sgr"]
            return src[0:rows_of(t), t, 128 * (k % 4):128 * (k % 4) + 128]

        even_out = Project(0, even_mix, EVT["qk"], ar(0, 8 * T, k=8), 4, 8)
        odd_in, attn = OddIn(), Attention()
        odd_out = Project(1, lambda t, k: att[0:rows_of(t), t, 128 * k:128 * k + 128], ar(0, 8 * T, k=8),
                          ar(8 * T, 8 * T, k=8), None, 6)
        outs = [even_out, odd_out]
        block = ctx.enter_context(nc.Block())

        @block.sync
        def _(sp):
            stream_mixer(sp, 0, [block_of(a["even_w_in"], c) for c in even_cols]
                         + [block_of(a["even_w_out"], c) for c in (0, BLK)], norms[0].in_)
            stream_moe(sp, 0)
            stream_mixer(sp, 1, [block_of(a["odd_w_in"], BLK * j) for j in range(6)]
                         + [block_of(a["odd_w_out"], c) for c in (0, BLK)], norms[2].in_)
            stream_moe(sp, 1)

        @block.scalar
        def _(act):
            step = Chain(act, act_step)
            load_x(act, norms[0].in_)
            act.dma_start(ident[:, :], a["c_ident"][:, :]).then_inc(consts_in, 16)
            act.dma_start(minus_half, a["c_mhalf"][:, :]).then_inc(consts_in, 16)
            for i, (n, l) in enumerate([("attn_norm_g", 0), ("ffn_norm_g", 0), ("attn_norm_g", 1), ("ffn_norm_g", 1)]):
                act.dma_start(gcol[:, i], a[n][l].rearrange("(k p) -> p k", p=128),
                              allow_slow_non_contiguous=True).then_inc(consts_in, 16)
            for i, n in enumerate(("even_m_norm_g", "even_r_norm_g")):
                act.dma_start(gcol[:, 4, 4 * i:4 * i + 4], a[n].rearrange("(k p) -> p k", p=128),
                              allow_slow_non_contiguous=True).then_inc(consts_in, 16)
            for i, n in enumerate(("odd_q_norm_g", "odd_k_norm_g")):
                for j in range(2):
                    act.dma_start(gcol[AD * j:AD * j + AD, 5, i:i + 1], a[n].rearrange("(p o) -> p o", o=1),
                                  allow_slow_non_contiguous=True).then_inc(consts_in, 16)
            even_in.consts(act)
            act.dma_start(gates.logit, a["even_ret_decay_logit"].rearrange("d h -> (d h)").unsqueeze(0)
                          .broadcast_to([128, 8])).then_inc(gates.logit_in, 16)
            ex[0].consts(act)
            ex[1].consts(act)
            act.wait_ge(consts_in, 192)
            for layer in range(2):
                n_in, n_ffn = norms[2 * layer], norms[2 * layer + 1]
                if layer:
                    fenced(act)
                    load_h(act, n_in.in_)
                act.wait_ge(n_in.in_, 16 * NT)
                fenced(act)
                n_in.act(act, step)
                fenced(act)
                if layer == 0:
                    even_in.act(act, step)
                    fenced(act)
                    mlstm.consts(act)
                    gates.act(act, step)
                    fenced(act)
                    mlstm.act(act, step)
                    fenced(act)
                    ret.consts(act)
                    ret.act(act, step)
                    fenced(act)
                    outs[layer].turn_act(act)
                    fenced(act)
                    load_x(act, even_out.h_in)
                else:
                    odd_in.act(act, step)
                    fenced(act)
                    attn.act(act, step)
                    fenced(act)
                    outs[layer].turn_act(act)
                    fenced(act)
                    load_h(act, odd_out.h_in)
                outs[layer].act(act, n_ffn)
                store_tiles(act, n_ffn, ex[layer].resid, ex[layer].normed, layer, stored[layer])
                ex[layer].select_act(act)
                act.wait_ge(stored[layer], 32 * STORES[layer])
                fenced(act)
                ex[layer].high_part(act, 0, 0)
                ex[layer].high_part(act, 0, 1)
                ex[layer].x_high(act, 0)
                ex[layer].loop(act, ex[layer].act_body)

        @block.vector
        def _(dve):
            step = Chain(dve, dve_step)
            for layer in range(2):
                if layer:
                    fenced(dve)
                fenced(dve)
                norms[2 * layer].dve(dve, step)
                fenced(dve)
                if layer == 0:
                    even_in.dve(dve, step)
                    fenced(dve)
                    gates.dve(dve, step)
                    fenced(dve)
                    mlstm.dve(dve, step)
                    fenced(dve)
                    ret.dve(dve, step)
                else:
                    odd_in.dve(dve, step)
                    fenced(dve)
                    attn.dve(dve, step)
                fenced(dve)
                outs[layer].turn_dve(dve, step)
                fenced(dve)
                outs[layer].dve(dve, norms[2 * layer + 1])
                ex[layer].select_dve(dve, step)
                fenced(dve)
                ex[layer].xT_copy(dve, 0)
                ex[layer].x_low(dve, 0)
                ex[layer].low_part(dve, 0, 0)
                ex[layer].low_part(dve, 0, 1)
                ex[layer].loop(dve, ex[layer].dve_body)

        @block.gpsimd
        def _(pool):
            for layer in range(2):
                if layer:
                    fenced(pool)
                fenced(pool)
                norms[2 * layer].pool(pool)
                fenced(pool)
                if layer == 0:
                    fenced(pool)
                    fenced(pool)
                    mlstm.pool(pool)
                    fenced(pool)
                    ret.pool(pool)
                else:
                    odd_in.pool(pool)
                    fenced(pool)
                fenced(pool)
                fenced(pool)
                norms[2 * layer + 1].pool(pool)
                fenced(pool)
                ex[layer].gather(pool, 0, 1)
                ex[layer].loop(pool, ex[layer].pool_body)
                pool.wait_ge(ex[layer].scattered, 16 * NE)

        @block.tensor
        def _(pe):
            for layer in range(2):
                if layer:
                    fenced(pe)
                fenced(pe)
                norms[2 * layer].pe(pe)
                fenced(pe)
                if layer == 0:
                    even_in.pe(pe)
                    fenced(pe)
                    gates.pe(pe)
                    fenced(pe)
                    mlstm.pe(pe)
                    fenced(pe)
                    ret.pe(pe)
                else:
                    odd_in.pe(pe)
                    fenced(pe)
                    attn.pe(pe)
                fenced(pe)
                outs[layer].turn_pe(pe)
                fenced(pe)
                outs[layer].pe(pe, norms[2 * layer + 1])
                ex[layer].select_pe(pe)
                fenced(pe)
                ex[layer].turn_xs(pe, 0, 0)
                ex[layer].turn_xs(pe, 0, 1)
                ex[layer].loop(pe, ex[layer].pe_body)


def constants():
    f = np.float32
    c = {}
    c["c_ident"] = np.eye(128, dtype=f)
    c["c_mhalf"] = np.full((128, 1), -0.5, f)
    c["c_iota"] = np.broadcast_to(np.arange(1, CAP + 1, dtype=f), (128, CAP)).copy()
    p = np.arange(128)
    tok = np.zeros((2, 128, NT), f)
    tok[:, :, 0] = p
    for b in range(4):
        tok[0, :, b + 1] = NM + (p % GRID_W) * GRID_H + 2 * b + p // GRID_W
        tok[1, :, b + 1] = NM + 128 * b + p
    c["c_token"] = tok
    half = HD // 2
    inv = (f(10000.0) ** (-np.arange(half, dtype=f) / f(half))).astype(f)
    ang = np.arange(T, dtype=f)[:, None] * inv[None, :]
    cs = np.concatenate([np.cos(ang), np.sin(ang)], -1).astype(f)
    rope = np.zeros((128, NT, HD), f)
    rope[:NM, 0] = cs[:NM]
    rope[:, 1:] = cs[NM:].reshape(4, 128, HD).transpose(1, 0, 2)
    c["c_rope"] = rope
    k, q = p[:, None], p[None, :]
    c["c_mf"] = (q >= k).astype(f)
    c["c_mb"] = (q <= k).astype(f)
    c["c_far"] = np.stack([np.where(q >= k, 0, FAR), np.where(q <= k, 0, FAR)], 1).astype(f)
    c["c_sel"] = np.broadcast_to(np.eye(NH, dtype=f)[:, :, None], (NH, NH, 128)).copy()
    j = np.arange(NR)[None, :]
    c["c_df"] = np.maximum(j - k, 0).astype(f)
    c["c_db"] = np.maximum(k - (j - 384), 0).astype(f)
    m = np.arange(NM)[:, None]
    c["c_dm"] = np.stack([NM + j - m, T - 1 - j - m], 1).astype(f)
    return c


def bias_tiles(rpb):
    p = np.arange(128)
    c, r = p[:, None] // GRID_H, p[:, None] % GRID_H
    kk = np.arange(256)[None, :]
    parts = []
    for q0, k0 in ((0, 0), (16, 8), (48, 32)):
        qc, kc, kr = q0 + c, k0 + kk // GRID_H, kk % GRID_H
        start = np.clip(qc - 8, 0, GRID_W - 16)
        seen = (kc >= start) & (kc < start + 16)
        t = rpb[:, kr - r + 7, np.clip(kc - qc, -15, 15) + 15]
        t[:, ~seen] = -FAR
        parts += [np.zeros((AH, 128, NM), np.float32), t]
    return np.concatenate(parts, -1)


INPUTS = ["x", "meta_tokens", "attn_norm_g", "ffn_norm_g", "even_w_in", "even_conv_w", "even_gate_b",
          "even_m_norm_g", "even_ret_decay_logit", "even_r_norm_g", "even_w_out", "odd_w_in", "odd_q_norm_g",
          "odd_k_norm_g", "odd_w_out", "router_w", "expert_w_gate", "expert_w_up", "expert_w_down"]


def kernel(**inputs):
    from concourse import bacc
    from concourse.bass_utils import run_bass_kernel_spmd

    arrays = {n: np.ascontiguousarray(inputs[n]) for n in INPUTS}
    for n in ("even_w_in", "even_conv_w", "even_gate_b", "even_m_norm_g", "even_ret_decay_logit", "even_r_norm_g",
              "even_w_out", "odd_w_in", "odd_q_norm_g", "odd_k_norm_g", "odd_w_out"):
        arrays[n] = arrays[n][0]
    arrays["even_conv_w"] = np.ascontiguousarray(arrays["even_conv_w"].reshape(CONV, 2 * NH, 128).transpose(2, 1, 0))
    arrays["rpb_tiles"] = bias_tiles(np.asarray(inputs["odd_rpb"])[0])
    arrays |= constants()
    nc = bacc.Bacc("TRN2", target_bir_lowering=False, num_devices=1)
    a = {n: nc.dram_tensor(f"in_{n}", v.shape, mybir.dt.from_np(v.dtype), kind="ExternalInput").ap()
         for n, v in arrays.items()}
    out = nc.dram_tensor("out_h", (T, D), F32, kind="ExternalOutput").ap()
    trunk(nc, a, out)
    r = run_bass_kernel_spmd(nc, [{f"in_{n}": v for n, v in arrays.items()}], core_ids=[0])
    return r.results[0]["out_h"][NM:].reshape(GRID_W, GRID_H, D).transpose(1, 0, 2).reshape(1, NR, D)
```

```python
from contextlib import ExitStack

import numpy as np

import concourse.bass as bass
from concourse import mybir

ALU = mybir.AluOpType
ACT = mybir.ActivationFunctionType
AX = mybir.AxisListType
F32 = mybir.dt.float32
F32R = mybir.dt.float32r
U32 = mybir.dt.uint32

D = 1024
KB = D // 128
NM = 16
NR = 512
T = NM + NR
NT = 5
GRID_W, GRID_H = 64, 8
EPS = 1e-6
BLK = 512
SLOTS = 6
HD = 128
NH = 4
CONV = 5
AH, AD = 16, 64
NE = 16
CAP = 2 * T // NE
FAR = 1e30
HEAD_SCALE = float(HD) ** -0.5
ARENA = 22600
PADS = 6


def rows_of(t):
    return NM if t == 0 else 128


def cols_of(t):
    return (0, NM) if t == 0 else (NM + 128 * (t - 1), NM + 128 * t)


def trunk(nc, a, out):
    ctx = ExitStack()
    with ctx:
        def sb(name, shape, dt=F32):
            return ctx.enter_context(nc.sbuf_tensor(name, shape, dt))

        def sem(name):
            return ctx.enter_context(nc.semaphore(name))

        h_dram = nc.dram_tensor("h_mid", [T, D], F32, kind="Internal").ap()
        hn_dram = [nc.dram_tensor(f"h_normed{i}", [T, D], F32, kind="Internal").ap() for i in range(2)]

        SPACES = [("ring", [128, SLOTS, KB, BLK]),
                  ("small", [128, 1600]),
                  ("uT", [128, KB, T]),
                  ("arena", [128, ARENA])]
        with ExitStack() as first:
            ring_rounded = [first.enter_context(nc.sbuf_tensor(f"ring{i}_r", [128, KB, BLK], F32R)) for i in range(SLOTS)]
            rounded = {n: first.enter_context(nc.sbuf_tensor(n + "_r", shape, F32R)) for n, shape in SPACES[1:]}
        ring, small, uT, arena = (sb(n, shape) for n, shape in SPACES)
        ident = sb("ident", [128, 128])
        gcol = sb("gcol", [128, 6, KB])
        bank = [ctx.enter_context(nc.psum_tensor(f"bank{i}", [128, 512], F32)) for i in range(8)]

        minus_half = small[:, 1599:1600]
        H = arena[:, ARENA - NT * D:ARENA].rearrange("p (t d) -> p t d", t=NT)

        def ar(off, n, **kw):
            assert off + n <= ARENA, (off, n)
            v = arena[:, off:off + n]
            if kw:
                names = " ".join(kw)
                v = v.rearrange(f"p ({names} z) -> p {names} z", **kw)
            return v

        def sm(off, n, **kw):
            v = small[:, off:off + n]
            if kw:
                names = " ".join(kw)
                v = v.rearrange(f"p ({names} z) -> p {names} z", **kw)
            return v

        ring_in = [sem(f"ring_in{i}") for i in range(SLOTS)]
        ring_used = [sem(f"ring_used{i}") for i in range(SLOTS)]
        fence = sem("fence")
        consts_in = sem("consts_in")
        dve_step = sem("dve_step")
        act_step = sem("act_step")

        class Chain:

            def __init__(self, eng, s):
                self.eng, self.s, self.n = eng, s, 0

            def __call__(self, ins):
                self.n += 1
                ins.then_inc(self.s, 1)
                self.eng.wait_ge(self.s, self.n)

        fences = {}

        def fenced(eng):
            fences[eng] = fences.get(eng, 0) + 1
            eng.drain().then_inc(fence, 1)
            eng.wait_ge(fence, 4 * fences[eng])

        def high(x):
            if x.tensor.name != "ring":
                return bass.AP(rounded[x.tensor.name], x.offset, x.ap)
            slot, offset = divmod(x.offset, KB * BLK)
            return bass.AP(ring_rounded[slot], offset, [(KB * BLK, 128)] + list(x.ap[1:]))

        def part(x):
            return high(x).bitcast(F32)

        def product3(pe, ps, still, moving, ks, start, stop, order=((0, 0), (0, 1), (1, 0)), before_last=None):
            for i, (a_, b_) in enumerate(order):
                if i == 2 and before_last:
                    before_last()
                for k in ks:
                    first, last = i == 0 and k == ks[0], i == 2 and k == ks[-1]
                    ins = pe.matmul(ps, high(still[a_](k)), high(moving[b_](k)), start=start and first, stop=stop and last)
            return ins

        EVEN_UNITS, ODD_UNITS = 10, 8
        mixer_slots = [[m % 3 for m in range(EVEN_UNITS)], [(1, 2, 0)[m % 3] for m in range(ODD_UNITS)]]
        HIGH_SLOTS, TOKEN_SLOT = (3, 4), 5
        moe_slots = [[1, 5, 2, 0, 3, 4], [0, 5, 1, 2, 3, 4]]
        seen_in, seen_used = [0] * SLOTS, [0] * SLOTS
        mixer_units, moe_base = [], []
        for layer in range(2):
            units = []
            for m, s in enumerate(mixer_slots[layer]):
                units.append((s, seen_in[s], seen_used[s], HIGH_SLOTS[m % 2], seen_used[HIGH_SLOTS[m % 2]]))
                seen_in[s] += 1
                seen_used[s] += 1
                seen_used[HIGH_SLOTS[m % 2]] += 1
            mixer_units.append(units)
            seen_used[TOKEN_SLOT] += 1
            moe_base.append((list(seen_in), list(seen_used)))
            seen_in = [n + NE for n in seen_in]
            seen_used = [n + NE for n in seen_used]
        MOE_UNITS = 6
        even_cols = [0, 512, 1024, 1536, 2064, 2576, 3088, 3600]

        def block_of(w, c):
            return w[:, c:c + BLK].rearrange("(k p) c -> p k c", p=128)

        def stream_mixer(sp, layer, sources, tokens, tokens_count):
            for m, src in enumerate(sources):
                s, _, used, _, _ = mixer_units[layer][m]
                if used:
                    sp.wait_ge(ring_used[s], used)
                if m == layer:
                    sp.wait_ge(tokens, tokens_count)
                sp.dma_start(ring[:, s], src).then_inc(ring_in[s], 16)

        def stream_moe(sp, layer):
            names = ["expert_w_gate", "expert_w_up", "expert_w_gate", "expert_w_up", "expert_w_down", "expert_w_down"]
            half = [0, 0, 1, 1, 0, 1]
            with sp.Fori(0, NE) as e:
                for j in range(MOE_UNITS):
                    s = moe_slots[layer][j]
                    w = a[names[j]][layer].rearrange("e (k p) c -> e p k c", p=128)
                    sp.wait_ge(ring_used[s], e + moe_base[layer][1][s])
                    sp.dma_start(ring[:, s], w[bass.ds(e, 1), :, :, BLK * half[j]:BLK * (half[j] + 1)]
                                 .rearrange("e p k c -> p (e k) c")).then_inc(ring_in[s], 16)

        token_meta = sm(920, KB * NM, k=KB)

        class TokenHigh:

            def cols(self, c0, c1):
                return token_meta[:, :, c0:c1] if c0 < NM else ring[:, TOKEN_SLOT, :, c0 - NM:c1 - NM]

        uH = TokenHigh()

        class Halves:
            hi, lo = sem("block_high"), sem("block_low")

            def __init__(self, layer):
                self.l, self.before = layer, EVEN_UNITS * layer

            def act(self, act, m):
                s, fills, _, h, used = mixer_units[self.l][m]
                act.wait_ge(ring_in[s], 16 * (fills + 1))
                if used:
                    act.wait_ge(ring_used[h], used)
                act.activation(high(ring[:, h]), ring[:, s], ACT.Copy).then_inc(self.hi, 1)

            def low(self, eng, m):
                s, _, _, h, _ = mixer_units[self.l][m]
                eng.wait_ge(self.hi, self.before + m + 1)
                eng.tensor_tensor(high(ring[:, s]), ring[:, s], part(ring[:, h]), ALU.subtract).then_inc(self.lo, 1)

            def ready(self, pe, m):
                pe.wait_ge(self.lo, self.before + m + 1)

            def weights(self, m, c0=0, c1=BLK):
                s, _, _, h, _ = mixer_units[self.l][m]
                return (lambda k: ring[:, h, k, c0:c1]), (lambda k: ring[:, s, k, c0:c1])

            def used(self, pe, m):
                s, _, _, h, _ = mixer_units[self.l][m]
                pe.sem_inc(ring_used[s], 1)
                pe.sem_inc(ring_used[h], 1)

        def tokens(c0, c1):
            return (lambda k: uH.cols(c0, c1)[:, k]), (lambda k: uT[:, k, c0:c1])

        halves = [Halves(i) for i in range(2)]

        STORES = [1 + 2 * (NT - 1), NT]

        POOL_LOWS, DVE_LOWS = (1, 2), (0, 3, 4)

        class Norm:
            sq, ms, rs, hn, tr, ev, hi = (sem("n_" + x) for x in ("squares", "mean", "rstd", "normed", "turned", "uT", "uT_high"))

            def __init__(self, k, gain):
                self.c, self.gain = NT * k, gain
                self.in_ = sem(f"n{k}_h_in")
                self.ss = small[:, 0:5]
                self.mean = small[:, 5:10]
                self.rstd = small[:, 10:15]
                self.hnorm = ar(8916, NT * D, t=NT)
                self.junk = ar(8916 + NT * D, D)

            def act_tile(self, act, t):
                n = rows_of(t)
                if t:
                    act.wait_ge(self.sq, self.c + t)
                act.activation(self.junk[0:n], H[0:n, t], ACT.Square,
                               accum_out=self.ss[0:n, t:t + 1]).then_inc(self.sq, 1)

            def dve_mean(self, dve, t):
                n = rows_of(t)
                dve.wait_ge(self.sq, self.c + t + 1)
                dve.tensor_scalar(self.mean[0:n, t:t + 1], self.ss[0:n, t:t + 1], 1.0 / D, EPS,
                                  ALU.mult, ALU.add).then_inc(self.ms, 1)

            def dve_scale(self, dve, t):
                n = rows_of(t)
                dve.wait_ge(self.rs, self.c + t + 1)
                dve.tensor_scalar(self.hnorm[0:n, t], H[0:n, t], self.rstd[0:n, t:t + 1], None,
                                  ALU.mult).then_inc(self.hn, 1)

            def dve_uT(self, dve, t):
                n = rows_of(t)
                c0, c1 = cols_of(t)
                for g in range(2):
                    dve.wait_ge(self.tr, 2 * self.c + 2 * t + g + 1)
                    ps = bank[4 + (2 * t + g) % 4][:, 0:4 * n].rearrange("p (k c) -> p k c", k=4)
                    dve.tensor_tensor(uT[:, 4 * g:4 * g + 4, c0:c1], ps,
                                      gcol[:, self.gain, 4 * g:4 * g + 4].unsqueeze(2).broadcast_to([128, 4, n]),
                                      ALU.mult).then_inc(self.ev, 1)

            def pool_tile(self, pool, t):
                n = rows_of(t)
                pool.wait_ge(self.ms, self.c + t + 1)
                pool.tensor_tensor(self.rstd[0:n, t:t + 1], self.mean[0:n, t:t + 1], minus_half[0:n, 0:1],
                                   ALU.pow).then_inc(self.rs, 1)

            def pe_tile(self, pe, t):
                n = rows_of(t)
                pe.wait_ge(self.hn, self.c + t + 1)
                for g in range(2):
                    i = 2 * t + g
                    if i >= 4:
                        pe.wait_ge(self.ev, 2 * self.c + i - 3)
                    for k in range(4):
                        ins = pe.transpose(bank[4 + i % 4][:, k * n:(k + 1) * n],
                                           self.hnorm[0:n, t, (4 * g + k) * 128:(4 * g + k + 1) * 128],
                                           ident[0:n, 0:n])
                    ins.then_inc(self.tr, 1)

            def act(self, act, step, h_in=0):
                for t in range(NT):
                    self.act_tile(act, t)
                for t in range(NT):
                    c0, c1 = cols_of(t)
                    act.wait_ge(self.ev, 2 * (self.c + t + 1))
                    act.activation(high(uH.cols(c0, c1)), uT[:, :, c0:c1], ACT.Copy).then_inc(self.hi, 1)

            def low(self, eng, t):
                c0, c1 = cols_of(t)
                eng.wait_ge(self.hi, self.c // 2 + t + 1)
                eng.tensor_tensor(high(uT[:, :, c0:c1]), uT[:, :, c0:c1], part(uH.cols(c0, c1)), ALU.subtract)

            def dve(self, dve, step):
                self.dve_mean(dve, 0)
                for t in range(NT):
                    if t + 1 < NT:
                        self.dve_mean(dve, t + 1)
                    self.dve_scale(dve, t)
                    if t:
                        self.dve_uT(dve, t - 1)
                self.dve_uT(dve, NT - 1)
                for t in DVE_LOWS:
                    self.low(dve, t)

            def pool(self, pool, low=False):
                for t in range(NT):
                    self.pool_tile(pool, t)
                if low:
                    for t in POOL_LOWS:
                        self.low(pool, t)

            def pe(self, pe):
                for t in range(NT):
                    self.pe_tile(pe, t)

        class Experts:
            consts_in, logits, sub, exp, aff_ready, affT, pos, posT_done, onehot, picked, chosen = (
                sem("sel_" + x) for x in ("consts_in", "logits", "sub", "exp", "aff_ready", "affT", "pos", "posT_done",
                                          "onehot", "picked", "chosen"))
            sent = sem("moe_sent")
            w_hi, w_lo, x_hi, x_lo, h_hi, h_lo = (sem("moe_" + x) for x in ("w_high", "w_low", "x_high", "x_low", "h_high", "h_low"))
            idx_g, idx_s, gathered, scattered, xs_turned, xT_in, silu, hidden0, hidden1, h_turned, y = (
                sem("moe_" + x) for x in ("idx_g", "idx_s", "gathered", "scattered", "xs_turned", "xT_in", "silu",
                                          "hidden0", "hidden1", "h_turned", "y"))
            hidden = [hidden0, hidden1]
            HIGH_OF = [0, 1, 2, 0, 3, 2]
            BEFORE = [(3, 0), (1, 0), (5, 0), (0, 1), (4, 0), (2, 1)]

            def __init__(self, layer, gain, normed, resid):
                self.l, self.gain, self.normed, self.resid = layer, gain, normed, resid
                self.once = layer + 1
                self.wr = sm(1056 + 128 * layer, KB * NE, k=KB)
                self.iota = sm(1312, CAP)
                self.tok = sm(1378 + NT * layer, NT)
                self.P = ar(0, NT * NE * CAP, t=NT, e=NE)
                self.aff = ar(5280, NT * NE, t=NT)
                self.a4 = ar(5360, NT * NE * 4, t=NT, e=NE)
                self.stat = ar(5680, 20)
                self.m8 = ar(5700, 8)[0:NE]
                self.posT = ar(5708, NT * NE, t=NT)
                self.work = ar(5788, PADS + T)[0:NE]
                self.mask = ar(6322, T)[0:NE]
                self.cum = ar(6850, T)[0:NE]
                self.pick = ar(7378, T)[0:NE]
                self.ones = ar(7906, T)[0:NE]
                self.idx = sm(1388, NE).bitcast(U32)[0:CAP]
                self.gate = sm(1404, NE)[0:CAP]
                self.idxg = sm(1420, 1).bitcast(U32)[0:CAP]
                self.idxs = sm(1421, 1).bitcast(U32)[0:CAP]
                self.xs = ar(0, D)[0:CAP]
                self.sg = ar(1024, D)[0:CAP]
                self.hid = ar(2048, D)[0:CAP]
                self.y_sb = ar(3072, D)[0:CAP]
                self.xT, self.xTh, self.hTh, self.hTl = (ar(4096 + i * KB * CAP, KB * CAP, k=KB) for i in range(4))
                self.wh = [ar(4096 + 4 * KB * CAP + i * KB * BLK, KB * BLK, k=KB) for i in (2, 1, 3, 0)]

            def consts(self, act):
                act.dma_start(self.wr, a["router_w"][self.l].rearrange("(k p) e -> p k e", p=128)).then_inc(self.consts_in, 16)
                act.dma_start(self.tok, a["c_token"][self.l]).then_inc(self.consts_in, 16)
                if self.l == 0:
                    act.dma_start(self.iota, a["c_iota"][:, :]).then_inc(self.consts_in, 16)

            VIEWS = [(NM, 0, 1), (128, 1, NT)]

            def route(self, pe, tiles):
                if 0 in tiles:
                    pe.wait_ge(self.consts_in, 80)
                    pe.wait_ge(outs[self.l].added, 2 * NT * self.once - 1)
                for t in tiles:
                    n = rows_of(t)
                    c0, c1 = cols_of(t)
                    pe.wait_ge(Norm.ev, 2 * NT * (2 * self.l + 1) + 2 * t + 2)
                    for k in range(KB):
                        ins = pe.matmul(bank[0][0:n, t * NE:(t + 1) * NE], uT[:, k, c0:c1], self.wr[:, k],
                                        start=(k == 0), stop=(k == KB - 1))
                if NT - 1 in tiles:
                    ins.then_inc(self.logits, 1)

            def select_pe(self, pe):
                pe.wait_ge(outs[self.l].added, 2 * NT * self.once)
                pe.wait_ge(self.aff_ready, self.once)
                for t in range(NT):
                    n = rows_of(t)
                    ps = bank[1][0:NE, 0:NM] if t == 0 else bank[2][0:NE, 128 * (t - 1):128 * t]
                    ins = pe.transpose(ps, self.aff[0:n, t], ident[0:n, 0:n])
                ins.then_inc(self.affT, 1)
                pe.wait_ge(self.pos, self.once)
                for t in range(NT):
                    n = rows_of(t)
                    c0, c1 = cols_of(t)
                    ins = pe.transpose(bank[3][0:n, t * NE:(t + 1) * NE], self.pick[:, c0:c1], ident[0:NE, 0:NE])
                ins.then_inc(self.posT_done, 1)
                for e in range(NE):
                    if e % 4 == 0:
                        pe.wait_ge(self.onehot, 4 * self.l + e // 4 + 1)
                    for t in range(NT):
                        ins = pe.matmul(bank[4][0:CAP, 4 * e:4 * e + 4], high(self.P[:, t, e]), high(self.a4[:, t, e]),
                                        start=(t == 0), stop=(t == NT - 1))
                ins.then_inc(self.picked, 1)

            def select_act(self, act):
                act.wait_ge(self.sub, self.once)
                for n, t0, t1 in self.VIEWS:
                    ins = act.activation(self.aff[0:n, t0:t1], self.aff[0:n, t0:t1], ACT.Exp)
                    ins.then_inc(self.exp, 1)

            def select_dve(self, dve, step):
                dve.wait_ge(self.consts_in, 80)
                dve.wait_ge(self.logits, self.once)
                lg = bank[0][:, 0:NT * NE].rearrange("p (t e) -> p t e", t=NT)
                for n, t0, t1 in self.VIEWS:
                    w = t1 - t0
                    step(dve.tensor_reduce(self.stat[0:n, t0:t1], lg[0:n, t0:t1], AX.X, ALU.max))
                    ins = dve.tensor_tensor(self.aff[0:n, t0:t1], lg[0:n, t0:t1],
                                            self.stat[0:n, t0:t1].unsqueeze(2).broadcast_to([n, w, NE]), ALU.subtract)
                    if t0:
                        ins.then_inc(self.sub, 1)
                    else:
                        step(ins)
                dve.memset(self.ones, 1.0)
                dve.memset(self.work[:, 0:PADS], 2.0)
                step(dve.tensor_scalar(high(self.a4[:, 0].rearrange("p e x -> p (e x)")),
                                       self.tok[:, 0:1].broadcast_to([128, 4 * NE]), 0.0, None, ALU.mult))
                step(dve.tensor_scalar(high(self.a4[:, 1:NT, :, 3]), self.tok[:, 1:NT].unsqueeze(2).broadcast_to([128, NT - 1, NE]),
                                       0.0, None, ALU.mult))
                step(dve.memset(self.posT[:, 0], 0.0))
                step(dve.tensor_copy(high(self.a4[:, :, :, 0]), self.tok.unsqueeze(2).broadcast_to([128, NT, NE])))
                dve.wait_ge(self.exp, 2 * self.once)
                for n, t0, t1 in self.VIEWS:
                    w = t1 - t0
                    step(dve.tensor_reduce(self.stat[0:n, 5 + t0:5 + t1], self.aff[0:n, t0:t1], AX.X, ALU.add))
                    step(dve.reciprocal(self.stat[0:n, 10 + t0:10 + t1], self.stat[0:n, 5 + t0:5 + t1]))
                    step(dve.tensor_tensor(self.aff[0:n, t0:t1], self.aff[0:n, t0:t1],
                                           self.stat[0:n, 10 + t0:10 + t1].unsqueeze(2).broadcast_to([n, w, NE]),
                                           ALU.mult))
                    a = self.aff[0:n, t0:t1]
                    ins = dve.tensor_copy(high(self.a4[0:n, t0:t1, :, 1]), a)
                    if t0:
                        ins.then_inc(self.aff_ready, 1)
                        dve.wait_ge(self.aff_ready, self.once)
                    else:
                        step(ins)
                    step(dve.tensor_tensor(high(self.a4[0:n, t0:t1, :, 2]), a, part(self.a4[0:n, t0:t1, :, 1]),
                                           ALU.subtract))
                dve.wait_ge(self.affT, self.once)
                step(dve.tensor_copy(self.work[:, PADS:PADS + NM], bank[1][0:NE, 0:NM]))
                grid = self.work[:, PADS + NM:]
                src = bank[2][0:NE, :]
                if self.l:
                    for b in range(4):
                        src_b = src[:, 128 * b:128 * b + 128].rearrange("p (c r) -> p r c", r=GRID_H)
                        step(dve.tensor_copy(grid.rearrange("p (r c) -> p r c", r=GRID_H)[:, :, 16 * b:16 * b + 16], src_b))
                else:
                    step(dve.tensor_copy(grid, src))
                for r in range((PADS + CAP) // 8):
                    step(dve.max(self.m8, self.work))
                    step(dve.match_replace(self.work, self.m8, self.work, -1.0))
                step(dve.tensor_scalar(self.mask, self.work[:, PADS:], 0.0, None, ALU.is_lt))
                step(dve.tensor_tensor_scan(self.cum, self.ones, self.mask, 0.0, ALU.mult, ALU.add))
                step(dve.tensor_tensor(self.pick[:, 0:NM], self.cum[:, 0:NM], self.mask[:, 0:NM], ALU.mult))
                if self.l:
                    for b in range(4):
                        cut = lambda x: x[:, NM:].rearrange("p (r c) -> p c r", r=GRID_H)[:, 16 * b:16 * b + 16, :]
                        dst = self.pick[:, NM + 128 * b:NM + 128 * b + 128].rearrange("p (c r) -> p c r", r=GRID_H)
                        ins = dve.tensor_tensor(dst, cut(self.cum), cut(self.mask), ALU.mult)
                        if b < 3:
                            step(ins)
                else:
                    ins = dve.tensor_tensor(self.pick[:, NM:], self.cum[:, NM:], self.mask[:, NM:], ALU.mult)
                ins.then_inc(self.pos, 1)
                dve.wait_ge(self.posT_done, self.once)
                pt = bank[3][:, 0:NT * NE].rearrange("p (t e) -> p t e", t=NT)
                step(dve.tensor_copy(self.posT[0:NM, 0], pt[0:NM, 0]))
                step(dve.tensor_copy(self.posT[:, 1:NT], pt[:, 1:NT]))
                for g in range(0, NE, 4):
                    for t in range(NT):
                        ins = dve.tensor_tensor(high(self.P[:, t, g:g + 4]), self.posT[:, t, g:g + 4].unsqueeze(2).broadcast_to([128, 4, CAP]),
                                                self.iota.unsqueeze(1).broadcast_to([128, 4, CAP]), ALU.is_equal)
                    ins.then_inc(self.onehot, 1)
                self.low_part(dve, 0, 0)
                dve.wait_ge(self.picked, self.once)
                ps = bank[4][0:CAP, 0:4 * NE].rearrange("p (e x) -> p e x", x=4)
                step(dve.tensor_copy(self.idx, ps[:, :, 0]))
                step(dve.tensor_copy(self.gate, ps[:, :, 1]))
                dve.tensor_tensor(self.gate, self.gate, ps[:, :, 2], ALU.add).then_inc(self.chosen, 1)

            def loop(self, eng, body):
                body(eng, 0, False)
                with eng.Fori(1, NE - 1) as e:
                    body(eng, e, False)
                body(eng, NE - 1, True)

            def freed(self, eng, s, e, per_expert, i=0):
                if self.l or i or not (isinstance(e, int) and e == 0):
                    eng.wait_ge(s, self.nth(e, per_expert, i))

            def units(self, j):
                s = moe_slots[self.l][j]
                return s, moe_base[self.l][0][s], moe_base[self.l][1][s]

            def turn_xs(self, pe, e, half):
                pe.wait_ge(self.gathered, self.nth(e, 16, 16))
                self.freed(pe, self.xT_in, e, 2, half)
                for k in range(4):
                    c = 128 * (4 * half + k)
                    ins = pe.transpose(bank[7][:, k * CAP:(k + 1) * CAP], self.xs[:, c:c + 128], ident[0:CAP, 0:CAP])
                ins.then_inc(self.xs_turned, 1)

            def nth(self, e, per_expert, i):
                return e * per_expert + (self.l * NE * per_expert + i)

            def pe_body(self, pe, e, last):
                def weights(j):
                    s, _, _ = self.units(j)
                    return (lambda k: self.wh[self.HIGH_OF[j]][:, k]), (lambda k: ring[:, s, k])

                x = (lambda k: self.xTh[:, k]), (lambda k: self.xT[:, k])
                hid = (lambda k: self.hTh[:, k]), (lambda k: self.hTl[:, k])

                def product(b, lhs, j, ks=range(KB)):
                    pe.wait_ge(self.w_hi, self.nth(e, MOE_UNITS, j + 1))
                    low = lambda: pe.wait_ge(self.w_lo, self.nth(e, MOE_UNITS, j + 1))
                    return product3(pe, bank[b][0:CAP, :], lhs, weights(j), ks, ks[0] == 0, ks[-1] == KB - 1,
                                    order=((0, 0), (1, 0), (0, 1)), before_last=low)

                def used(j):
                    return ring_used[self.units(j)[0]]

                def turn_hidden(half):
                    pe.wait_ge(self.hidden[half], self.nth(e, 1, 1))
                    self.freed(pe, self.h_lo, e, 2, half)
                    for k in range(4):
                        ins = pe.transpose(bank[6][:, k * CAP:(k + 1) * CAP],
                                           self.hid[:, half * BLK + 128 * k:half * BLK + 128 * k + 128],
                                           ident[0:CAP, 0:CAP])
                    ins.then_inc(self.h_turned, 1)

                pe.wait_ge(self.x_lo, self.nth(e, 2, 2))
                self.freed(pe, self.hidden[0], e, 1)
                product(0, x, 0).then_inc(used(0), 1)
                product(1, x, 1).then_inc(used(1), 1)
                self.freed(pe, self.hidden[1], e, 1)
                product(2, x, 2).then_inc(used(2), 1)
                turn_hidden(0)
                product(3, x, 3).then_inc(used(3), 1)
                pe.wait_ge(self.h_lo, self.nth(e, 2, 1))
                self.freed(pe, self.y, e, 2)
                product(4, hid, 4, range(4))
                turn_hidden(1)
                if not last:
                    self.turn_xs(pe, e + 1, 0)
                product(5, hid, 5, range(4))
                if not last:
                    self.turn_xs(pe, e + 1, 1)
                pe.wait_ge(self.h_lo, self.nth(e, 2, 2))
                product(4, hid, 4, range(4, KB)).then_inc(used(4), 1)
                product(5, hid, 5, range(4, KB)).then_inc(used(5), 1)

            def high_part(self, act, e, j):
                s, fills, _ = self.units(j)
                other, same = self.BEFORE[j]
                act.wait_ge(ring_in[s], (e + fills + 1) * 16)
                s2, _, uses = self.units(other)
                act.wait_ge(ring_used[s2], e + uses + same)
                act.activation(high(self.wh[self.HIGH_OF[j]]), ring[:, s], ACT.Copy).then_inc(self.w_hi, 1)

            def low_part(self, dve, e, j):
                s, _, _ = self.units(j)
                dve.wait_ge(self.w_hi, self.nth(e, MOE_UNITS, j + 1))
                dve.tensor_tensor(high(ring[:, s]), ring[:, s], part(self.wh[self.HIGH_OF[j]]),
                                  ALU.subtract).then_inc(self.w_lo, 1)

            def x_high(self, act, e, halves_=range(2)):
                for half in halves_:
                    act.wait_ge(self.xT_in, self.nth(e, 2, half + 1))
                    act.activation(high(self.xTh[:, 4 * half:4 * half + 4]), self.xT[:, 4 * half:4 * half + 4],
                                   ACT.Copy).then_inc(self.x_hi, 1)

            def x_low(self, dve, e, halves_=range(2)):
                for half in halves_:
                    x, xh = self.xT[:, 4 * half:4 * half + 4], self.xTh[:, 4 * half:4 * half + 4]
                    dve.wait_ge(self.x_hi, self.nth(e, 2, half + 1))
                    dve.tensor_tensor(high(x), x, part(xh), ALU.subtract).then_inc(self.x_lo, 1)

            def act_body(self, act, e, last):
                def silu(half):
                    s, _, n = self.units(2 * half)
                    act.wait_ge(ring_used[s], e + n + 1)
                    self.freed(act, self.hidden[half], e, 1)
                    act.activation(self.sg[:, half * BLK:half * BLK + BLK], bank[2 * half][0:CAP, :],
                                   ACT.Silu).then_inc(self.silu, 1)

                def hidden_high(half):
                    act.wait_ge(self.h_turned, self.nth(e, 2, half + 1))
                    act.activation(high(self.hTh[:, 4 * half:4 * half + 4]),
                                   bank[6][:, 0:4 * CAP].rearrange("p (k c) -> p k c", k=4),
                                   ACT.Copy).then_inc(self.h_hi, 1)

                self.high_part(act, e, 2)
                silu(0)
                self.high_part(act, e, 3)
                self.high_part(act, e, 4)
                silu(1)
                hidden_high(0)
                self.high_part(act, e, 5)
                if not last:
                    self.high_part(act, e + 1, 0)
                hidden_high(1)
                if not last:
                    self.x_high(act, e + 1, [0])
                    self.high_part(act, e + 1, 1)
                    self.x_high(act, e + 1, [1])

            def xT_copy(self, dve, e, halves_=range(2)):
                for half in halves_:
                    dve.wait_ge(self.xs_turned, self.nth(e, 2, half + 1))
                    g = gcol[:, self.gain, 4 * half:4 * half + 4]
                    dve.tensor_tensor(self.xT[:, 4 * half:4 * half + 4],
                                      bank[7][:, 0:4 * CAP].rearrange("p (k c) -> p k c", k=4),
                                      g.unsqueeze(2).broadcast_to([128, 4, CAP]), ALU.mult).then_inc(self.xT_in, 1)

            def dve_body(self, dve, e, last):
                def hidden_values(half):
                    s, _, n = self.units(2 * half + 1)
                    dve.wait_ge(ring_used[s], e + n + 1)
                    dve.wait_ge(self.silu, self.nth(e, 2, half + 1))
                    dve.tensor_tensor(self.hid[:, half * BLK:half * BLK + BLK], self.sg[:, half * BLK:half * BLK + BLK],
                                      bank[2 * half + 1][0:CAP, :], ALU.mult).then_inc(self.hidden[half], 1)

                def hidden_low(half):
                    dve.wait_ge(self.h_hi, self.nth(e, 2, half + 1))
                    dve.tensor_tensor(high(self.hTl[:, 4 * half:4 * half + 4]),
                                      bank[6][:, 0:4 * CAP].rearrange("p (k c) -> p k c", k=4),
                                      part(self.hTh[:, 4 * half:4 * half + 4]), ALU.subtract).then_inc(self.h_lo, 1)

                self.low_part(dve, e, 2)
                self.low_part(dve, e, 3)
                hidden_values(0)
                self.low_part(dve, e, 4)
                hidden_low(0)
                self.low_part(dve, e, 5)
                hidden_values(1)
                hidden_low(1)
                if not last:
                    self.xT_copy(dve, e + 1, [0])
                    self.low_part(dve, e + 1, 0)
                    self.xT_copy(dve, e + 1, [1])
                    self.x_low(dve, e + 1)
                self.freed(dve, self.scattered, e, 16)
                for half in range(2):
                    if not last and half:
                        self.low_part(dve, e + 1, 1)
                    s, _, n = self.units(4 + half)
                    dve.wait_ge(ring_used[s], e + n + 1)
                    dve.tensor_scalar(self.y_sb[:, half * BLK:half * BLK + BLK], bank[4 + half][0:CAP, :],
                                      self.gate[:, bass.ds(e, 1)], None, ALU.mult).then_inc(self.y, 1)

            def gather(self, pool, e):
                pool.tensor_copy(self.idxg, self.idx[:, bass.ds(e, 1)]).then_inc(self.idx_g, 1)
                pool.wait_ge(self.idx_g, self.nth(e, 1, 1))
                pool.sem_inc(self.sent, 1)
                pool.indirect_dma_start(out=self.xs, out_offset=None, in_=self.normed,
                                        in_offset=bass.IndirectOffsetOnAxis(ap=self.idxg, axis=0)).then_inc(self.gathered, 16)

            def pool_body(self, pool, e, last):
                if not last:
                    pool.wait_ge(self.xs_turned, self.nth(e, 2, 2))
                    self.gather(pool, e + 1)
                self.freed(pool, self.scattered, e, 16)
                pool.tensor_copy(self.idxs, self.idx[:, bass.ds(e, 1)]).then_inc(self.idx_s, 1)
                pool.wait_ge(self.idx_s, self.nth(e, 1, 1))
                pool.wait_ge(self.y, self.nth(e, 2, 2))
                pool.sem_inc(self.sent, 1)
                pool.indirect_dma_start(out=self.resid, out_offset=bass.IndirectOffsetOnAxis(ap=self.idxs, axis=0),
                                        in_=self.y_sb, in_offset=None, compute_op=ALU.add).then_inc(self.scattered, 16)

        ex = []
        for layer in range(2):
            x = Experts(layer, 1 + 2 * layer, hn_dram[layer], h_dram if layer == 0 else out)
            ex.append(x)

        EV, at = {}, 0
        for nm, n in (("rows", 4 * T), ("v1", NT * NH * (HD + 1)), ("qk", 8 * T), ("rqk", 8 * T),
                      ("sgo", NT * BLK), ("sgr", NT * BLK), ("rv", NT * BLK), ("tmp", 1780)):
            EV[nm] = at
            at += n
        EVT = {"v1": ar(EV["v1"], NT * NH * (HD + 1), t=NT, h=NH), "qk": ar(EV["qk"], 8 * T, k=8),
               "rqk": ar(EV["rqk"], 8 * T, k=8), "sgo": ar(EV["sgo"], NT * BLK, t=NT),
               "sgr": ar(EV["sgr"], NT * BLK, t=NT), "rv": ar(EV["rv"], NT * BLK, t=NT)}
        lgam = sm(1516, 8)
        uflat = uT[:, :, :].rearrange("p k t -> p (k t)")

        class EvenIn:
            ORDER = ["mq", "mk", "mv", "mo", "rq", "rk", "rv", "rg"]

            def __init__(self):
                (self.consts_in, self.product, self.taken, self.raw, self.conv, self.wg_high, self.wg_low, self.gate_product,
                 self.gate_copied, self.rows_in, self.meta_product, self.meta_copied, self.meta_turned, self.rope,
                 self.turned, self.turned_taken, self.pad) = (
                    sem("ei_" + x) for x in ("consts_in", "product", "taken", "raw", "conv", "wg_high", "wg_low",
                    "gate_product", "gate_copied", "rows_in", "meta_product", "meta_copied", "meta_turned", "rope",
                    "turned", "turned_taken", "pad"))
                self.convw = sm(20, 2 * NH * CONV, f=2 * NH)
                self.wg = sm(60, KB * 16, k=KB)
                self.wg_h = ar(EV["sgr"], KB * 16, k=KB)
                self.gates = ar(EV["sgr"] + KB * 16, T)[0:16]
                self.meta = ar(EV["sgr"] + KB * 16 + T, BLK)[0:NM]
                self.rows = [ar(EV["rows"] + i * T, T)[0:NH] for i in range(4)]
                self.gb = sm(268, 1)[0:16]
                self.rawbuf = [ar(EV["tmp"] + i * (T + 4), T + 4) for i in range(2)]
                self.rope_a, self.rope_b, self.rope_o = (ar(EV["sgr"] + i * BLK, BLK) for i in range(3))
                self.cs = sm(280, NT * 128, t=NT)
                self.groups = []
                for u in range(8):
                    n = 4 if u < 2 else NT
                    self.groups += [(u, i) for i in range(n)]

            def consts(self, act):
                act.dma_start(self.convw, a["even_conv_w"][:, :, :]).then_inc(self.consts_in, 16)
                act.dma_start(self.wg, a["even_w_in"][:, 2048:2064].rearrange("(k p) c -> p k c", p=128)).then_inc(self.consts_in, 16)
                act.dma_start(self.gb, a["even_gate_b"].rearrange("(c o) -> c o", o=1),
                              allow_slow_non_contiguous=True).then_inc(self.consts_in, 16)
                act.dma_start(self.cs, a["c_rope"][:, :, :]).then_inc(self.consts_in, 16)

            def pe(self, pe, gates):
                pe.wait_ge(self.wg_low, 1)
                wg = (lambda k: self.wg_h[:, k]), (lambda k: self.wg[:, k])
                product3(pe, bank[6][0:16, :], wg, tokens(NM, T), range(KB), True, True)
                product3(pe, bank[7][0:16, 0:NM], wg, tokens(0, NM), range(KB), True, True).then_inc(self.gate_product, 1)
                turn = 0
                for g, (u, i) in enumerate(self.groups):
                    if i == 0:
                        halves[0].ready(pe, u)
                    if (u, i) == (3, 3):
                        gates.pe(pe)
                    if g >= 4:
                        pe.wait_ge(self.taken, g - 3)
                    b = bank[g % 4]
                    if u < 2:
                        if i == 0:
                            product3(pe, bank[4][0:NM, :], tokens(0, NM), halves[0].weights(u), range(KB), True,
                                     True).then_inc(self.meta_product, 1)
                        w = halves[0].weights(u, 128 * i, 128 * i + 128)
                        ins = product3(pe, b[:, :], w, tokens(NM, T), range(KB), True, True)
                        if i == 0:
                            pe.wait_ge(self.meta_copied, u + 1)
                            if u:
                                pe.wait_ge(self.taken, 4)
                            for f in range(4):
                                turn_ = pe.transpose(bank[5][:, NM * f:NM * f + NM], self.meta[:, 128 * f:128 * f + 128],
                                                     ident[0:NM, 0:NM])
                            turn_.then_inc(self.meta_turned, 1)
                    else:
                        c0, c1 = cols_of(i)
                        ins = product3(pe, b[0:rows_of(i), :], tokens(c0, c1), halves[0].weights(u), range(KB), True, True)
                    ins.then_inc(self.product, 1)
                    for u2, i2 in ([self.groups[g - 1]] if self.groups[g - 1][0] in (4, 5) and g else []):
                        n = rows_of(i2)
                        if turn == 0:
                            pe.wait_ge(self.gate_copied, 1)
                        pe.wait_ge(self.rope, turn + 1)
                        if turn >= 2:
                            pe.wait_ge(self.turned_taken, turn - 1)
                        for h in range(NH):
                            ins2 = pe.transpose(bank[6 + turn % 2][:, h * n:(h + 1) * n],
                                                self.rope_o[0:n, 128 * h:128 * h + 128], ident[0:n, 0:n])
                        ins2.then_inc(self.turned, 1)
                        turn += 1
                    if i == (3 if u < 2 else NT - 1):
                        pe.wait_ge(self.product, g + 1)
                        halves[0].used(pe, u)
                pe.sem_inc(ring_used[TOKEN_SLOT], 1)

            def act(self, act, step, gates):
                act.wait_ge(self.consts_in, 64)
                act.activation(high(self.wg_h), self.wg, ACT.Copy).then_inc(self.wg_high, 1)
                halves[0].act(act, 0)
                act.wait_ge(self.gate_copied, 1)
                for i in range(4):
                    act.dma_start(self.rows[i], self.gates[NH * i:NH * i + NH]).then_inc(self.rows_in, 16)
                for g, (u, i) in enumerate(self.groups):
                    n = rows_of(i)
                    b = bank[g % 4]
                    if i == 1:
                        halves[0].act(act, u + 1)
                    if (u, i) == (2, 2):
                        gates.act_decay(act, step)
                    if (u, i) == (3, 1):
                        gates.act_maxima(act)
                    if (u, i) == (6, 0):
                        act.wait_ge(self.taken, g)
                        mlstm.consts(act)
                    if u < 2:
                        f = 4 * u + i
                        if i == 0:
                            act.wait_ge(self.meta_product, u + 1)
                            if u:
                                act.wait_ge(self.meta_turned, u)
                            act.activation(self.meta, bank[4][0:NM, :], ACT.Copy).then_inc(self.meta_copied, 1)
                        act.wait_ge(self.meta_turned, u + 1)
                        act.wait_ge(self.product, g + 1)
                        if f >= 2:
                            act.wait_ge(self.conv, f - 1)
                        else:
                            act.wait_ge(self.pad, 1)
                        step(act.activation(self.rawbuf[f % 2][:, 2:2 + NM], bank[5][:, NM * i:NM * i + NM], ACT.Copy))
                        act.activation(self.rawbuf[f % 2][:, 2 + NM:2 + T], b[:, :], ACT.Copy).then_inc(self.taken, 1)
                        if f >= 1:
                            self.silu_conv(act, f - 1)
                        if f == 7:
                            self.silu_conv(act, 7)
                    elif u in (4, 5):
                        if u == 4:
                            continue
                    else:
                        act.wait_ge(self.product, g + 1)
                        act.wait_ge(self.taken, g)
                        if u == 2:
                            dst = EVT["v1"][0:n, i, :, 0:HD]
                            act.activation(dst, b[0:n, :].rearrange("p (h e) -> p h e", h=NH), ACT.Copy).then_inc(self.taken, 1)
                        else:
                            if u == 7 and i == 0:
                                act.wait_ge(self.rows_in, 64)
                            dst, f = {3: (EVT["sgo"], ACT.Sigmoid), 6: (EVT["rv"], ACT.Copy), 7: (EVT["sgr"], ACT.Silu)}[u]
                            act.activation(dst[0:n, i], b[0:n, :], f).then_inc(self.taken, 1)

            def silu_conv(self, act, f):
                act.wait_ge(self.conv, f + 1)
                act.activation(EVT["qk"][:, f], EVT["qk"][:, f], ACT.Silu).then_inc(self.raw, 1)

            def dve(self, dve, step, gates):
                for r in self.rawbuf:
                    step(dve.memset(r[:, 0:2], 0.0))
                    ins = dve.memset(r[:, T + 2:T + 4], 0.0)
                    if r is self.rawbuf[1]:
                        ins.then_inc(self.pad, 1)
                    else:
                        step(ins)
                step(dve.memset(EVT["v1"][:, :, :, HD:HD + 1], 1.0))
                dve.wait_ge(self.wg_high, 1)
                dve.tensor_tensor(high(self.wg), self.wg, part(self.wg_h), ALU.subtract).then_inc(self.wg_low, 1)
                halves[0].low(dve, 0)
                dve.wait_ge(self.gate_product, 1)
                dve.tensor_scalar(self.gates[:, NM:T], bank[6][0:16, :], self.gb, None, ALU.add)
                dve.tensor_scalar(self.gates[:, 0:NM], bank[7][0:16, 0:NM], self.gb, None, ALU.add).then_inc(self.gate_copied, 1)
                turn = 0
                for g, (u, i) in enumerate(self.groups):
                    n = rows_of(i)
                    b = bank[g % 4]
                    if (u, i) == (2, 0):
                        dve.wait_ge(self.rows_in, 64)
                        gates.dve_decay(dve, step)
                        halves[0].low(dve, u + 1)
                        gates.dve_maxima(dve, step)
                    elif i == 2 and u != 2:
                        halves[0].low(dve, u + 1)
                    if (u, i) == (4, 0):
                        gates.dve_columns(dve, step)
                    if u < 2:
                        f = 4 * u + i
                        dve.wait_ge(self.taken, g + 1)
                        raw, acc = self.rawbuf[f % 2], EVT["qk"][:, f]
                        step(dve.tensor_scalar(acc, raw[:, 0:T], self.convw[:, f, 0:1], None, ALU.mult))
                        for w in range(1, CONV):
                            ins = dve.scalar_tensor_tensor(acc, raw[:, w:w + T], self.convw[:, f, w:w + 1], acc,
                                                           ALU.mult, ALU.add)
                            if w < CONV - 1:
                                step(ins)
                            else:
                                ins.then_inc(self.conv, 1)
                    elif u in (4, 5):
                        dve.wait_ge(self.product, g + 1)
                        dve.wait_ge(self.taken, g)
                        x = b[0:n, :].rearrange("p (h s e) -> p h s e", h=NH, s=2)
                        xv = lambda y: y[0:n].rearrange("p (h s e) -> p h s e", h=NH, s=2)
                        cos = self.cs[0:n, i, 0:64].unsqueeze(1).broadcast_to([n, NH, 64])
                        sin = self.cs[0:n, i, 64:128].unsqueeze(1).broadcast_to([n, NH, 64])
                        A, B, O = xv(self.rope_a), xv(self.rope_b), xv(self.rope_o)
                        if turn:
                            dve.wait_ge(self.turned, turn)
                        step(dve.tensor_tensor(A[:, :, 0], x[:, :, 0], cos, ALU.mult))
                        step(dve.tensor_tensor(A[:, :, 1], x[:, :, 1], cos, ALU.mult))
                        step(dve.tensor_tensor(B[:, :, 0], x[:, :, 1], sin, ALU.mult))
                        dve.tensor_tensor(B[:, :, 1], x[:, :, 0], sin, ALU.mult).then_inc(self.taken, 1)
                        dve.wait_ge(self.taken, g + 1)
                        step(dve.tensor_tensor(O[:, :, 0], A[:, :, 0], B[:, :, 0], ALU.subtract))
                        dve.tensor_tensor(O[:, :, 1], A[:, :, 1], B[:, :, 1], ALU.add).then_inc(self.rope, 1)
                        if turn:
                            self.copy_turned(dve, turn - 1)
                        turn += 1
                self.copy_turned(dve, turn - 1)

            def copy_turned(self, dve, turn):
                u, i = turn // NT, turn % NT
                n = rows_of(i)
                c0, c1 = cols_of(i)
                dve.wait_ge(self.turned, turn + 1)
                dve.tensor_copy(EVT["rqk"][:, 4 * u:4 * u + 4, c0:c1],
                                bank[6 + turn % 2][:, 0:4 * n].rearrange("p (h c) -> p h c", h=NH)).then_inc(self.turned_taken, 1)

        class Gates:

            def __init__(self, rows):
                (self.neg, self.soft, self.rows, self.m, self.turned, self.lneg, self.lsoft,
                 self.logit_in) = (
                    sem("g_" + x) for x in ("neg", "soft", "rows", "m", "turned", "lneg", "lsoft", "logit_in"))
                self.raw = rows
                self.logit, self.lg_e = sm(1500, 8), sm(1508, 8)
                z = [ar(EV["rqk"] + i * T, T)[0:NH] for i in range(7)]
                self.t, self.ones, self.zeros = z[0], z[1], z[2]
                self.F, self.em = z[3:5], z[5:7]
                self.Mx = [ar(EV["tmp"] + i * T, T)[0:NH] for i in range(2)]
                self.cols_sb = ar(EV["tmp"] + 2 * T, 2 * 2 * NT * NH, d=2, x=2, t=NT)

            def order(self, d, x):
                return x[:, NM:T] if d == 0 else x[:, T - 1:NM - 1:-1]

            def act_decay(self, act, step):
                for d in range(2):
                    act.wait_ge(self.neg, d + 1)
                    step(act.activation(self.em[d], self.em[d], ACT.Exp))
                    act.activation(self.em[d], self.em[d], ACT.Ln, bias=1.0).then_inc(self.soft, 1)
                act.wait_ge(self.lneg, 1)
                step(act.activation(self.lg_e, self.lg_e, ACT.Exp))
                act.activation(self.lg_e, self.lg_e, ACT.Ln, bias=1.0).then_inc(self.lsoft, 1)

            def act_maxima(self, act):
                act.wait_ge(self.m, 1)
                for d in range(2):
                    act.activation(self.em[d], self.em[d], ACT.Exp, scale=-1.0).then_inc(self.rows, 1)

            def dve_decay(self, dve, step):
                step(dve.memset(self.ones, 1.0))
                step(dve.memset(self.zeros, 0.0))
                step(dve.memset(self.cols_sb, 1.0))
                for d in range(2):
                    f = self.raw[2 * d + 1]
                    dve.scalar_tensor_tensor(self.em[d], f, -1.0, f, ALU.mult, ALU.min).then_inc(self.neg, 1)
                dve.wait_ge(self.logit_in, 16)
                dve.scalar_tensor_tensor(self.lg_e, self.logit, -1.0, self.logit, ALU.mult, ALU.min).then_inc(self.lneg, 1)

            def dve_maxima(self, dve, step):
                dve.wait_ge(self.lsoft, 1)
                step(dve.scalar_tensor_tensor(lgam, self.logit, 0.0, self.lg_e, ALU.min, ALU.subtract))
                for d in range(2):
                    i, f = self.raw[2 * d], self.raw[2 * d + 1]
                    F, M = self.F[d], self.Mx[d]
                    dve.wait_ge(self.soft, d + 1)
                    step(dve.scalar_tensor_tensor(self.t, f, 0.0, self.em[d], ALU.min, ALU.subtract))
                    step(dve.tensor_tensor_scan(F[:, 0:NM], self.ones[:, 0:NM], self.t[:, 0:NM], 0.0, ALU.mult, ALU.add))
                    step(dve.tensor_tensor_scan(self.order(d, F), self.ones[:, NM:T], self.order(d, self.t),
                                                F[:, NM - 1:NM], ALU.mult, ALU.add))
                    step(dve.tensor_tensor(i, i, F, ALU.subtract))
                    step(dve.tensor_tensor_scan(M[:, 0:NM], self.zeros[:, 0:NM], i[:, 0:NM], 0.0, ALU.add, ALU.max))
                    step(dve.tensor_tensor_scan(self.order(d, M), self.zeros[:, NM:T], self.order(d, i),
                                                M[:, NM - 1:NM], ALU.add, ALU.max))
                    ins = dve.tensor_tensor(self.em[d], F, M, ALU.add)
                    if d:
                        ins.then_inc(self.m, 1)
                    else:
                        step(ins)

            def dve_columns(self, dve, step):
                dve.wait_ge(self.turned, 1)
                ps = bank[7][:, 0:2 * 2 * NT * NH].rearrange("p (d x t h) -> p d x t h", d=2, x=2, t=NT)
                for d in range(2):
                    for x in range(2):
                        step(dve.tensor_copy(self.cols_sb[0:NM, d, x, 0], ps[0:NM, d, x, 0]))
                        step(dve.tensor_copy(self.cols_sb[:, d, x, 1:NT], ps[:, d, x, 1:NT]))

            def pe(self, pe):
                pe.wait_ge(self.rows, 2)
                for d in range(2):
                    for x, row in enumerate((self.raw[2 * d], self.em[d])):
                        for t in range(NT):
                            n = rows_of(t)
                            c0, c1 = cols_of(t)
                            o = ((d * 2 + x) * NT + t) * NH
                            ins = pe.transpose(bank[7][0:n, o:o + NH], row[:, c0:c1], ident[0:NH, 0:NH])
                ins.then_inc(self.turned, 1)

            def a_col(self, d, t, h):
                return self.cols_sb[0:rows_of(t), d, 0, t, h:h + 1]

            def em_col(self, d, t0, t1, n, h):
                return self.cols_sb[0:n, d, 1, t0:t1, h]

        def qcols(kt, d):
            return (128 * kt, NR) if d == 0 else (0, 128 * kt + 128)

        PACK = [[0, 512, 896, 1152], [0, 128, 384, 768]]
        TRI = 1280

        class HeadNorm:

            def __init__(self, k, gate):
                self.sq, self.ms, self.rs, self.done = (sem(f"hn{k}_{x}") for x in ("sq", "ms", "rs", "done"))
                self.gate = gate
                self.buf = [ar(EV["tmp"] + 2 * T + 80, NT * HD, t=NT), ar(EV["rows"], NT * HD, t=NT)]
                self.junk = ar(EV["rows"] + 640, HD)
                self.ss, self.mean, self.rstd = (sm(1524 + 5 * i, 5) for i in range(3))

            def act(self, act, h):
                if h:
                    act.wait_ge(self.ms, 2 * h)
                for t in range(NT):
                    n = rows_of(t)
                    if NT * h + t:
                        act.wait_ge(self.sq, NT * h + t)
                    act.activation(self.junk[0:n], self.buf[h % 2][0:n, t], ACT.Square,
                                   accum_out=self.ss[0:n, t:t + 1]).then_inc(self.sq, 1)

            def dve_mean(self, dve, h):
                dve.wait_ge(self.sq, NT * (h + 1))
                if h:
                    dve.wait_ge(self.rs, 2 * h)
                for n, t0, t1 in ((NM, 0, 1), (128, 1, NT)):
                    dve.tensor_scalar(self.mean[0:n, t0:t1], self.ss[0:n, t0:t1], 1.0 / HD, EPS, ALU.mult,
                                      ALU.add).then_inc(self.ms, 1)

            def pool(self, pool, h):
                for i, (n, t0, t1) in enumerate(((NM, 0, 1), (128, 1, NT))):
                    pool.wait_ge(self.ms, 2 * h + i + 1)
                    if h:
                        pool.wait_ge(self.done, h)
                    pool.tensor_tensor(self.rstd[0:n, t0:t1], self.mean[0:n, t0:t1],
                                       minus_half[0:n, 0:1].broadcast_to([n, t1 - t0]), ALU.pow).then_inc(self.rs, 1)

            def dve_apply(self, dve, h):
                dve.wait_ge(self.rs, 2 * h + 2)
                for t in range(NT):
                    n = rows_of(t)
                    g = self.gate[0:n, t, HD * h:HD * h + HD]
                    ins = dve.scalar_tensor_tensor(g, self.buf[h % 2][0:n, t], self.rstd[0:n, t:t + 1], g,
                                                   ALU.mult, ALU.mult)
                ins.then_inc(self.done, 1)

        OUT_AT = [(6, 2 * (HD + 1)), (6, 0), (6, HD + 1), (7, 0), (7, HD + 1)]

        class MLSTM:

            def __init__(self, gates):
                (self.mbc, self.diag, self.dexp, self.sprod, self.sd, self.oprod, self.oread, self.comb,
                 self.pre, self.pre_d, self.pre_e, self.pre_sd, self.masks_in) = (
                    sem("ml_" + x) for x in ("mbc", "diag", "dexp", "sprod", "sd", "oprod", "oread", "comb", "pre", "pre_d", "pre_e", "pre_sd",
                    "masks_in"))
                self.g = gates
                self.D = [uflat[:, d * TRI:(d + 1) * TRI] for d in range(2)]
                self.Dm = [uflat[0:NM, 2 * TRI + d * NR:2 * TRI + (d + 1) * NR] for d in range(2)]
                self.Dmm = uflat[0:NM, 2 * TRI + 2 * NR:2 * TRI + 2 * NR + 2 * NH * NM].rearrange("p (d h q) -> p d h q", d=2, h=NH)
                self.sel = sm(280, NH * 128, h=NH)[0:NH]
                self.far = ar(EV["rows"] + 1420, 256, d=2)
                self.dn = sm(1540, 5)
                self.rd = sm(1545, 5)
                self.out = ar(EV["rows"] + 768, NT * (HD + 1), t=NT)
                self.norm = HeadNorm(0, EVT["sgo"])

            def consts(self, act):
                act.dma_start(self.sel, a["c_sel"][:, :, :]).then_inc(self.masks_in, 16)
                act.dma_start(self.far, a["c_far"][:, :, :]).then_inc(self.masks_in, 16)

            def q(self, h):
                return EVT["qk"][:, h]

            def k(self, h):
                return EVT["qk"][:, NH + h]

            def pe(self, pe):
                for h in range(NH):
                    pe.matmul(bank[7][0:NM, 128 + NM * h:128 + NM * h + NM], self.k(h)[:, 0:NM], self.q(h)[:, 0:NM],
                              start=True, stop=True)
                pe.wait_ge(self.masks_in, 32)
                for d in range(2):
                    for h in range(NH):
                        o = NM * (NH * d + h)
                        ins = pe.matmul(bank[7][0:NM, o:o + NM], self.sel[:, h, 0:NM], self.g.Mx[d][:, 0:NM],
                                        start=True, stop=True)
                ins.then_inc(self.pre, 1)

                def scores(h):
                    if h:
                        pe.wait_ge(self.sd, 2 * h)
                    for kt in range(4):
                        pe.matmul(bank[kt][:, :], self.k(h)[:, NM + 128 * kt:NM + 128 * kt + 128], self.q(h)[:, NM:T],
                                  start=True, stop=True)
                    pe.matmul(bank[4][0:NM, :], self.k(h)[:, 0:NM], self.q(h)[:, NM:T], start=True,
                              stop=True).then_inc(self.sprod, 1)

                def maxima(s):
                    h, d = s // 2, s % 2
                    if s:
                        pe.wait_ge(self.dexp, s)
                    pe.matmul(bank[5][:, :], self.sel[:, h], self.g.Mx[d][:, NM:T], start=True, stop=True).then_inc(self.mbc, 1)

                scores(0)
                maxima(0)
                pe.wait_ge(self.pre_sd, 2)
                for s in range(2 * NH):
                    h, d = s // 2, s % 2
                    if s < 2 * NH - 1:
                        maxima(s + 1)
                    pe.wait_ge(self.sd, s + 1)
                    if d and h < NH - 1:
                        scores(h + 1)
                    if s:
                        pe.wait_ge(self.oread, s)
                    for t in range(1, NT):
                        qt = t - 1
                        bk, o = OUT_AT[t]
                        ps = bank[bk][:, o:o + HD + 1]
                        pe.matmul(ps, self.Dm[d][:, 128 * qt:128 * qt + 128], EVT["v1"][0:NM, 0, h], start=True, stop=False)
                        kts = range(0, qt + 1) if d == 0 else range(qt, 4)
                        for kt in kts:
                            c = PACK[d][kt] + 128 * qt - qcols(kt, d)[0]
                            ins = pe.matmul(ps, self.D[d][:, c:c + 128], EVT["v1"][:, kt + 1, h], start=False,
                                            stop=(kt == kts[-1]))
                    bk, o = OUT_AT[0]
                    pe.matmul(bank[bk][0:NM, o:o + HD + 1], self.Dmm[:, d, h], EVT["v1"][0:NM, 0, h], start=True,
                              stop=True).then_inc(self.oprod, 1)
                ret.pe_first(pe)

            def act(self, act, step):
                act.wait_ge(self.pre_d, 1)
                act.activation(self.Dmm, self.Dmm, ACT.Exp, scale=-1.0).then_inc(self.pre_e, 1)
                for s in range(2 * NH):
                    h, d = s // 2, s % 2
                    act.wait_ge(self.diag, s + 1)
                    for kt in range(4):
                        c0, c1 = qcols(kt, d)
                        o = PACK[d][kt]
                        if d == 0:
                            c0, o = c0 + 128, o + 128
                        else:
                            c1 -= 128
                        if c1 > c0:
                            act.activation(self.D[d][:, o:o + c1 - c0], bank[5][:, c0:c1], ACT.Exp,
                                           bias=self.g.a_col(d, kt + 1, h), scale=-1.0)
                    act.activation(self.Dm[d], bank[5][0:NM, :], ACT.Exp, bias=self.g.a_col(d, 0, h), scale=-1.0)
                    for kt in range(4):
                        o = PACK[d][kt] + (0 if d == 0 else 128 * kt)
                        ins = act.activation(self.D[d][:, o:o + 128], self.D[d][:, o:o + 128], ACT.Exp, scale=-1.0)
                    ins.then_inc(self.dexp, 1)
                    if s == 1:
                        halves[0].act(act, 9)
                    if s == 2 * NH - 2:
                        act.wait_ge(self.sprod, NH)
                        ret.consts(act)
                    if d and h:
                        self.squares(act, h - 1)
                self.squares(act, NH - 1)

            def squares(self, act, h):
                act.wait_ge(self.comb, 2 * h + 2)
                self.norm.act(act, h)

            def dve(self, dve, step):
                def diag(s):
                    h, d = s // 2, s % 2
                    dve.wait_ge(self.mbc, s + 1)
                    if s >= 2:
                        dve.wait_ge(self.oprod, s - 1)
                    for kt in range(4):
                        o = PACK[d][kt] + (0 if d == 0 else 128 * kt)
                        ins = dve.scalar_tensor_tensor(self.D[d][:, o:o + 128], bank[5][:, 128 * kt:128 * kt + 128],
                                                       self.g.a_col(d, kt + 1, h), self.far[:, d], ALU.subtract, ALU.max)
                    ins.then_inc(self.diag, 1)

                def weigh(s):
                    h, d = s // 2, s % 2
                    dve.wait_ge(self.sprod, h + 1)
                    dve.wait_ge(self.dexp, s + 1)
                    for kt in range(4):
                        c0, c1 = qcols(kt, d)
                        o = PACK[d][kt]
                        x = self.D[d][:, o:o + c1 - c0]
                        dve.scalar_tensor_tensor(x, bank[kt][:, c0:c1], HEAD_SCALE, x, ALU.mult, ALU.mult)
                    dve.scalar_tensor_tensor(self.Dm[d], bank[4][0:NM, :], HEAD_SCALE, self.Dm[d], ALU.mult,
                                             ALU.mult).then_inc(self.sd, 1)

                def take(s):
                    dve.wait_ge(self.oprod, s + 1)
                    for (n, t0, t1, bk, o) in ((NM, 0, 1, 6, 2 * (HD + 1)), (128, 1, 3, 6, 0), (128, 3, 5, 7, 0)):
                        src = bank[bk][0:n, o:o + (HD + 1) * (t1 - t0)].rearrange("p (t e) -> p t e", t=t1 - t0)
                        ins = dve.tensor_copy(self.out[0:n, t0:t1], src)
                    ins.then_inc(self.oread, 1)

                def combine(s):
                    h, d = s // 2, s % 2
                    hm = self.norm.buf[h % 2]
                    den, num = self.out[:, :, HD], self.out[:, :, 0:HD]
                    dve.wait_ge(self.oread, s + 1)
                    step(dve.scalar_tensor_tensor(self.dn, den, -1.0, self.g.em_col(d, 0, NT, 128, h), ALU.mult, ALU.max))
                    step(dve.tensor_tensor(self.dn, den, self.dn, ALU.max))
                    step(dve.reciprocal(self.rd, self.dn))
                    rd = self.rd.unsqueeze(2).broadcast_to([128, NT, HD])
                    if d == 0:
                        if h >= 2:
                            dve.wait_ge(self.norm.done, h - 1)
                        ins = dve.tensor_tensor(hm, num, rd, ALU.mult)
                    else:
                        step(dve.tensor_tensor(num, num, rd, ALU.mult))
                        ins = dve.tensor_tensor(hm, hm, num, ALU.add)
                    ins.then_inc(self.comb, 1)
                    dve.wait_ge(self.comb, s + 1)

                step(dve.memset(self.out[:, 0], 1.0))
                dve.wait_ge(self.pre, 1)
                for d in range(2):
                    for h in range(NH):
                        o = NM * (NH * d + h)
                        ins = dve.scalar_tensor_tensor(self.Dmm[:, d, h], bank[7][0:NM, o:o + NM], self.g.a_col(d, 0, h),
                                                       self.far[0:NM, 0, 0:NM], ALU.subtract, ALU.max)
                ins.then_inc(self.pre_d, 1)
                dve.wait_ge(self.pre_e, 1)
                for d in range(2):
                    dve.scalar_tensor_tensor(self.Dmm[:, d], bank[7][0:NM, 128:128 + NH * NM].rearrange("p (h q) -> p h q", h=NH),
                                             HEAD_SCALE, self.Dmm[:, d], ALU.mult, ALU.mult).then_inc(self.pre_sd, 1)
                diag(0)
                for s in range(2 * NH):
                    h, d = s // 2, s % 2
                    weigh(s)
                    if s:
                        take(s - 1)
                    if s < 2 * NH - 1:
                        diag(s + 1)
                    if s:
                        combine(s - 1)
                    if d and h:
                        self.norm.dve_mean(dve, h - 1)
                        self.norm.dve_apply(dve, h - 1)
                take(2 * NH - 1)
                combine(2 * NH - 1)
                self.norm.dve_mean(dve, NH - 1)
                self.norm.dve_apply(dve, NH - 1)

            def pool(self, pool):
                halves[0].low(pool, 9)
                for h in range(NH):
                    self.norm.pool(pool, h)

        class Retention:

            def __init__(self):
                (self.consts_in, self.pre, self.table, self.sprod, self.sd, self.oprod, self.comb,
                 self.mm, self.mexp, self.msd) = (
                    sem("re_" + x) for x in ("consts_in", "pre", "table", "sprod", "sd", "oprod", "comb", "mm", "mexp", "msd"))
                both = [uflat[:, 0:5 * NR], ar(EV["qk"], 5 * NR)]
                self.SD = [x[:, 0:4 * NR].rearrange("p (k q) -> p k q", k=4) for x in both]
                self.SDm = [x[0:NM, 4 * NR:5 * NR] for x in both]
                self.E = uflat[:, 5 * NR:5 * NR + 896]
                self.ED = uflat[:, 5 * NR + 896:5 * NR + 1024]
                self.Em = ar(EV["rows"] + 1420, NR)[0:NM]
                self.mmE = sm(280, NH * 2 * NM, h=NH, d=2)[0:NM]
                self.mm = sm(420, NH * NM, h=NH)[0:NM]
                c = EV["qk"] + 5 * NR
                self.DF, self.DB = ar(c, NR), ar(c + NR, NR)
                self.MF, self.MB = ar(c + 2 * NR, 128), ar(c + 2 * NR + 128, 128)
                dm = uflat[0:NM, 8 * T - NR:8 * T]
                self.dm = [dm, dm[:, ::-1]]
                self.meta_distances = dm
                self.Em2 = ar(EV["rows"] + 768, NR)[0:NM]
                self.norm = HeadNorm(1, EVT["sgr"])

            def consts(self, act):
                for dst, n in ((self.DF, "c_df"), (self.DB, "c_db"), (self.MF, "c_mf"), (self.MB, "c_mb")):
                    act.dma_start(dst, a[n][:, :]).then_inc(self.consts_in, 16)
                act.dma_start(self.meta_distances, a["c_dm"][:, :]).then_inc(self.consts_in, 16)

            def q(self, h):
                return EVT["rqk"][:, h]

            def k(self, h):
                return EVT["rqk"][:, NH + h]

            def lg(self, d, h, n=128):
                return lgam[0:n, NH * d + h:NH * d + h + 1]

            def pe_scores(self, pe, h):
                if h:
                    pe.wait_ge(self.sd, h)
                for kt in range(4):
                    pe.matmul(bank[kt][:, :], self.k(h)[:, NM + 128 * kt:NM + 128 * kt + 128], self.q(h)[:, NM:T],
                              start=True, stop=True)
                pe.matmul(bank[4][0:NM, :], self.k(h)[:, 0:NM], self.q(h)[:, NM:T], start=True,
                          stop=True).then_inc(self.sprod, 1)

            def pe_first(self, pe):
                pe.wait_ge(mlstm.sd, 2 * NH)
                pe.wait_ge(mlstm.dexp, 2 * NH)
                for h in range(NH):
                    ins = pe.matmul(bank[5][0:NM, NM * h:NM * h + NM], self.k(h)[:, 0:NM], self.q(h)[:, 0:NM],
                                    start=True, stop=True)
                ins.then_inc(self.pre, 1)
                self.pe_scores(pe, 0)

            def pe(self, pe):
                for h in range(NH):
                    pe.wait_ge(self.sd, h + 1)
                    if h < NH - 1:
                        self.pe_scores(pe, h + 1)
                    if h:
                        pe.wait_ge(self.comb, h)
                    v = lambda t, n: EVT["rv"][0:n, t, HD * h:HD * h + HD]
                    for t in range(1, NT):
                        qt = t - 1
                        bk, o = OUT_AT[t]
                        ps = bank[bk][:, o:o + HD]
                        pe.matmul(ps, self.SDm[h % 2][:, 128 * qt:128 * qt + 128], v(0, NM), start=True, stop=False)
                        for kt in range(4):
                            pe.matmul(ps, self.SD[h % 2][:, kt, 128 * qt:128 * qt + 128], v(kt + 1, 128), start=False, stop=(kt == 3))
                    bk, o = OUT_AT[0]
                    if h == 0:
                        pe.wait_ge(self.msd, 1)
                    pe.matmul(bank[bk][0:NM, o:o + HD], self.mm[:, h], v(0, NM), start=True, stop=True).then_inc(self.oprod, 1)

            def act(self, act, step):
                act.wait_ge(self.consts_in, 80)
                for h in range(NH):
                    if h:
                        act.wait_ge(self.sd, h)
                    act.activation(self.E[:, 384:896], self.DF, ACT.Exp, scale=self.lg(0, h))
                    act.activation(self.E[:, 0:384], self.DB[:, 0:384], ACT.Exp, scale=self.lg(1, h))
                    act.activation(self.ED, self.DB[:, 384:512], ACT.Exp, scale=self.lg(1, h))
                    act.activation(self.Em, self.dm[0], ACT.Exp, scale=self.lg(0, h, NM))
                    act.activation(self.Em2, self.dm[1], ACT.Exp, scale=self.lg(1, h, NM)).then_inc(self.table, 1)
                    if h == 0:
                        for i in range(NH):
                            for d in range(2):
                                ins = act.activation(self.mmE[:, i, d], self.DF[0:NM, 0:NM], ACT.Exp, scale=self.lg(d, i, NM))
                        ins.then_inc(self.mexp, 1)
                    if h > 1:
                        act.wait_ge(self.comb, h - 1)
                        self.norm.act(act, h - 2)
                for h in range(NH - 1, NH):
                    act.wait_ge(self.comb, h)
                    self.norm.act(act, h - 1)
                act.wait_ge(self.comb, NH)
                self.norm.act(act, NH - 1)

            def dve(self, dve, step):
                dve.wait_ge(self.consts_in, 80)
                def weigh(h):
                    dve.wait_ge(self.table, h + 1)
                    diag = self.E[:, 384:512]
                    step(dve.tensor_tensor(diag, diag, self.MF, ALU.mult))
                    step(dve.tensor_tensor(self.ED, self.ED, self.MB, ALU.mult))
                    step(dve.tensor_tensor(diag, diag, self.ED, ALU.add))
                    step(dve.tensor_tensor(self.Em, self.Em, self.Em2, ALU.add))
                    dve.wait_ge(self.sprod, h + 1)
                    if h >= 2:
                        dve.wait_ge(self.oprod, h - 1)
                    for kt in range(4):
                        dve.scalar_tensor_tensor(self.SD[h % 2][:, kt], bank[kt][:, :], HEAD_SCALE,
                                                 self.E[:, 384 - 128 * kt:896 - 128 * kt], ALU.mult, ALU.mult)
                    dve.scalar_tensor_tensor(self.SDm[h % 2], bank[4][0:NM, :], HEAD_SCALE, self.Em, ALU.mult,
                                             ALU.mult).then_inc(self.sd, 1)

                weigh(0)
                dve.wait_ge(self.mexp, 1)
                dve.wait_ge(self.pre, 1)
                for h in range(NH):
                    step(dve.tensor_tensor(self.mm[:, h], self.mmE[:, h, 0], self.mmE[:, h, 1], ALU.add))
                    step(dve.tensor_tensor(self.mm[:, h], self.mm[:, h], self.MF[0:NM, 0:NM], ALU.mult))
                dve.scalar_tensor_tensor(self.mm, bank[5][0:NM, 0:NH * NM].rearrange("p (h q) -> p h q", h=NH),
                                         HEAD_SCALE, self.mm, ALU.mult, ALU.mult).then_inc(self.msd, 1)
                for h in range(NH):
                    if h < NH - 1:
                        weigh(h + 1)
                    dve.wait_ge(self.oprod, h + 1)
                    if h >= 2:
                        dve.wait_ge(self.norm.done, h - 1)
                    hm = self.norm.buf[h % 2]
                    for t in range(NT):
                        n = rows_of(t)
                        bk, o = OUT_AT[t]
                        ins = dve.tensor_copy(hm[0:n, t], bank[bk][0:n, o:o + HD])
                    ins.then_inc(self.comb, 1)
                    if h:
                        self.norm.dve_mean(dve, h - 1)
                        self.norm.dve_apply(dve, h - 1)
                self.norm.dve_mean(dve, NH - 1)
                self.norm.dve_apply(dve, NH - 1)

            def pool(self, pool):
                for h in range(NH):
                    self.norm.pool(pool, h)

        class Project:

            turned, copied, high, h_in, product, added = (
                sem("pr_" + x) for x in ("turned", "copied", "high", "h_in", "product", "added"))

            def __init__(self, layer, mix, mixT, mixH, gain, base):
                self.mix, self.mixT, self.mixH, self.gain, self.base = mix, mixT, mixH, gain, base
                self.halves = halves[layer]
                self.c = 2 * NT * layer
                self.h_count = 16 * NT * (layer + 1)

            def turn_pe(self, pe):
                for t in range(NT):
                    n = rows_of(t)
                    for g in range(2):
                        i = 2 * t + g
                        if i >= 4:
                            pe.wait_ge(self.copied, self.c + i - 3)
                        for k in range(4):
                            ins = pe.transpose(bank[i % 4][:, k * n:(k + 1) * n], self.mix(t, 4 * g + k), ident[0:n, 0:n])
                        ins.then_inc(self.turned, 1)

            def turn_dve(self, dve, step):
                for t in range(NT):
                    n = rows_of(t)
                    c0, c1 = cols_of(t)
                    for g in range(2):
                        i = 2 * t + g
                        dve.wait_ge(self.turned, self.c + i + 1)
                        ps = bank[i % 4][:, 0:4 * n].rearrange("p (k c) -> p k c", k=4)
                        dst = self.mixT[:, 4 * g:4 * g + 4, c0:c1]
                        if self.gain is None:
                            ins = dve.tensor_copy(dst, ps)
                        else:
                            ins = dve.tensor_tensor(dst, ps, gcol[:, self.gain, 4 * g:4 * g + 4].unsqueeze(2)
                                                    .broadcast_to([128, 4, n]), ALU.mult)
                        ins.then_inc(self.copied, 1)

                self.turn_low(dve, DVE_LOWS)

            def turn_low(self, eng, tiles):
                for t in tiles:
                    c0, c1 = cols_of(t)
                    eng.wait_ge(self.high, self.c // 2 + t + 1)
                    eng.tensor_tensor(high(self.mixT[:, :, c0:c1]), self.mixT[:, :, c0:c1], part(self.mixH[:, :, c0:c1]),
                                      ALU.subtract)

            def turn_act(self, act):
                for t in range(NT):
                    c0, c1 = cols_of(t)
                    act.wait_ge(self.copied, self.c + 2 * t + 2)
                    act.activation(high(self.mixH[:, :, c0:c1]), self.mixT[:, :, c0:c1], ACT.Copy).then_inc(self.high, 1)

            def pe(self, pe, norm, experts):
                for half in range(2):
                    u = self.base + half
                    self.halves.ready(pe, u)
                    for t in range(NT):
                        g = NT * half + t
                        c0, c1 = cols_of(t)
                        if g >= 4:
                            pe.wait_ge(self.added, self.c + g - 3)
                        mix = (lambda k: self.mixH[:, k, c0:c1]), (lambda k: self.mixT[:, k, c0:c1])
                        product3(pe, bank[g % 4][0:rows_of(t), :], mix, self.halves.weights(u), range(KB), True,
                                 True).then_inc(self.product, 1)
                        if half and t:
                            norm.pe_tile(pe, t - 1)
                    pe.wait_ge(self.product, self.c + NT * half + NT)
                    self.halves.used(pe, u)
                experts.route(pe, (0, 1))
                norm.pe_tile(pe, NT - 1)
                experts.route(pe, (2, 3, 4))

            def act(self, act, norm):
                for t in range(NT):
                    act.wait_ge(self.added, self.c + NT + t + 1)
                    norm.act_tile(act, t)

            def dve(self, dve, norm):
                dve.wait_ge(self.h_in, self.h_count)
                for half in range(2):
                    for t in range(NT):
                        g = NT * half + t
                        n = rows_of(t)
                        x = H[0:n, t, BLK * half:BLK * half + BLK]
                        dve.wait_ge(self.product, self.c + g + 1)
                        dve.tensor_tensor(x, bank[g % 4][0:n, :], x, ALU.add).then_inc(self.added, 1)
                        if half:
                            norm.dve_mean(dve, t)
                            if t == NT - 1:
                                norm.dve_uT(dve, t - 1)
                            dve.wait_ge(self.added, self.c + g + 1)
                            norm.dve_scale(dve, t)
                            if 0 < t < NT - 1:
                                norm.dve_uT(dve, t - 1)
                norm.dve_uT(dve, NT - 1)
        OD_Q, OD_K, OD_V, OD_VS, OD_ATT = 0, 4224, 8448, 13568, 16640
        qT, kT = ar(OD_Q, 8 * T, k=8), ar(OD_K, 8 * T, k=8)
        vtok = ar(OD_V, NT * D, t=NT)
        vmid = ar(OD_VS, 3 * D, t=3)
        att = ar(OD_ATT, NT * D, t=NT)

        class OddIn:

            def __init__(self):
                (self.product, self.taken, self.sq, self.ms, self.rs, self.qn, self.turned,
                 self.copied, self.vmid) = (
                    sem("oi_" + x) for x in ("product", "taken", "sq", "ms", "rs", "qn", "turned", "copied", "vmid"))
                self.junk = ar(OD_ATT, BLK)
                self.qn_sb = [ar(OD_ATT + BLK * (i + 1), BLK) for i in range(2)]
                self.ss, self.mean, self.rstd = (sm(20 + 8 * i, 8) for i in range(3))
                self.groups = [(u, t) for u in range(6) for t in range(NT)]

            def pe(self, pe):
                def turn(g):
                    n = rows_of(self.groups[g][1])
                    pe.wait_ge(self.qn, g + 1)
                    if g >= 2:
                        pe.wait_ge(self.copied, g - 1)
                    for k in range(4):
                        ins = pe.transpose(bank[4 + g % 2][:, k * n:(k + 1) * n],
                                           self.qn_sb[g % 2][0:n, 128 * k:128 * k + 128], ident[0:n, 0:n])
                    ins.then_inc(self.turned, 1)

                for g, (j, t) in enumerate(self.groups):
                    if t == 0:
                        halves[1].ready(pe, j)
                    if g >= 4:
                        pe.wait_ge(self.taken, g - 3)
                    c0, c1 = cols_of(t)
                    product3(pe, bank[g % 4][0:rows_of(t), :], tokens(c0, c1), halves[1].weights(j), range(KB), True,
                             True).then_inc(self.product, 1)
                    if 1 <= g <= 4 * NT:
                        turn(g - 1)
                    if (j, t) == (4, 1):
                        pe.wait_ge(self.copied, 4 * NT)
                        attn.pe_meta_scores(pe)
                    if (j, t) == (4, 4):
                        attn.pe_meta_turn(pe)
                    if (j, t) == (5, 2):
                        pe.wait_ge(self.taken, 5 * NT + 1)
                        attn.pe_meta_values(pe)
                    if t == NT - 1:
                        pe.wait_ge(self.product, g + 1)
                        halves[1].used(pe, j)
                pe.sem_inc(ring_used[TOKEN_SLOT], 1)

            def act(self, act, step):
                for g, (j, t) in enumerate(self.groups):
                    n = rows_of(t)
                    if t == 1:
                        halves[1].act(act, j + 1)
                    act.wait_ge(self.product, g + 1)
                    if j < 4:
                        if g:
                            act.wait_ge(self.ms, g)
                        act.activation(self.junk[0:n], bank[g % 4][0:n, :], ACT.Square).then_inc(self.sq, 1)
                    else:
                        act.wait_ge(self.taken, g)
                        act.activation(vtok[0:n, t, BLK * (j - 4):BLK * (j - 3)], bank[g % 4][0:n, :],
                                       ACT.Copy).then_inc(self.taken, 1)
                    if (j, t) == (4, 2):
                        attn.act_meta(act)

            def shift_values(self, eng):
                eng.wait_ge(self.taken, 6 * NT)
                for i in range(3):
                    eng.dma_start(vmid[0:64, i], vtok[64:128, i + 1]).then_inc(self.vmid, 16)
                    eng.dma_start(vmid[64:128, i], vtok[0:64, i + 2]).then_inc(self.vmid, 16)

            def dve(self, dve, step):
                step(dve.tensor_scalar(gcol[:, 5, 0:1], gcol[:, 5, 0:1], float(AD) ** -0.5, None, ALU.mult))
                for g, (j, t) in enumerate(self.groups[:4 * NT]):
                    n = rows_of(t)
                    if t == 2:
                        halves[1].low(dve, j + 1)
                    dve.wait_ge(self.sq, g + 1)
                    step(dve.tensor_reduce(self.ss[0:n], self.junk[0:n].rearrange("p (h e) -> p h e", e=AD), AX.X, ALU.add))
                    dve.tensor_scalar(self.mean[0:n], self.ss[0:n], 1.0 / AD, EPS, ALU.mult, ALU.add).then_inc(self.ms, 1)
                    if g:
                        self.copy(dve, g - 1)
                    dve.wait_ge(self.rs, g + 1)
                    dve.tensor_tensor(self.qn_sb[g % 2][0:n].rearrange("p (h e) -> p h e", e=AD),
                                      bank[g % 4][0:n, :].rearrange("p (h e) -> p h e", e=AD),
                                      self.rstd[0:n].unsqueeze(2).broadcast_to([n, 8, AD]), ALU.mult).then_inc(self.taken, 1)
                    dve.wait_ge(self.taken, g + 1)
                    dve.sem_inc(self.qn, 1)
                self.copy(dve, 4 * NT - 1)
                attn.dve_meta_scores(dve, step)
                halves[1].low(dve, 5)
                attn.dve_meta_weights(dve, step)
                halves[1].low(dve, 6)
                attn.dve_meta_values(dve)

            def copy(self, dve, g):
                j, t = self.groups[g]
                c0, c1 = cols_of(t)
                dst = (qT if j < 2 else kT)[:, 4 * (j % 2):4 * (j % 2) + 4, c0:c1]
                dve.wait_ge(self.turned, g + 1)
                dve.tensor_scalar(dst, bank[4 + g % 2][:, 0:4 * (c1 - c0)].rearrange("p (k c) -> p k c", k=4),
                                  gcol[:, 5, j // 2:j // 2 + 1], None, ALU.mult).then_inc(self.copied, 1)

            def pool(self, pool):
                for g, (j, t) in enumerate(self.groups[:4 * NT]):
                    n = rows_of(t)
                    pool.wait_ge(self.ms, g + 1)
                    if g:
                        pool.wait_ge(self.taken, g)
                    pool.tensor_tensor(self.rstd[0:n], self.mean[0:n], minus_half[0:n, 0:1].broadcast_to([n, 8]),
                                       ALU.pow).then_inc(self.rs, 1)

        class Attention:
            KEY0 = [0, 64, 192, 256]
            TABLE = [0, 1, 1, 2]
            W = 256
            GROUPS, UNITS = 8, 4 * AH

            def __init__(self):
                (self.product, self.neg, self.exp, self.turned, self.copied, self.pv, self.comb,
                 self.prep, self.s_meta, self.s_taken, self.p_turned, self.p_taken, self.o_meta, self.o_taken, self.v_in,
                 self.m_s, self.m_sub, self.m_exp, self.m_p, self.m_t, self.m_pt, self.m_o,
                 self.m_done) = (
                    sem("at_" + x) for x in ("product", "neg", "exp", "turned", "copied", "pv", "comb", "prep", "s_meta",
                    "s_taken", "p_turned", "p_taken", "o_meta", "o_taken", "v_in", "m_s", "m_sub", "m_exp", "m_p", "m_t", "m_pt",
                    "m_o", "m_done"))
                self.bias = [uflat[:, 1024 * i:1024 * i + 1024].rearrange("p (h k) -> p h k", h=4) for i in range(2)]
                self.bias_in = [sem(f"at_bias_in{i}") for i in range(2)]
                cut = lambda at, n: [uflat[:, at + n * i:at + n * (i + 1)] for i in range(2)]
                self.P, self.PT = cut(2048, self.W), cut(2560, self.W)
                self.Pm, self.Sm = cut(3072, 8 * NM), cut(3328, 8 * NM)
                self.PmT = uflat[:, 4096:4224]
                self.vm = [ar(21760, BLK), uflat[:, 3584:4096]]
                self.km = sm(608, 8 * 2 * NM, k=8)
                self.mn, self.mn_grid = sm(20, 2), sm(22, 2)
                self.mn_meta, self.mx = sm(864, 16, g=2), sm(880, 8)
                self.sum, self.sum_meta = sm(888, 16, g=2), sm(904, 16, g=2)
                self.total, self.rinv = sm(920, 8), sm(928, 8)
                self.mp = sm(40, AH * NM, h=AH)[0:NM]
                self.mpT = sm(300, AH * NM, h=AH)[0:NM]
                self.ms_ = sm(560, 3 * AH, x=3)[0:NM]

            def unit(self, u):
                g = u // 8
                return g, g // 4, g % 4, u % 8, 8 * (g // 4) + u % 8

            def slot(self, h):
                return h // 2 + 8 * (h % 2)

            def values(self, b):
                t = lambda i: vtok[:, i + 1]
                return [(t(0), t(1)), (vmid[:, 0], vmid[:, 1]), (vmid[:, 1], vmid[:, 2]), (t(2), t(3))][b]

            def load_bias(self, act, c):
                g, _, b, _, h = self.unit(4 * c)
                act.dma_start(self.bias[c % 2], a["rpb_tiles"][self.TABLE[b], h:h + 4].rearrange("h q k -> q h k")) \
                    .then_inc(self.bias_in[c % 2], 16)

            def act(self, act, step):
                self.load_bias(act, 0)
                self.load_bias(act, 1)
                halves[1].act(act, 7)
                for u in range(self.UNITS):
                    g, _, b, j, h = self.unit(u)
                    act.wait_ge(self.neg, u + 1)
                    if j == 0 and g >= 2:
                        act.wait_ge(self.comb, g - 1)
                    mn = self.mn[:, u % 2:u % 2 + 1]
                    act.activation(self.P[u % 2], self.P[u % 2], ACT.Exp, bias=mn, scale=-1.0,
                                   accum_out=self.sum[:, g % 2, j:j + 1])
                    act.activation(self.Pm[g % 2][:, NM * j:NM * j + NM], self.Sm[g % 2][:, NM * j:NM * j + NM], ACT.Exp,
                                   bias=mn, accum_out=self.sum_meta[:, g % 2, j:j + 1]).then_inc(self.exp, 1)
                    if u % 4 == 3 and u // 4 + 2 < self.UNITS // 4:
                        self.load_bias(act, u // 4 + 2)
                    if u == 0:
                        act.wait_ge(self.prep, 1)
                    if u < 8:
                        for h in (2 * u, 2 * u + 1):
                            act.dma_start(self.vm[h // 8][NM * (h % 8):NM * (h % 8) + NM, AD * (h % 8):AD * (h % 8) + AD],
                                          vtok[0:NM, 0, AD * h:AD * h + AD]).then_inc(self.v_in, 16)
                    if u % 8 == 2 and u > 8:
                        self.take_values(act, u // 8 - 1)
                self.take_values(act, self.GROUPS - 1)

            def place(self, g):
                return att[:, g % 4 + 1, BLK * (g // 4):BLK * (g // 4) + BLK]

            def take_values(self, act, g):
                act.wait_ge(self.pv, 8 * g + 8)
                act.activation(self.place(g), bank[4 + g % 2][:, :], ACT.Copy).then_inc(self.o_taken, 1)

            def dve(self, dve, step):
                dve.memset(self.vm[0], 0.0)
                dve.memset(self.vm[1], 0.0).then_inc(self.prep, 1)
                step(dve.memset(self.km, 0.0))
                for i in range(2):
                    rows = slice(AD * i, AD * i + AD)
                    dve.tensor_copy(self.km[rows, :, NM * i:NM * i + NM], kT[rows, :, 0:NM]).then_inc(self.prep, 1)
                def meta_scores(g):
                    dve.wait_ge(self.s_meta, g + 1)
                    if g >= 2:
                        dve.wait_ge(self.exp, 8 * g - 8)
                    dve.tensor_copy(self.Sm[g % 2], bank[7][:, 0:8 * NM]).then_inc(self.s_taken, 1)
                    dve.wait_ge(self.s_taken, g + 1)
                    step(dve.tensor_reduce(self.mx, self.Sm[g % 2].rearrange("p (h k) -> p h k", h=8), AX.X, ALU.max))
                    step(dve.tensor_scalar(self.mn_meta[:, g % 2], self.mx, -1.0, None, ALU.mult))

                def scores(u):
                    g, _, b, j, h = self.unit(u)
                    if j == 0:
                        meta_scores(g)
                    c = u // 4
                    dve.wait_ge(self.bias_in[c % 2], 16 * (c // 2 + 1))
                    dve.wait_ge(self.product, u + 1)
                    if u >= 2:
                        dve.wait_ge(self.turned, u - 1)
                    step(dve.tensor_tensor_reduce(self.P[u % 2], bank[u % 2][:, 0:self.W], self.bias[c % 2][:, u % 4],
                                                  -1.0, 3e38, ALU.add, ALU.min, self.mn_grid[:, u % 2:u % 2 + 1]))
                    dve.tensor_tensor(self.mn[:, u % 2:u % 2 + 1], self.mn_grid[:, u % 2:u % 2 + 1], self.mn_meta[:, g % 2, j:j + 1],
                                      ALU.min).then_inc(self.neg, 1)

                def meta_weights(g):
                    dve.wait_ge(self.p_turned, g + 1)
                    dve.tensor_copy(self.PmT, bank[7][:, 256:384]).then_inc(self.p_taken, 1)

                def sums(g):
                    dve.wait_ge(self.exp, 8 * g + 8)
                    step(dve.tensor_tensor(self.total, self.sum[:, g % 2], self.sum_meta[:, g % 2], ALU.add))
                    step(dve.reciprocal(self.rinv, self.total))

                def combine(g):
                    dve.wait_ge(self.o_taken, g + 1)
                    dve.wait_ge(self.o_meta, g + 1)
                    dve.tensor_tensor(self.place(g), self.place(g), bank[6][:, :], ALU.add).then_inc(self.comb, 1)

                def scale(g):
                    dve.wait_ge(self.comb, g + 1)
                    o3 = self.place(g).rearrange("p (h e) -> p h e", h=8)
                    step(dve.tensor_tensor(o3, o3, self.rinv.unsqueeze(2).broadcast_to([128, 8, AD]), ALU.mult))

                scores(0)
                for u in range(self.UNITS):
                    if u + 1 < self.UNITS:
                        scores(u + 1)
                    dve.wait_ge(self.turned, u + 1)
                    if u >= 2:
                        dve.wait_ge(self.pv, u - 1)
                    dve.tensor_copy(self.PT[u % 2], bank[2 + u % 2][:, 0:self.W]).then_inc(self.copied, 1)
                    if u % 8 == 0 and u:
                        meta_weights(u // 8 - 1)
                    if u > 8 and u % 8 in (1, 3, 5):
                        {1: sums, 3: combine, 5: scale}[u % 8](u // 8 - 1)
                meta_weights(self.GROUPS - 1)
                sums(self.GROUPS - 1)
                combine(self.GROUPS - 1)
                scale(self.GROUPS - 1)

            def head(self, x, h, c0, c1):
                return x[AD * (h % 2):AD * (h % 2) + AD, h // 2, c0:c1]

            def pe_meta_scores(self, pe):
                for h in range(AH):
                    ins = pe.matmul(bank[6 + h % 2][0:NM, NM * (h // 2):NM * (h // 2) + NM], self.head(qT, h, 0, NM),
                                    self.head(kT, h, 0, NM), start=True, stop=True)
                ins.then_inc(self.m_s, 1)

            def pe_meta_turn(self, pe):
                pe.wait_ge(self.m_p, 1)
                for h in range(AH):
                    ins = pe.transpose(bank[4][0:NM, NM * h:NM * h + NM], self.mp[:, self.slot(h)], ident[0:NM, 0:NM])
                ins.then_inc(self.m_t, 1)

            def pe_meta_values(self, pe):
                pe.wait_ge(self.m_pt, 1)
                for h in range(AH):
                    ins = pe.matmul(bank[5 + h // 8][0:NM, AD * (h % 8):AD * (h % 8) + AD], self.mpT[:, h],
                                    vtok[0:NM, 0, AD * h:AD * h + AD], start=True, stop=True)
                ins.then_inc(self.m_o, 1)

            def act_meta(self, act):
                act.wait_ge(self.m_sub, 2)
                act.activation(self.mp, self.mp, ACT.Exp).then_inc(self.m_exp, 1)

            def dve_meta_scores(self, dve, step):
                dve.wait_ge(self.m_s, 1)
                for i in range(2):
                    ps = bank[6 + i][0:NM, 0:8 * NM].rearrange("p (h k) -> p h k", h=8)
                    mx = self.ms_[:, 0, 8 * i:8 * i + 8]
                    step(dve.tensor_reduce(mx, ps, AX.X, ALU.max))
                    dve.tensor_tensor(self.mp[:, 8 * i:8 * i + 8], ps, mx.unsqueeze(2).broadcast_to([NM, 8, NM]),
                                      ALU.subtract).then_inc(self.m_sub, 1)

            def dve_meta_weights(self, dve, step):
                dve.wait_ge(self.m_exp, 1)
                step(dve.tensor_reduce(self.ms_[:, 1], self.mp, AX.X, ALU.add))
                step(dve.reciprocal(self.ms_[:, 2], self.ms_[:, 1]))
                dve.tensor_tensor(self.mp, self.mp, self.ms_[:, 2].unsqueeze(2).broadcast_to([NM, AH, NM]),
                                  ALU.mult).then_inc(self.m_p, 1)
                dve.wait_ge(self.m_t, 1)
                dve.tensor_copy(self.mpT, bank[4][0:NM, 0:AH * NM].rearrange("p (h k) -> p h k", h=AH)).then_inc(self.m_pt, 1)

            def dve_meta_values(self, dve):
                dve.wait_ge(self.m_o, 1)
                for i in range(2):
                    dve.tensor_copy(att[0:NM, 0, BLK * i:BLK * i + BLK], bank[5 + i][0:NM, :]).then_inc(self.m_done, 1)

            def pe(self, pe):
                head = self.head

                def meta_scores(g):
                    hg, b = g // 4, g % 4
                    if g:
                        pe.wait_ge(self.s_taken, g)
                        pe.wait_ge(self.p_taken, g - 1) if g > 1 else None
                    for p in range(4):
                        ins = pe.matmul(bank[7][:, 2 * NM * p:2 * NM * (p + 1)], qT[:, 4 * hg + p, NM + 128 * b:NM + 128 * b + 128],
                                        self.km[:, 4 * hg + p], start=True, stop=True)
                    ins.then_inc(self.s_meta, 1)

                def scores(u):
                    g, _, b, j, h = self.unit(u)
                    if j == 0:
                        meta_scores(g)
                    k0 = NM + self.KEY0[b]
                    pe.matmul(bank[u % 2][:, 0:self.W], head(qT, h, NM + 128 * b, NM + 128 * b + 128),
                              head(kT, h, k0, k0 + self.W), start=True, stop=True).then_inc(self.product, 1)

                def values(u):
                    g, _, b, j, h = self.unit(u)
                    pe.wait_ge(self.copied, u + 1)
                    if j == 0 and g >= 2:
                        pe.wait_ge(self.comb, g - 1)
                    if u == 8:
                        pe.wait_ge(odd_in.vmid, 96)
                    o = bank[4 + g % 2][:, AD * j:AD * j + AD]
                    v0, v1 = self.values(b)
                    hs = slice(AD * h, AD * h + AD)
                    pe.matmul(o, self.PT[u % 2][:, 0:128], v0[:, hs], start=True, stop=False)
                    pe.matmul(o, self.PT[u % 2][:, 128:256], v1[:, hs], start=False, stop=True).then_inc(self.pv, 1)

                def turn_meta(g):
                    if g + 1 < self.GROUPS:
                        pe.wait_ge(self.s_taken, g + 2)
                    pe.transpose(bank[7][:, 256:384], self.Pm[g % 2], ident[:, :]).then_inc(self.p_turned, 1)

                def meta_values(g):
                    pe.wait_ge(self.p_taken, g + 1)
                    if g:
                        pe.wait_ge(self.comb, g)
                    pe.matmul(bank[6][:, :], self.PmT, self.vm[g // 4], start=True, stop=True).then_inc(self.o_meta, 1)

                pe.wait_ge(self.prep, 3)
                scores(0)
                scores(1)
                for u in range(self.UNITS):
                    pe.wait_ge(self.exp, u + 1)
                    if u >= 2:
                        pe.wait_ge(self.copied, u - 1)
                    P, ps = self.P[u % 2], bank[2 + u % 2]
                    pe.transpose(ps[:, 0:128], P[:, 0:128], ident[:, :])
                    pe.transpose(ps[:, 128:256], P[:, 128:256], ident[:, :]).then_inc(self.turned, 1)
                    if u + 2 < self.UNITS:
                        scores(u + 2)
                    if u:
                        values(u - 1)
                    if u % 8 == 0 and u:
                        turn_meta(u // 8 - 1)
                    if u % 8 == 1 and u > 8:
                        if u == 9:
                            pe.wait_ge(self.v_in, 16 * AH)
                        meta_values(u // 8 - 1)
                values(self.UNITS - 1)
                turn_meta(self.GROUPS - 1)
                meta_values(self.GROUPS - 1)

        def store_tile(eng, x, dram, layer, t, s):
            if t == 0:
                eng.dma_start(dram[0:NM, :], x[0:NM, 0]).then_inc(s, 16)
            elif layer:
                c0, c1 = cols_of(t)
                eng.dma_start(dram[c0:c1, :], x[:, t]).then_inc(s, 16)
            else:
                by_row = dram[NM:T, :].rearrange("(c r) d -> r c d", r=GRID_H)
                for i in range(2):
                    eng.dma_start(by_row[2 * (t - 1) + i], x[GRID_W * i:GRID_W * (i + 1), t]).then_inc(s, 16)

        def store_tiles(eng, norm, h, hn, layer, s):
            for t in range(NT):
                eng.wait_ge(norm.hn, norm.c + t + 1)
                store_tile(eng, H, h, layer, t, s)
                store_tile(eng, norm.hnorm, hn, layer, t, s)

        def load_h(eng, s):
            for t in range(NT):
                c0, c1 = cols_of(t)
                eng.dma_start(H[0:rows_of(t), t], h_dram[c0:c1, :]).then_inc(s, 16)

        def load_x(eng, s):
            for t in range(NT):
                src = a["meta_tokens"] if t == 0 else a["x"][0, 128 * (t - 1):128 * t, :]
                eng.dma_start(H[0:rows_of(t), t], src).then_inc(s, 16)

        def gain_columns(name, layer):
            return a[name][layer].rearrange("(k p) -> p k", p=128)

        def load_constants(eng):
            for i, n, l in ((1, "ffn_norm_g", 0), (2, "attn_norm_g", 1), (3, "ffn_norm_g", 1)):
                eng.dma_start(gcol[:, i], gain_columns(n, l), allow_slow_non_contiguous=True).then_inc(consts_in, 16)
            for i, n in enumerate(("even_m_norm_g", "even_r_norm_g")):
                eng.dma_start(gcol[:, 4, 4 * i:4 * i + 4], a[n].rearrange("(k p) -> p k", p=128),
                              allow_slow_non_contiguous=True).then_inc(consts_in, 16)
            for i, n in enumerate(("odd_q_norm_g", "odd_k_norm_g")):
                for j in range(2):
                    eng.dma_start(gcol[AD * j:AD * j + AD, 5, i:i + 1], a[n].rearrange("(p o) -> p o", o=1),
                                  allow_slow_non_contiguous=True).then_inc(consts_in, 16)
            even_in.consts(eng)
            eng.dma_start(gates.logit, a["even_ret_decay_logit"].rearrange("d h -> (d h)").unsqueeze(0)
                          .broadcast_to([128, 8])).then_inc(gates.logit_in, 16)
            ex[0].consts(eng)
            ex[1].consts(eng)

        norms = [Norm(i, i) for i in range(4)]
        stored = [sem(f"stored{i}") for i in range(2)]
        even_in = EvenIn()
        gates = Gates(even_in.rows)
        mlstm, ret = MLSTM(gates), Retention()

        def even_mix(t, k):
            src = EVT["sgo"] if k < 4 else EVT["sgr"]
            return src[0:rows_of(t), t, 128 * (k % 4):128 * (k % 4) + 128]

        even_out = Project(0, even_mix, EVT["qk"], ar(0, 8 * T, k=8), 4, 8)
        odd_in, attn = OddIn(), Attention()
        odd_out = Project(1, lambda t, k: att[0:rows_of(t), t, 128 * k:128 * k + 128], ar(0, 8 * T, k=8),
                          ar(8 * T, 8 * T, k=8), None, 6)
        outs = [even_out, odd_out]
        block = ctx.enter_context(nc.Block())

        @block.sync
        def _(sp):
            load_x(sp, norms[0].in_)
            sp.wait_ge(norms[0].in_, 16 * (NT + 2))
            load_constants(sp)
            stream_mixer(sp, 0, [block_of(a["even_w_in"], c) for c in even_cols]
                         + [block_of(a["even_w_out"], c) for c in (0, BLK)], norms[0].in_, 16 * (NT + 2))
            stream_moe(sp, 0)
            stream_mixer(sp, 1, [block_of(a["odd_w_in"], BLK * j) for j in range(6)]
                         + [block_of(a["odd_w_out"], c) for c in (0, BLK)], norms[2].in_, 16 * NT)
            odd_in.shift_values(sp)
            sp.wait_ge(attn.bias_in[1], 16)
            stream_moe(sp, 1)

        @block.scalar
        def _(act):
            step = Chain(act, act_step)
            act.dma_start(ident[:, :], a["c_ident"][:, :]).then_inc(norms[0].in_, 16)
            act.dma_start(gcol[:, 0], gain_columns("attn_norm_g", 0), allow_slow_non_contiguous=True).then_inc(norms[0].in_, 16)
            for layer in range(2):
                n_in, n_ffn = norms[2 * layer], norms[2 * layer + 1]
                if layer:
                    halves[1].act(act, 0)
                    fenced(act)
                    load_h(act, n_in.in_)
                act.wait_ge(n_in.in_, 16 * (NT if layer else NT + 2))
                fenced(act)
                n_in.act(act, step)
                if layer == 0:
                    act.wait_ge(consts_in, 16 * 9)
                fenced(act)
                if layer == 0:
                    even_in.act(act, step, gates)
                    fenced(act)
                    mlstm.act(act, step)
                    fenced(act)
                    ret.act(act, step)
                    fenced(act)
                    outs[layer].turn_act(act)
                    fenced(act)
                    load_x(act, even_out.h_in)
                else:
                    odd_in.act(act, step)
                    fenced(act)
                    attn.act(act, step)
                    fenced(act)
                    outs[layer].turn_act(act)
                    fenced(act)
                    load_h(act, odd_out.h_in)
                outs[layer].act(act, n_ffn)
                store_tiles(act, n_ffn, ex[layer].resid, ex[layer].normed, layer, stored[layer])
                ex[layer].select_act(act)
                act.wait_ge(stored[layer], 32 * STORES[layer])
                ex[layer].high_part(act, 0, 0)
                ex[layer].high_part(act, 0, 1)
                fenced(act)
                ex[layer].x_high(act, 0)
                ex[layer].loop(act, ex[layer].act_body)

        @block.vector
        def _(dve):
            step = Chain(dve, dve_step)
            dve.memset(minus_half, -0.5)
            for layer in range(2):
                if layer:
                    halves[1].low(dve, 0)
                    fenced(dve)
                fenced(dve)
                norms[2 * layer].dve(dve, step)
                fenced(dve)
                if layer == 0:
                    even_in.dve(dve, step, gates)
                    fenced(dve)
                    mlstm.dve(dve, step)
                    fenced(dve)
                    ret.dve(dve, step)
                else:
                    odd_in.dve(dve, step)
                    fenced(dve)
                    attn.dve(dve, step)
                fenced(dve)
                outs[layer].turn_dve(dve, step)
                fenced(dve)
                outs[layer].dve(dve, norms[2 * layer + 1])
                ex[layer].select_dve(dve, step)
                fenced(dve)
                ex[layer].low_part(dve, 0, 1)
                ex[layer].xT_copy(dve, 0)
                ex[layer].x_low(dve, 0)
                ex[layer].loop(dve, ex[layer].dve_body)

        @block.gpsimd
        def _(pool):
            for layer in range(2):
                if layer:
                    fenced(pool)
                fenced(pool)
                norms[2 * layer].pool(pool, low=True)
                fenced(pool)
                if layer == 0:
                    fenced(pool)
                    mlstm.pool(pool)
                    fenced(pool)
                    ret.pool(pool)
                else:
                    odd_in.pool(pool)
                    fenced(pool)
                    halves[1].low(pool, 7)
                fenced(pool)
                outs[layer].turn_low(pool, POOL_LOWS)
                fenced(pool)
                norms[2 * layer + 1].pool(pool)
                fenced(pool)
                ex[layer].gather(pool, 0)
                ex[layer].loop(pool, ex[layer].pool_body)
                pool.wait_ge(ex[layer].scattered, 16 * NE * (layer + 1))

        @block.tensor
        def _(pe):
            for layer in range(2):
                if layer:
                    fenced(pe)
                fenced(pe)
                norms[2 * layer].pe(pe)
                fenced(pe)
                if layer == 0:
                    even_in.pe(pe, gates)
                    fenced(pe)
                    mlstm.pe(pe)
                    fenced(pe)
                    ret.pe(pe)
                else:
                    odd_in.pe(pe)
                    fenced(pe)
                    attn.pe(pe)
                fenced(pe)
                outs[layer].turn_pe(pe)
                fenced(pe)
                outs[layer].pe(pe, norms[2 * layer + 1], ex[layer])
                ex[layer].select_pe(pe)
                fenced(pe)
                ex[layer].turn_xs(pe, 0, 0)
                ex[layer].turn_xs(pe, 0, 1)
                ex[layer].loop(pe, ex[layer].pe_body)


def constants():
    f = np.float32
    c = {}
    c["c_ident"] = np.eye(128, dtype=f)
    c["c_iota"] = np.broadcast_to(np.arange(1, CAP + 1, dtype=f), (128, CAP)).copy()
    p = np.arange(128)
    tok = np.zeros((2, 128, NT), f)
    tok[:, :, 0] = p
    for b in range(4):
        tok[0, :, b + 1] = NM + (p % GRID_W) * GRID_H + 2 * b + p // GRID_W
        tok[1, :, b + 1] = NM + 128 * b + p
    c["c_token"] = tok
    half = HD // 2
    inv = (f(10000.0) ** (-np.arange(half, dtype=f) / f(half))).astype(f)
    ang = np.arange(T, dtype=f)[:, None] * inv[None, :]
    cs = np.concatenate([np.cos(ang), np.sin(ang)], -1).astype(f)
    rope = np.zeros((128, NT, HD), f)
    rope[:NM, 0] = cs[:NM]
    rope[:, 1:] = cs[NM:].reshape(4, 128, HD).transpose(1, 0, 2)
    c["c_rope"] = rope
    k, q = p[:, None], p[None, :]
    c["c_mf"] = (q >= k).astype(f)
    c["c_mb"] = (q <= k).astype(f)
    c["c_far"] = np.stack([np.where(q >= k, 0, FAR), np.where(q <= k, 0, FAR)], 1).astype(f)
    c["c_sel"] = np.broadcast_to(np.eye(NH, dtype=f)[:, :, None], (NH, NH, 128)).copy()
    j = np.arange(NR)[None, :]
    c["c_df"] = np.maximum(j - k, 0).astype(f)
    c["c_db"] = np.maximum(k - (j - 384), 0).astype(f)
    m = np.arange(NM)[:, None]
    c["c_dm"] = (NM + j - m).astype(f)
    return c


def bias_tiles(rpb):
    p = np.arange(128)
    c, r = p[:, None] // GRID_H, p[:, None] % GRID_H
    kk = np.arange(256)[None, :]
    parts = []
    for q0, k0 in ((0, 0), (16, 8), (48, 32)):
        qc, kc, kr = q0 + c, k0 + kk // GRID_H, kk % GRID_H
        start = np.clip(qc - 8, 0, GRID_W - 16)
        seen = (kc >= start) & (kc < start + 16)
        t = rpb[:, kr - r + 7, np.clip(kc - qc, -15, 15) + 15]
        t[:, ~seen] = -FAR
        parts.append(t)
    return np.stack(parts)


INPUTS = ["x", "meta_tokens", "attn_norm_g", "ffn_norm_g", "even_w_in", "even_conv_w", "even_gate_b",
          "even_m_norm_g", "even_ret_decay_logit", "even_r_norm_g", "even_w_out", "odd_w_in", "odd_q_norm_g",
          "odd_k_norm_g", "odd_w_out", "router_w", "expert_w_gate", "expert_w_up", "expert_w_down"]


def kernel(**inputs):
    from concourse import bacc
    from concourse.bass_utils import run_bass_kernel_spmd

    arrays = {n: np.ascontiguousarray(inputs[n]) for n in INPUTS}
    for n in ("even_w_in", "even_conv_w", "even_gate_b", "even_m_norm_g", "even_ret_decay_logit", "even_r_norm_g",
              "even_w_out", "odd_w_in", "odd_q_norm_g", "odd_k_norm_g", "odd_w_out"):
        arrays[n] = arrays[n][0]
    arrays["even_conv_w"] = np.ascontiguousarray(arrays["even_conv_w"].reshape(CONV, 2 * NH, 128).transpose(2, 1, 0))
    arrays["rpb_tiles"] = bias_tiles(np.asarray(inputs["odd_rpb"])[0])
    arrays |= constants()
    nc = bacc.Bacc("TRN2", target_bir_lowering=False, num_devices=1)
    a = {n: nc.dram_tensor(f"in_{n}", v.shape, mybir.dt.from_np(v.dtype), kind="ExternalInput").ap()
         for n, v in arrays.items()}
    out = nc.dram_tensor("out_h", (T, D), F32, kind="ExternalOutput").ap()
    trunk(nc, a, out)
    r = run_bass_kernel_spmd(nc, [{f"in_{n}": v for n, v in arrays.items()}], core_ids=[0])
    return r.results[0]["out_h"][NM:].reshape(GRID_W, GRID_H, D).transpose(1, 0, 2).reshape(1, NR, D)
```
